# Optimizing a Trainium2 kernel written in Bass

```python
import math
import jax, jax.numpy as jnp
from jax import lax
import numpy as np

D_MODEL = 1024
BATCH = 1
SEQ = 512
DEPTH = 2

CHUNK = 64
D_FF = 2816
FFN_RES = 0.5
D_CONV = D_MODEL // 2
CONV_A_WIDTH = 31
N_HEADS_B = 8
HEAD_DIM = 64
D_ATTN = N_HEADS_B * HEAD_DIM
Q_BLOCK = 128
CONV_C_WIDTH = 3
D_SHORT = D_MODEL
N_EVEN = (DEPTH + 1) // 2
N_ODD = DEPTH // 2
D_IN_EVEN = 2 * D_CONV + 3 * D_ATTN + N_HEADS_B
D_IN_ODD = 3 * D_SHORT
EPS = 1e-6

kernel_name = "hybrid_conformer_fox_shortconv_trunk"

def rmsnorm(x, g):
    xf = x.astype(jnp.float32)
    y = xf * lax.rsqrt(jnp.mean(xf * xf, axis=-1, keepdims=True) + EPS)
    return (y * g.astype(jnp.float32)).astype(x.dtype)

def swiglu(x, w_gate, w_up, w_down):
    return (jax.nn.silu(x @ w_gate) * (x @ w_up)) @ w_down

def causal_depthwise_conv(x, w):
    k_width = w.shape[0]
    return lax.conv_general_dilated(
        x, w[:, None, :].astype(x.dtype), window_strides=(1,),
        padding=[(k_width - 1, 0)],
        dimension_numbers=("NWC", "WIO", "NWC"),
        feature_group_count=x.shape[-1])

def forgetting_attention(q, k, v, log_f):
    b, s_len, h, dh = q.shape
    nb = s_len // Q_BLOCK
    scale = 1.0 / math.sqrt(dh)
    cum = jnp.cumsum(log_f, axis=1).transpose(0, 2, 1)
    qh = q.transpose(0, 2, 1, 3)
    kh = k.transpose(0, 2, 1, 3)
    vh = v.transpose(0, 2, 1, 3)
    q_blocks = qh.reshape(b, h, nb, Q_BLOCK, dh).transpose(2, 0, 1, 3, 4)
    f_blocks = cum.reshape(b, h, nb, Q_BLOCK).transpose(2, 0, 1, 3)
    q_pos = jnp.arange(s_len).reshape(nb, Q_BLOCK)
    k_pos = jnp.arange(s_len)

    def block(args):
        qi, fi, pi = args
        logits = jnp.einsum("bhqd,bhkd->bhqk", qi, kh,
                            preferred_element_type=jnp.float32) * scale
        logits = logits + fi[..., None] - cum[:, :, None, :]
        logits = jnp.where(k_pos[None, :] <= pi[:, None], logits, -jnp.inf)
        p = jax.nn.softmax(logits, axis=-1)
        return jnp.einsum("bhqk,bhkd->bhqd", p.astype(vh.dtype), vh)

    o = lax.map(block, (q_blocks, f_blocks, q_pos))
    return o.transpose(1, 0, 3, 2, 4).reshape(b, s_len, h * dh)

def even_mixer(h, w_in, b_f, conv_w, conv_b, conv_norm, q_norm, k_norm, w_out):
    b, s_len, _ = h.shape
    z = h @ w_in
    splits = np.cumsum([D_CONV, D_CONV, D_ATTN, D_ATTN, D_ATTN]).tolist()
    u, g, q, k, v, f_logit = jnp.split(z, splits, axis=-1)
    a = u * jax.nn.sigmoid(g)
    a = causal_depthwise_conv(a, conv_w) + conv_b
    a = jax.nn.silu(rmsnorm(a, conv_norm))
    q = rmsnorm(q.reshape(b, s_len, N_HEADS_B, HEAD_DIM), q_norm)
    k = rmsnorm(k.reshape(b, s_len, N_HEADS_B, HEAD_DIM), k_norm)
    v = v.reshape(b, s_len, N_HEADS_B, HEAD_DIM)
    log_f = jax.nn.log_sigmoid(f_logit.astype(jnp.float32) + b_f.astype(jnp.float32))
    o = forgetting_attention(q, k, v, log_f)
    return jnp.concatenate([a, o.astype(a.dtype)], axis=-1) @ w_out

def odd_mixer(h, w_in, conv_w, w_out):
    z = h @ w_in
    gate_b, gate_c, hh = jnp.split(z, 3, axis=-1)
    y = gate_b * causal_depthwise_conv(gate_c * hh, conv_w)
    return y @ w_out

def setup_inputs(seed: int = 0) -> dict:
    key = jax.random.key(seed)
    ks = iter(jax.random.split(key, 32))
    f32 = jnp.float32

    def nrm(shape, fan_in):
        return jax.random.normal(next(ks), shape, f32) * (fan_in ** -0.5)

    def gain(shape):
        return 1.0 + 0.02 * jax.random.normal(next(ks), shape, f32)

    return {
        "x": jax.random.normal(next(ks), (BATCH, SEQ, D_MODEL), f32),
        "ffn1_norm": gain((DEPTH, D_MODEL)),
        "ffn1_w_gate": nrm((DEPTH, D_MODEL, D_FF), D_MODEL),
        "ffn1_w_up": nrm((DEPTH, D_MODEL, D_FF), D_MODEL),
        "ffn1_w_down": nrm((DEPTH, D_FF, D_MODEL), D_FF),
        "mix_norm": gain((DEPTH, D_MODEL)),
        "ffn2_norm": gain((DEPTH, D_MODEL)),
        "ffn2_w_gate": nrm((DEPTH, D_MODEL, D_FF), D_MODEL),
        "ffn2_w_up": nrm((DEPTH, D_MODEL, D_FF), D_MODEL),
        "ffn2_w_down": nrm((DEPTH, D_FF, D_MODEL), D_FF),
        "ev_w_in": nrm((N_EVEN, D_MODEL, D_IN_EVEN), D_MODEL),
        "ev_b_f": jax.random.uniform(next(ks), (N_EVEN, N_HEADS_B), f32, 1.0, 5.0),
        "ev_conv_w": nrm((N_EVEN, CONV_A_WIDTH, D_CONV), CONV_A_WIDTH),
        "ev_conv_b": 0.01 * jax.random.normal(next(ks), (N_EVEN, D_CONV), f32),
        "ev_conv_norm": gain((N_EVEN, D_CONV)),
        "ev_q_norm": gain((N_EVEN, HEAD_DIM)),
        "ev_k_norm": gain((N_EVEN, HEAD_DIM)),
        "ev_w_out": nrm((N_EVEN, D_CONV + D_ATTN, D_MODEL), D_CONV + D_ATTN),
        "od_w_in": nrm((N_ODD, D_MODEL, D_IN_ODD), D_MODEL),
        "od_conv_w": nrm((N_ODD, CONV_C_WIDTH, D_SHORT), CONV_C_WIDTH),
        "od_w_out": nrm((N_ODD, D_SHORT, D_MODEL), D_SHORT),
    }

def reference(x, ffn1_norm, ffn1_w_gate, ffn1_w_up, ffn1_w_down, mix_norm,
              ffn2_norm, ffn2_w_gate, ffn2_w_up, ffn2_w_down,
              ev_w_in, ev_b_f, ev_conv_w, ev_conv_b, ev_conv_norm, ev_q_norm,
              ev_k_norm, ev_w_out, od_w_in, od_conv_w, od_w_out):
    for layer in range(DEPTH):
        x = x + FFN_RES * swiglu(rmsnorm(x, ffn1_norm[layer]), ffn1_w_gate[layer],
                                 ffn1_w_up[layer], ffn1_w_down[layer])
        h = rmsnorm(x, mix_norm[layer])
        if layer % 2 == 0:
            i = layer // 2
            x = x + even_mixer(h, ev_w_in[i], ev_b_f[i], ev_conv_w[i], ev_conv_b[i],
                               ev_conv_norm[i], ev_q_norm[i], ev_k_norm[i], ev_w_out[i])
        else:
            i = layer // 2
            x = x + odd_mixer(h, od_w_in[i], od_conv_w[i], od_w_out[i])
        x = x + FFN_RES * swiglu(rmsnorm(x, ffn2_norm[layer]), ffn2_w_gate[layer],
                                 ffn2_w_up[layer], ffn2_w_down[layer])
    return x


_drawn_inputs = setup_inputs


def setup_inputs(seed=0):
    import zlib

    import numpy as np

    out = dict(_drawn_inputs(seed))
    spreads = {}
    factors = {'ffn1_norm': 3.495,
     'ffn2_norm': 4.824,
     'ev_conv_b': 5.274,
     'ev_conv_norm': 4.657,
     'ev_q_norm': 8.0,
     'ev_k_norm': 8.0}
    for name, (base, spread) in spreads.items():
        noise = np.random.default_rng([zlib.crc32(name.encode()), seed]).standard_normal(out[name].shape)
        drawn = base * np.exp(spread * noise) if base else spread * noise
        out[name] = __import__('jax').numpy.asarray(drawn.astype(out[name].dtype))
    for name, factor in factors.items():
        out[name] = (out[name] * factor).astype(out[name].dtype)
    return out
```

```python
import math
from contextlib import ExitStack

import concourse.bass as bass
from concourse import mybir

P = 128
BANKS = 8
EPS = 1e-6
MASKED = -1.0e30


class Phase:

    def __init__(self, kind, units, row_tiles, **more):
        self.kind, self.units, self.row_tiles = kind, units, row_tiles
        self.groups = units // 4
        self.norm = more.get("norm")
        self.next_norm = more.get("next_norm")
        self.gate = more.get("gate")
        self.source = more.get("source")
        self.weights = more.get("weights")
        self.factor = more.get("factor", 1.0)
        self.next = None


def plan(phases):
    unit = pair = gate_act = h = 0
    for n, ph in enumerate(phases):
        ph.unit0, ph.pair0, ph.act0, ph.h0, ph.pair_end = unit, pair, gate_act, h, pair
        unit += ph.units
        if ph.kind == "pair":
            pair += ph.units // 2
            if ph.gate != "none":
                gate_act += ph.units // 2
            if ph.gate == "silu":
                h += ph.units // 2
        if n:
            phases[n - 1].next = ph
    return phases


def trunk(nc, t_in, out):
    f32, f32r = mybir.dt.float32, mybir.dt.float32r
    ACT, ALU, AX = mybir.ActivationFunctionType, mybir.AluOpType, mybir.AxisListType

    x_in = t_in["x"]
    _, S, D = x_in.shape
    FF = t_in["ffn1_w_gate"].shape[2]
    CONV = t_in["ev_conv_w"].shape[2]
    TAPS = t_in["ev_conv_w"].shape[1]
    TAPS_C = t_in["od_conv_w"].shape[1]
    HEADS = t_in["ev_b_f"].shape[1]
    HD = t_in["ev_q_norm"].shape[1]
    ATT = HEADS * HD
    KD, KF, TB = D // P, FF // P, S // P
    CB, AB = CONV // P, ATT // P
    HALF = KF // 2
    QK = 2 * AB

    w = {k: v[0] if v.shape[0] == 1 else v for k, v in t_in.items() if k.startswith(("ev_w", "od_w"))}

    def swiglu(name, layer, norm, next_norm):
        return [
            Phase("pair", 2 * KF, KD, norm=norm, gate="silu",
                  weights=(t_in[name + "_w_gate"][layer], 0, t_in[name + "_w_up"][layer], 0)),
            Phase("resid", 2 * KD, HALF, next_norm=next_norm, source="h", factor=0.5,
                  weights=t_in[name + "_w_down"][layer]),
        ]

    even_in, odd_in = w["ev_w_in"], w["od_w_in"]
    phases = plan(
        swiglu("ffn1", 0, 0, 1)
        + [Phase("pair", 2 * CB, KD, norm=1, gate="sigmoid", weights=(even_in, CONV, even_in, 0)),
           Phase("qk", QK, KD, norm=1, weights=(even_in, 2 * CONV)),
           Phase("v", KD // 2, KD, norm=1, weights=(even_in, 2 * CONV + 2 * ATT)),
           Phase("resid", KD, KD, next_norm=2, source="cat", weights=w["ev_w_out"])]
        + swiglu("ffn2", 0, 2, 3)
        + swiglu("ffn1", 1, 3, 4)
        + [Phase("pair", 2 * KD, KD, norm=4, gate="none", weights=(odd_in, D, odd_in, 2 * D)),
           Phase("single", KD, KD, norm=4, weights=(odd_in, 0)),
           Phase("resid", KD, KD, next_norm=5, source="y", weights=w["od_w_out"])]
        + swiglu("ffn2", 1, 5, None)
    )
    A_GATE, QKP, VP, A_OUT = phases[2], phases[3], phases[4], phases[5]
    LAST = phases[-1]
    TOTAL = LAST.unit0 + LAST.units

    base = -(-nc.sbuf_base // 64) * 64
    end = [base]

    def room(nbytes):
        at = end[0]
        end[0] += -(-nbytes // 32) * 32
        return at

    def at(name, shape, dt, offset):
        return nc.alloc_sbuf_tensor_at(name, shape, dt, offset=offset)

    def own(name, shape, dt=f32):
        return at(name, shape, dt, room(4 * math.prod(shape[1:])))

    ROW = 4 * S
    SLOT = P * HALF
    x = own("x", [P, KD, S])
    XG = room(2 * KD * ROW)
    xg_hi, xg_lo = at("xg_hi", [P, KD, S], f32r, XG), at("xg_lo", [P, KD, S], f32r, XG + KD * ROW)
    H = room(2 * KF * ROW)
    h_hi, h_lo = at("h_hi", [P, KF, S], f32r, H), at("h_lo", [P, KF, S], f32r, H + KF * ROW)
    raw = own("raw", [P, 4, SLOT])
    w_hi, w_lo = own("w_hi", [P, 2, SLOT], f32r), own("w_lo", [P, 2, SLOT], f32r)
    rstd = own("rstd", [P, S])
    GATE, ACTED, SCALED, HID = room(2 * ROW), room(2 * ROW), room(ROW), room(ROW)
    gate = at("gate", [P, 2, S], f32, GATE)
    acted = at("acted", [P, 2, S], f32, ACTED)
    scaled = at("scaled", [P, S], f32, SCALED)
    hid = at("hid", [P, S], f32, HID)
    sq = own("sq", [P, 2, S])
    sq_sum = own("sq_sum", [P, S])
    cum = own("cum", [HEADS, S])
    ident, ones = own("ident", [P, P]), own("ones", [P, P])
    ident_r, mask_r = own("ident_r", [P, P], f32r), own("mask_r", [P, P], f32r)
    GAINS = 6 * KD
    V_CB, V_CN, V_OD = GAINS, GAINS + CB, GAINS + 2 * CB
    V_Q = V_OD + TAPS_C * KD
    NVEC = V_Q + 2
    vec = own("vec", [P, NVEC])
    conv_w = own("conv_w", [P, TAPS * CB])
    qk_gain = own("qk_gain", [P, 2])
    head_sel = own("head_sel", [P, QK, 2 * HEADS])
    wf_raw = own("wf_raw", [P, KD, HEADS])
    b_f = own("b_f", [HEADS, 1])
    rstd_col = own("rstd_col", [P, TB])
    neg_max = own("neg_max", [P, HEADS * TB])
    row_sum, row_inv = own("row_sum", [P, HEADS * TB]), own("row_inv", [P, HEADS * TB])

    mean_sq, root = at("mean_sq", [P, S], f32, GATE), at("root", [P, S], f32, GATE + ROW)
    rough, corr = at("rough", [P, S], f32, ACTED), at("corr", [P, S], f32, ACTED + ROW)

    x_rows = at("x_rows", [P, TB, D], f32, H)
    vec_rows = at("vec_rows", [NVEC, P], f32, H + TB * D * 4)
    conv_rows = at("conv_rows", [TAPS * CB, P], f32, H + TB * D * 4 + 4 * P)

    q_hi, q_lo = at("q_hi", [P, AB, S], f32r, H), at("q_lo", [P, AB, S], f32r, H + AB * ROW)
    k_hi, k_lo = at("k_hi", [P, AB, S], f32r, H + 2 * AB * ROW), at("k_lo", [P, AB, S], f32r, H + 3 * AB * ROW)
    VAT = H + 4 * AB * ROW
    v_hi, v_lo = at("v_hi", [P, TB, ATT], f32r, VAT), at("v_lo", [P, TB, ATT], f32r, VAT + TB * ATT * 4)
    wf_hi, wf_lo = at("wf_hi", [P, KD, P], f32r, VAT), at("wf_lo", [P, KD, P], f32r, VAT + KD * P * 4)
    CAT = VAT + 2 * TB * ATT * 4
    cat_hi, cat_lo = at("cat_hi", [P, KD, S], f32r, CAT), at("cat_lo", [P, KD, S], f32r, CAT + KD * ROW)
    conv = at("conv", [P, CB, S], f32, CAT)
    qk_raw = at("qk_raw", [P, QK, S], f32, CAT + KD * ROW)
    AIN = CAT + 2 * KD * ROW
    a_in = at("a_in", [P, CB, S], f32, AIN)
    assert AIN + CB * ROW <= H + 2 * KF * ROW
    a_mean, a_root = at("a_mean", [P, S], f32, AIN), at("a_root", [P, S], f32, AIN + ROW)
    a_rough, a_corr = at("a_rough", [P, S], f32, AIN + 2 * ROW), at("a_corr", [P, S], f32, AIN + 3 * ROW)
    a_nrm = at("a_nrm", [P, 2, S], f32, AIN)
    a_act = at("a_act", [P, 2, S], f32, AIN + 2 * ROW)
    head_fan = at("head_fan", [2 * HEADS, QK, P], f32, SCALED)
    qk_nrm = at("qk_nrm", [P, 2, S], f32, ACTED)
    lf = [at(f"lf{i}", [HEADS, S], f32, a) for i, a in enumerate((GATE, GATE + ROW, ACTED, ACTED + ROW, HID))]
    CP = P
    row_sel = at("row_sel", [CP, HEADS, P], f32r, GATE)
    cum_r, ncum_r = at("cum_r", [CP, S], f32r, SCALED), at("ncum_r", [CP, S], f32r, HID)
    probs = at("probs", [P, 2, S], f32, ACTED)
    pt_hi = [at(f"pt_hi{i}", [P, TB, S], f32r, XG + 2 * i * TB * ROW) for i in range(2)]
    pt_lo = [at(f"pt_lo{i}", [P, TB, S], f32r, XG + (2 * i + 1) * TB * ROW) for i in range(2)]
    y_hi, y_lo = at("y_hi", [P, KD, S], f32r, H), at("y_lo", [P, KD, S], f32r, H + KD * ROW)
    c_in = at("c_in", [P, KD, S], f32, H + 2 * KD * ROW)
    c_out = at("c_out", [P, KD, S], f32, H + 3 * KD * ROW)
    fin = at("fin", [P, 2, S], f32, XG)
    out_rows = at("out_rows", [P, 2, TB, P], f32, XG + 2 * ROW)
    assert end[0] <= nc.sbuf_top, (end[0], nc.sbuf_top)

    STEPS = HEADS * TB + 5
    TAPS_A, TAPS_QK = [0, 9, 9, 9], [5] * QK
    left = TAPS * CB - sum(TAPS_A) - sum(TAPS_QK)
    TAPS_T = [2] * (left // 2) + [left % 2]

    def blocks_done_at(t):
        before = sum(TAPS_A) + sum(TAPS_QK) + sum(TAPS_T[:t])
        done = before + (TAPS_T[t] if t < len(TAPS_T) else 0)
        return [b for b in range(CB) if (before < TAPS * (b + 1) or t == 0) and TAPS * (b + 1) <= done]

    SRC = {"h": (h_hi, h_lo), "cat": (cat_hi, cat_lo), "y": (y_hi, y_lo)}

    def raws(ap):
        return ap.bitcast(f32)

    with ExitStack() as ctx:
        bank = [ctx.enter_context(nc.psum_tensor(f"bank{i}", [P, S], f32)) for i in range(BANKS)]

        def sem(name):
            return ctx.enter_context(nc.semaphore(name))

        x_arrived = [sem(f"x_arrived{i}") for i in range(2)]
        vec_arrived, conv_arrived, wf_arrived = sem("vec_arrived"), sem("conv_arrived"), sem("wf_arrived")
        w_arrived = [sem(f"w_arrived{i}") for i in range(4)]
        consts_ready, sel_ready, vec_turned, vec_ready = (
            sem("consts_ready"), sem("sel_ready"), sem("vec_turned"), sem("vec_ready"))
        qgain_ready, mask_cleared, identr_ready = (
            sem("qgain_ready"), sem("mask_cleared"), sem("identr_ready"))
        whi_ready, wlo_ready, unit_done = sem("whi_ready"), sem("wlo_ready"), sem("unit_done")
        x_turned = sem("x_turned")
        x_new, xhi_ready, xlo_ready = sem("x_new"), sem("xhi_ready"), sem("xlo_ready")
        sq_ready, sq_added, sq_cleared = sem("sq_ready"), sem("sq_added"), sem("sq_cleared")
        ssq_done, mean_ready, root_ready, rstd_ready = (
            sem("ssq_done"), sem("mean_ready"), sem("root_ready"), sem("rstd_ready"))
        gate_scaled, gate_acted, gate_ready, pair_out = (
            sem("gate_scaled"), sem("gate_acted"), sem("gate_ready"), sem("pair_out"))
        hhi_ready, hlo_ready = sem("hhi_ready"), sem("hlo_ready")
        step = sem("step")
        wf_cleared, wfhi_ready, wflo_ready, f_done = (
            sem("wf_cleared"), sem("wfhi_ready"), sem("wflo_ready"), sem("f_done"))
        col_done, col_ready = sem("col_done"), sem("col_ready")
        lf_in, lf_abs, lf_exp, lf_log, cum_ready = (
            sem("lf_in"), sem("lf_abs"), sem("lf_exp"), sem("lf_log"), sem("cum_ready"))
        cum_cleared, cumhi_ready, cumlo_ready = sem("cum_cleared"), sem("cumhi_ready"), sem("cumlo_ready")
        fan_ready, rsel_ready, rsel_step = sem("fan_ready"), sem("rsel_ready"), sem("rsel_step")
        qk_out, qk_sq, qk_sum = sem("qk_out"), sem("qk_sq"), sem("qk_sum")
        qk_mean, qk_root, qk_rstd, qk_fanned = sem("qk_mean"), sem("qk_root"), sem("qk_rstd"), sem("qk_fanned")
        qk_scaled, qkhi_ready, qklo_ready = sem("qk_scaled"), sem("qkhi_ready"), sem("qklo_ready")
        vhi_ready, vlo_ready = sem("vhi_ready"), sem("vlo_ready")
        scores_done, max_ready, exp_done, probs_ready = (
            sem("scores_done"), sem("max_ready"), sem("exp_done"), sem("probs_ready"))
        probs_turned, pthi_ready, ptlo_ready, pv_done = (
            sem("probs_turned"), sem("pthi_ready"), sem("ptlo_ready"), sem("pv_done"))
        ohi_ready, olo_ready = sem("ohi_ready"), sem("olo_ready")
        conv_done, a_sq, a_added, a_sum = sem("conv_done"), sem("a_sq"), sem("a_added"), sem("a_sum")
        am_ready, ar_ready = sem("am_ready"), sem("ar_ready")
        a_scaled, a_acted, ahi_ready, alo_ready = (
            sem("a_scaled"), sem("a_acted"), sem("ahi_ready"), sem("alo_ready"))
        conv3_step, conv3_done, y_gated = sem("conv3_step"), sem("conv3_done"), sem("y_gated")
        y_out, yhi_ready, ylo_ready = sem("y_out"), sem("yhi_ready"), sem("ylo_ready")
        out_turned, out_staged = sem("out_turned"), sem("out_staged")
        out_sent = [sem(f"out_sent{i}") for i in range(2)]

        block = ctx.enter_context(nc.Block())

        def unit_view(ph, tensor, slot):
            if ph.kind == "v":
                return tensor[:, slot, 0:2 * ATT].rearrange("p (k n) -> p k n", k=2)
            return tensor[:, slot, 0:ph.row_tiles * P].rearrange("p (k n) -> p k n", k=ph.row_tiles)

        @block.sync
        def _(sp):
            def load(ph, g, u):
                if isinstance(ph.weights, tuple) and ph.kind == "pair":
                    gw, gc, uw, uc = ph.weights
                    src, c0 = (gw, gc) if u % 2 == 0 else (uw, uc)
                    rows = src.rearrange("(k p) n -> p k n", p=P)
                    src = rows[:, :, bass.ds(c0 + (g * 2 + u // 2) * P, P)]
                elif ph.kind == "resid" and ph.row_tiles == HALF:
                    rows = ph.weights.rearrange("(k p) n -> p k n", p=P)
                    k0 = (u % 2) * HALF
                    src = rows[:, k0:k0 + HALF, bass.ds((g * 2 + u // 2) * P, P)]
                elif ph.kind == "v":
                    src = ph.weights[0].rearrange("(k p) n -> p k n", p=P)
                    src = src[:, 2 * u:2 * u + 2, ph.weights[1]:ph.weights[1] + ATT]
                else:
                    ww, c0 = ph.weights if isinstance(ph.weights, tuple) else (ph.weights, 0)
                    src = ww.rearrange("(k p) n -> p k n", p=P)[:, :, bass.ds(c0 + (g * 4 + u) * P, P)]
                if isinstance(g, int):
                    if ph.unit0 + 4 * g + u >= 4:
                        sp.wait_ge(wlo_ready, ph.unit0 + 4 * g + u - 3)
                else:
                    sp.wait_ge(wlo_ready, g * 4 + (ph.unit0 + u - 3))
                sp.dma_start(unit_view(ph, raw, u), src).then_inc(w_arrived[u], 16)

            for i in range(2):
                sp.dma_start(x_rows[:, 2 * i:2 * i + 2, :],
                             x_in[0].rearrange("(t p) d -> p t d", p=P)[:, 2 * i:2 * i + 2, :]).then_inc(x_arrived[i], 16)
            for ph in phases:
                for u in range(4):
                    load(ph, 0, u)
                if ph.groups > 1:
                    with sp.Fori(1, ph.groups) as g:
                        for u in range(4):
                            load(ph, g, u)

        @block.gpsimd
        def _(pool):
            pool.memset(ident[:, :], 0.0).then_inc(consts_ready, 1)
            pool.memset(ones[:, :], 1.0).then_inc(consts_ready, 1)
            pool.memset(sq_sum[:, :], 0.0).then_inc(sq_cleared, 1)
            pool.wait_ge(consts_ready, 2)
            pool.affine_select(out=ident[:, :], in_=ident[:, :], compare_op=ALU.not_equal, fill=1.0, base=0,
                               pattern=[[-1, P]], channel_multiplier=1).then_inc(consts_ready, 1)
            pool.memset(head_sel[:, :, :], 0.0).then_inc(sel_ready, 1)
            pool.wait_ge(sel_ready, 1)
            for t in range(QK):
                for half in range(2):
                    pool.memset(head_sel[half * HD:(half + 1) * HD, t, 2 * t + half:2 * t + half + 1], 1.0)\
                        .then_inc(sel_ready, 1)
            pool.wait_ge(sel_ready, 1 + 2 * QK)
            pool.memset(raws(mask_r[:, :]), 0.0).then_inc(mask_cleared, 1)
            pool.wait_ge(mask_cleared, 1)
            pool.affine_select(out=mask_r[:, :], in_=raws(mask_r[:, :]), compare_op=ALU.is_ge, fill=MASKED, base=0,
                               pattern=[[-1, P]], channel_multiplier=1).then_inc(sel_ready, 1)

            def add_squares(norm):
                if norm:
                    pool.wait_ge(ssq_done, norm)
                    pool.memset(sq_sum[:, :], 0.0).then_inc(sq_cleared, 1)
                pool.wait_ge(sq_cleared, norm + 1)
                with pool.Fori(0, KD // 2) as g:
                    for half in range(2):
                        pool.wait_ge(sq_ready, g * 2 + (KD * norm + half + 1))
                        pool.tensor_tensor(sq_sum[:, :], sq_sum[:, :], sq[:, half, :], ALU.add)\
                            .then_inc(sq_added, 1)
                        pool.wait_ge(sq_added, g * 2 + (KD * norm + half + 1))

            def gates(ph):
                pool.wait_ge(rstd_ready, ph.norm + 1)
                n = ph.units // 2

                def one(f, par):
                    src = gate if ph.gate == "none" else acted
                    if ph.gate == "none":
                        pool.wait_ge(gate_scaled, f + (ph.pair0 + 1))
                    else:
                        pool.wait_ge(gate_acted, f + (ph.act0 + 1))
                    if not isinstance(f, int) or ph.pair0 + f > 0:
                        pool.wait_ge(pair_out, f + ph.pair0)
                    pool.tensor_tensor(scaled[:, :], src[:, par, :], rstd[:, :], ALU.mult).then_inc(gate_ready, 1)

                one(0, 0)
                one(1, 1)
                with pool.Fori(1, n // 2) as g:
                    for par in range(2):
                        one(g * 2 + par, par)

            for ph in phases:
                if ph.norm == 0 and ph.kind == "pair":
                    add_squares(0)
                if ph is A_GATE:
                    pool.wait_ge(unit_done, ph.unit0)
                    pool.memset(raws(wf_hi[:, :, :]), 0.0).then_inc(wf_cleared, 1)
                    pool.memset(raws(wf_lo[:, :, :]), 0.0).then_inc(wf_cleared, 1)
                if ph.kind == "pair":
                    gates(ph)
                if ph.kind == "single":
                    with pool.Fori(0, KD) as f:
                        pool.wait_ge(conv3_done, f + 1)
                        tile = c_out[:, bass.ds(f, 1), :]
                        pool.tensor_tensor(tile, tile, rstd[:, :].unsqueeze(1), ALU.mult).then_inc(y_gated, 1)
                if ph is A_GATE:
                    pool.wait_ge(pair_out, ph.pair0 + CB)
                    pool.wait_ge(cum_ready, 1)
                    pool.memset(head_fan[:, :, :], 0.0).then_inc(fan_ready, 1)
                    pool.wait_ge(fan_ready, 1)
                    view = head_fan[:, :, :].rearrange("r t (a c) -> r t a c", a=2)
                    pool.affine_select(out=view, in_=view, compare_op=ALU.not_equal, fill=1.0, base=0,
                                       pattern=[[-2, QK], [-1, 2], [0, HD]], channel_multiplier=1)\
                        .then_inc(fan_ready, 1)
                if ph is VP:
                    pool.wait_ge(qklo_ready, QK)
                    pool.memset(raws(row_sel[:, :, :]), 0.0).then_inc(rsel_step, 1)
                    pool.memset(raws(cum_r[:, :]), 0.0).then_inc(cum_cleared, 1)
                    pool.memset(raws(ncum_r[:, :]), 0.0).then_inc(cum_cleared, 1)
                    for n, off in enumerate(range(0, CP, 32)):
                        pool.wait_ge(rsel_step, n + 1)
                        pool.affine_select(out=row_sel[:, :, :], in_=raws(row_sel[:, :, :]), compare_op=ALU.not_equal,
                                           fill=1.0, base=-off, pattern=[[-1, HEADS], [0, P]],
                                           channel_multiplier=1).then_inc(rsel_ready if off == CP - 32 else rsel_step, 1)
                    pool.wait_ge(ssq_done, 2)
                    for b in range(1, CB):
                        pool.wait_ge(a_sq, b + 1)
                        if b > 1:
                            pool.wait_ge(a_added, b - 1)
                        first = sq[:, 0, :] if b == 1 else sq_sum[:, :]
                        pool.tensor_tensor(sq_sum[:, :], first, sq[:, b % 2, :], ALU.add).then_inc(a_added, 1)
                if ph.kind == "resid" and ph.next_norm is not None:
                    if ph is A_OUT:
                        pool.wait_ge(a_sum, 1)
                    add_squares(ph.next_norm)

        @block.scalar
        def _(act):
            r = 0
            for layer in range(2):
                for name in ("ffn1_norm", "mix_norm", "ffn2_norm"):
                    act.dma_start(vec_rows[r:r + KD, :], t_in[name][layer].rearrange("(k p) -> k p", p=P))\
                        .then_inc(vec_arrived, 16)
                    r += KD
            act.dma_start(vec_rows[V_CB:V_CN, :], t_in["ev_conv_b"][0].rearrange("(k p) -> k p", p=P))\
                .then_inc(vec_arrived, 16)
            act.dma_start(vec_rows[V_CN:V_OD, :], t_in["ev_conv_norm"][0].rearrange("(k p) -> k p", p=P))\
                .then_inc(vec_arrived, 16)
            for t in range(TAPS_C):
                act.dma_start(vec_rows[V_OD + t * KD:V_OD + (t + 1) * KD, :],
                              t_in["od_conv_w"][0, t].rearrange("(k p) -> k p", p=P)).then_inc(vec_arrived, 16)
            for n, name in enumerate(("ev_q_norm", "ev_k_norm")):
                for half in range(2):
                    act.dma_start(vec_rows[V_Q + n:V_Q + n + 1, half * HD:(half + 1) * HD], t_in[name])\
                        .then_inc(vec_arrived, 16)
            act.dma_start(conv_rows[:, :], t_in["ev_conv_w"][0].rearrange("t (b p) -> (t b) p", p=P))\
                .then_inc(conv_arrived, 16)
            act.dma_start(wf_raw[:, :, :],
                          even_in.rearrange("(k p) n -> p k n", p=P)[:, :, 2 * CONV + 3 * ATT:])\
                .then_inc(wf_arrived, 16)
            act.dma_start(b_f[:, :], t_in["ev_b_f"].rearrange("o h -> h o")).then_inc(wf_arrived, 16)

            def split_hi(ph, g, u):
                if u >= 4 and isinstance(g, int) and g == ph.groups - 1:
                    ph, g, u = ph.next, 0, u - 4
                    if ph is None:
                        return
                n = ph.row_tiles * P
                i = ph.unit0 + u if not isinstance(g, int) else ph.unit0 + u + 4 * g
                if isinstance(g, int):
                    act.wait_ge(w_arrived[u % 4], 16 * (i // 4 + 1))
                    if i >= 2:
                        act.wait_ge(unit_done, i - 1)
                else:
                    act.wait_ge(w_arrived[u % 4], g * 16 + 16 * (i // 4 + 1))
                    act.wait_ge(unit_done, g * 4 + (i - 1))
                act.activation(w_hi[:, u % 2, 0:n], raw[:, u % 4, 0:n], ACT.Copy).then_inc(whi_ready, 1)

            def new_x(j, half, norm):
                act.wait_ge(x_new, j + (KD * norm + 1))
                if not isinstance(j, int) or KD * norm + j >= 2:
                    act.wait_ge(sq_added, j + (KD * norm - 1))
                one = bass.ds(j, 1)
                act.activation(xg_hi[:, one, :], x[:, one, :], ACT.Copy, scale=vec[:, bass.ds(j + norm * KD, 1)])\
                    .then_inc(xhi_ready, 1)
                act.activation(sq[:, half:half + 1, :], x[:, one, :], ACT.Square).then_inc(sq_ready, 1)

            def norm_root(ready, n, mean, out_root, done):
                act.wait_ge(ready, n)
                act.activation(out_root, mean, ACT.Sqrt).then_inc(done, 1)

            def pair(ph):
                def group(g):
                    first = isinstance(g, int) and g == 0
                    for u in range(4):
                        f, par = g * 2 + u // 2, u // 2
                        if not (first and u == 1):
                            split_hi(ph, g, u + 2)
                        if first and u == 0:
                            norm_root(mean_ready, ph.norm + 1, mean_sq[:, :], root[:, :], root_ready)
                            split_hi(ph, g, 3)
                        if u % 2 == 0 and ph.gate != "none":
                            func = ACT.Silu if ph.gate == "silu" else ACT.Sigmoid
                            act.wait_ge(gate_scaled, f + (ph.pair0 + 1))
                            if not first:
                                act.wait_ge(gate_ready, f + (ph.pair0 - 1))
                            act.activation(acted[:, par, :], gate[:, par, :], func).then_inc(gate_acted, 1)
                        if u % 2 == 1 and ph.gate == "silu":
                            act.wait_ge(pair_out, f + (ph.pair0 + 1))
                            act.activation(h_hi[:, bass.ds(f, 1), :], hid[:, :], ACT.Copy).then_inc(hhi_ready, 1)

                run_groups(ph, group)

            def run_groups(ph, group):
                peeled = 2 if ph is LAST else 1
                for g in range(min(peeled, ph.groups)):
                    group(g)
                if ph.groups - 1 > peeled:
                    with act.Fori(peeled, ph.groups - 1) as g:
                        group(g)
                if ph.groups > peeled:
                    group(ph.groups - 1)

            def resid(ph):
                per_tile = 2 if ph.row_tiles == HALF else 1

                def group(g):
                    for u in range(4):
                        split_hi(ph, g, u + 2)
                        if u % per_tile == per_tile - 1 and ph.next_norm is not None:
                            j = g * (4 // per_tile) + u // per_tile
                            new_x(j, (u // per_tile) % 2, ph.next_norm)
                        if ph is LAST and u % 2 == 1:
                            send(g * 2 + u // 2 - 1, 1 - u // 2)

                run_groups(ph, group)
                if ph is LAST:
                    send(KD - 1, 1)
                    for i in range(2):
                        act.wait_ge(out_sent[i], 16 * (KD // 2))

            def send(j, par):
                if isinstance(j, int):
                    if j < 0:
                        return
                    if j >= 2:
                        act.wait_ge(out_sent[par], 16 * (j // 2))
                else:
                    act.wait_ge(out_sent[par], (j - par) * 8)
                act.wait_ge(out_turned, j + 1)
                act.activation(out_rows[:, par, :, :], bank[6 + par][:, :].rearrange("p (t c) -> p t c", t=TB),
                               ACT.Copy).then_inc(out_staged, 1)
                act.wait_ge(out_staged, j + 1)
                act.dma_start(out[0].rearrange("(t p) d -> p t d", p=P)[:, :, bass.ds(j * P, P)],
                              out_rows[:, par, :, :]).then_inc(out_sent[par], 16)

            def attention(ph):
                for t in range(STEPS):
                    h, qb = t // TB, t % TB
                    if t < HEADS * TB:
                        n = (qb + 1) * P
                        act.wait_ge(max_ready, t + 1)
                        if t >= 2:
                            act.wait_ge(probs_turned, t - 1)
                        act.activation(probs[:, t % 2, 0:n], bank[t % 3][:, 0:n], ACT.Exp,
                                       bias=neg_max[:, t:t + 1], accum_out=row_sum[:, t:t + 1]).then_inc(exp_done, 1)
                    if 0 <= t - 2 < HEADS * TB:
                        tt = t - 2
                        h, qb = tt // TB, tt % TB
                        act.wait_ge(probs_turned, tt + 1)
                        if h >= 2:
                            act.wait_ge(pv_done, h - 1)
                        act.activation(pt_hi[h % 2][:, 0:qb + 1, qb * P:(qb + 1) * P],
                                       bank[4 + tt % 2][:, 0:(qb + 1) * P].rearrange("p (k q) -> p k q", q=P),
                                       ACT.Copy).then_inc(pthi_ready, 1)
                    if t >= 8 and (t - 8) % TB == 0:
                        h = (t - 8) // TB
                        p0 = (h % 2) * HD
                        act.wait_ge(pv_done, h + 1)
                        act.activation(cat_hi[p0:p0 + HD, CB + h // 2, :], bank[6 + h % 2][p0:p0 + HD, :], ACT.Copy)\
                            .then_inc(ohi_ready, 1)
                    for b in blocks_done_at(t):
                        act.wait_ge(conv_done, b + 1)
                        if b >= 2:
                            act.wait_ge(a_added, 1)
                        act.activation(sq[:, b % 2, :], conv[:, b, :], ACT.Square).then_inc(a_sq, 1)
                norm_root(am_ready, 1, a_mean[:, :], a_root[:, :], ar_ready)
                for b in range(CB):
                    act.wait_ge(a_scaled, b + 1)
                    if b >= 2:
                        act.wait_ge(alo_ready, b - 1)
                    act.activation(a_act[:, b % 2, :], a_nrm[:, b % 2, :], ACT.Silu,
                                   scale=vec[:, V_CN + b:V_CN + b + 1]).then_inc(a_acted, 1)
                    act.wait_ge(a_acted, b + 1)
                    act.activation(cat_hi[:, b, :], a_act[:, b % 2, :], ACT.Copy).then_inc(ahi_ready, 1)

            act.wait_ge(consts_ready, 3)
            act.activation(ident_r[:, :], ident[:, :], ACT.Copy).then_inc(identr_ready, 1)
            act.wait_ge(vec_ready, 2)
            act.activation(qk_gain[:, 0:1], vec[:, V_Q:V_Q + 1], ACT.Copy, scale=1.0 / math.sqrt(HD))\
                .then_inc(qgain_ready, 1)
            act.activation(qk_gain[:, 1:2], vec[:, V_Q + 1:V_Q + 2], ACT.Copy).then_inc(qgain_ready, 1)
            new_x(0, 0, 0)
            new_x(1, 1, 0)
            with act.Fori(1, KD // 2) as g:
                for half in range(2):
                    new_x(g * 2 + half, half, 0)
            split_hi(phases[0], 0, 0)
            split_hi(phases[0], 0, 1)
            for ph in phases:
                if ph.kind == "pair":
                    pair(ph)
                elif ph.kind == "resid":
                    resid(ph)
                elif ph.kind == "single":
                    for i in range(ph.units):
                        split_hi(ph, i // 4, i % 4 + 2)
                        act.wait_ge(y_out, i + 1)
                        act.activation(y_hi[:, i, :], hid[:, :], ACT.Copy).then_inc(yhi_ready, 1)
                elif ph.kind == "qk":
                    act.wait_ge(wf_arrived, 32)
                    act.wait_ge(wf_cleared, 2)
                    act.activation(wf_hi[:, :, 0:HEADS], wf_raw[:, :, :], ACT.Copy).then_inc(wfhi_ready, 1)
                    for i in range(ph.units):
                        split_hi(ph, i // 4, i % 4 + 2)
                        if i == 1:
                            act.wait_ge(lf_in, 1)
                            act.activation(lf[1][:, :], lf[0][:, :], ACT.Abs).then_inc(lf_abs, 1)
                            act.wait_ge(lf_abs, 1)
                            act.activation(lf[2][:, :], lf[1][:, :], ACT.Exp, scale=-1.0).then_inc(lf_exp, 1)
                            act.wait_ge(lf_exp, 1)
                            act.activation(lf[3][:, :], lf[2][:, :], ACT.Ln, bias=1.0).then_inc(lf_log, 1)
                        act.wait_ge(qk_out, i + 1)
                        if i >= 2:
                            act.wait_ge(qk_sum, i - 1)
                        act.activation(sq[:, i % 2, :], qk_raw[:, i, :], ACT.Square).then_inc(qk_sq, 1)
                elif ph.kind == "v":
                    split_hi(ph, 0, 2)
                    split_hi(ph, 0, 3)
                    norm_root(qk_mean, 1, mean_sq[0:2 * HEADS, :], root[0:2 * HEADS, :], qk_root)
                    for i in range(2, 4):
                        split_hi(ph, 0, i + 2)
                    act.wait_ge(unit_done, ph.unit0 + ph.units)
                    for tb in range(TB):
                        act.wait_ge(col_ready, 1)
                        act.activation(v_hi[:, tb, :], bank[tb][:, :], ACT.Copy, scale=rstd_col[:, tb:tb + 1])\
                            .then_inc(vhi_ready, 1)
                    act.wait_ge(qgain_ready, 2)
                    for t in range(QK):
                        dst = q_hi if t < AB else k_hi
                        act.wait_ge(qk_scaled, t + 1)
                        act.activation(dst[:, t % AB, :], qk_nrm[:, t % 2, :], ACT.Copy,
                                       scale=qk_gain[:, t // AB:t // AB + 1]).then_inc(qkhi_ready, 1)
                    act.wait_ge(cum_cleared, 2)
                    for r in range(0, CP, HD):
                        act.activation(cum_r[r:r + HEADS, :], cum[:, :], ACT.Copy).then_inc(cumhi_ready, 1)
                        act.activation(ncum_r[r:r + HEADS, :], cum[:, :], ACT.Copy, scale=-1.0)\
                            .then_inc(cumhi_ready, 1)
                    attention(ph)

        @block.vector
        def _(dve):
            links = [0]

            def link(instruction):
                links[0] += 1
                instruction.then_inc(step, 1)
                dve.wait_ge(step, links[0])

            def run_groups(ph, group):
                group(0)
                if ph.groups > 2:
                    with dve.Fori(1, ph.groups - 1) as g:
                        group(g)
                if ph.groups > 1:
                    group(ph.groups - 1)

            def split_lo(ph, g, u):
                if u >= 4 and isinstance(g, int) and g == ph.groups - 1:
                    ph, g, u = ph.next, 0, u - 4
                    if ph is None:
                        return
                n = ph.row_tiles * P
                dve.wait_ge(whi_ready, g * 4 + (ph.unit0 + u + 1))
                dve.tensor_tensor(w_lo[:, u % 2, 0:n], raw[:, u % 4, 0:n], raws(w_hi[:, u % 2, 0:n]), ALU.subtract)\
                    .then_inc(wlo_ready, 1)

            def xg_low(j, norm):
                dve.wait_ge(xhi_ready, j + (KD * norm + 1))
                one = bass.ds(j, 1)
                dve.scalar_tensor_tensor(xg_lo[:, one, :], x[:, one, :], vec[:, bass.ds(j + norm * KD, 1)],
                                         raws(xg_hi[:, one, :]), ALU.mult, ALU.subtract).then_inc(xlo_ready, 1)

            def invert(mean, rough_, corr_, out_, size):
                link(dve.tensor_tensor(corr_, rough_, rough_, ALU.mult))
                link(dve.scalar_tensor_tensor(corr_, corr_, -0.5, mean, ALU.mult, ALU.mult))
                return dve.scalar_tensor_tensor(out_, corr_, 1.5, rough_, ALU.add, ALU.mult)

            taps = [0]

            def conv_taps(n):
                for _ in range(n):
                    if taps[0] == TAPS * CB:
                        return
                    b, k = taps[0] // TAPS, TAPS - 1 - taps[0] % TAPS
                    wk = conv_w[:, k * CB + b:k * CB + b + 1]
                    shift = TAPS - 1 - k
                    if shift == 0:
                        dve.wait_ge(pair_out, A_GATE.pair0 + b + 1)
                        op = dve.tensor_scalar(conv[:, b, :], a_in[:, b, :], wk, vec[:, V_CB + b:V_CB + b + 1],
                                               ALU.mult, ALU.add)
                    else:
                        op = dve.scalar_tensor_tensor(conv[:, b, shift:S], a_in[:, b, 0:S - shift], wk,
                                                      conv[:, b, shift:S], ALU.mult, ALU.add)
                    if k == 0:
                        op.then_inc(conv_done, 1)
                    else:
                        link(op)
                    taps[0] += 1

            def pair(ph):
                def group(g):
                    first = isinstance(g, int) and g == 0
                    for u in range(4):
                        f, half = g * 2 + u // 2, u // 2
                        if not (first and u == 1):
                            split_lo(ph, g, u + 2)
                        if first and u == 0:
                            dve.wait_ge(ssq_done, ph.norm + 1)
                            dve.tensor_scalar(mean_sq[:, :], bank[6][:, :], 1.0 / D, EPS, ALU.mult, ALU.add)\
                                .then_inc(mean_ready, 1)
                            dve.wait_ge(root_ready, ph.norm + 1)
                            link(dve.reciprocal(rough[:, :], root[:, :]))
                            split_lo(ph, g, 3)
                            invert(mean_sq[:, :], rough[:, :], corr[:, :], rstd[:, :], D).then_inc(rstd_ready, 1)
                            dve.wait_ge(rstd_ready, ph.norm + 1)
                        dve.wait_ge(unit_done, g * 4 + (ph.unit0 + u + 1))
                        if u % 2 == 0:
                            dve.tensor_tensor(gate[:, half, :], bank[u][:, :], rstd[:, :], ALU.mult)\
                                .then_inc(gate_scaled, 1)
                            continue
                        dve.wait_ge(gate_ready, f + (ph.pair0 + 1))
                        if ph.gate == "silu":
                            dve.tensor_tensor(hid[:, :], bank[u][:, :], scaled[:, :], ALU.mult).then_inc(pair_out, 1)
                            dve.wait_ge(hhi_ready, f + (ph.h0 + 1))
                            one = bass.ds(f, 1)
                            dve.tensor_tensor(h_lo[:, one, :], hid[:, :].unsqueeze(1), raws(h_hi[:, one, :]),
                                              ALU.subtract).then_inc(hlo_ready, 1)
                        elif ph.gate == "sigmoid":
                            dve.tensor_tensor(a_in[:, f, :], bank[u][:, :], scaled[:, :], ALU.mult)\
                                .then_inc(pair_out, 1)
                            conv_taps(TAPS_A[f])
                        else:
                            c1, o1 = c_in[:, bass.ds(f, 1), :], c_out[:, bass.ds(f, 1), :]
                            dve.tensor_tensor(c1, bank[u][:, :].unsqueeze(1), scaled[:, :].unsqueeze(1), ALU.mult)\
                                .then_inc(pair_out, 1)
                            dve.wait_ge(pair_out, f + (ph.pair0 + 1))
                            for s in range(TAPS_C):
                                wk = vec[:, bass.ds(f + (V_OD + (TAPS_C - 1 - s) * KD), 1)]
                                if s == 0:
                                    op = dve.tensor_scalar(o1, c1, wk, None, ALU.mult)
                                else:
                                    o_, c_ = c_out[:, bass.ds(f, 1), s:S], c_in[:, bass.ds(f, 1), 0:S - s]
                                    op = dve.scalar_tensor_tensor(o_, c_, wk, o_, ALU.mult, ALU.add)
                                if s < TAPS_C - 1:
                                    op.then_inc(conv3_step, 1)
                                    dve.wait_ge(conv3_step, f * (TAPS_C - 1) + (s + 1))
                                else:
                                    op.then_inc(conv3_done, 1)

                run_groups(ph, group)

            def resid(ph):
                per_tile = 2 if ph.row_tiles == HALF else 1

                def group(g):
                    for u in range(4):
                        if u % per_tile == per_tile - 1:
                            j, half = g * (4 // per_tile) + u // per_tile, (u // per_tile) % 2
                            one = bass.ds(j, 1)
                            dve.wait_ge(unit_done, g * 4 + (ph.unit0 + u + 1))
                            ps = bank[4 + half][:, :].unsqueeze(1)
                            if ph is LAST:
                                if not isinstance(j, int) or j >= 2:
                                    dve.wait_ge(out_turned, j - 1)
                                dve.scalar_tensor_tensor(fin[:, half:half + 1, :], ps, ph.factor, x[:, one, :],
                                                         ALU.mult, ALU.add).then_inc(x_new, 1)
                            else:
                                dve.scalar_tensor_tensor(x[:, one, :], ps, ph.factor, x[:, one, :],
                                                         ALU.mult, ALU.add).then_inc(x_new, 1)
                        split_lo(ph, g, u + 2)
                        if u % per_tile == per_tile - 1 and ph is not LAST:
                            xg_low(j, ph.next_norm)

                run_groups(ph, group)

            def attention(ph):
                split_lo(ph, 0, 2)
                split_lo(ph, 0, 3)
                heads = slice(0, 2 * HEADS)
                dve.wait_ge(qk_sum, QK)
                dve.wait_ge(cum_ready, 1)
                dve.tensor_scalar(mean_sq[heads, :], bank[6][heads, :], 1.0 / HD, EPS, ALU.mult, ALU.add)\
                    .then_inc(qk_mean, 1)
                dve.wait_ge(qk_root, 1)
                link(dve.reciprocal(rough[heads, :], root[heads, :]))
                invert(mean_sq[heads, :], rough[heads, :], corr[heads, :], rstd[heads, :], HD).then_inc(qk_rstd, 1)
                split_lo(ph, 0, 4)
                split_lo(ph, 0, 5)
                for tb in range(TB):
                    dve.wait_ge(vhi_ready, tb + 1)
                    dve.scalar_tensor_tensor(v_lo[:, tb, :], bank[tb][:, :], rstd_col[:, tb:tb + 1],
                                             raws(v_hi[:, tb, :]), ALU.mult, ALU.subtract).then_inc(vlo_ready, 1)
                for t in range(QK):
                    lo, hi = (q_lo, q_hi) if t < AB else (k_lo, k_hi)
                    dve.wait_ge(qk_fanned, t + 1)
                    dve.tensor_tensor(qk_nrm[:, t % 2, :], qk_raw[:, t, :], bank[4 + t % 2][:, :], ALU.mult)\
                        .then_inc(qk_scaled, 1)
                    dve.wait_ge(qkhi_ready, t + 1)
                    dve.scalar_tensor_tensor(lo[:, t % AB, :], qk_nrm[:, t % 2, :], qk_gain[:, t // AB:t // AB + 1],
                                             raws(hi[:, t % AB, :]), ALU.mult, ALU.subtract).then_inc(qklo_ready, 1)
                dve.wait_ge(cumhi_ready, 2 * (CP // HD))
                for r in range(32, CP, HD):
                    dve.tensor_tensor(cum_r[r:r + HEADS, :], cum[:, :], raws(cum_r[0:HEADS, :]), ALU.subtract)\
                        .then_inc(cumlo_ready, 1)
                    dve.tensor_tensor(ncum_r[r:r + HEADS, :], raws(cum_r[0:HEADS, :]), cum[:, :], ALU.subtract)\
                        .then_inc(cumlo_ready, 1)
                for t in range(STEPS):
                    if t < HEADS * TB:
                        n = (t % TB + 1) * P
                        dve.wait_ge(scores_done, t + 1)
                        dve.tensor_reduce(neg_max[:, t:t + 1], bank[t % 3][:, 0:n], AX.X, ALU.max, negate=True)\
                            .then_inc(max_ready, 1)
                    if 0 <= t - 1 < HEADS * TB:
                        tt = t - 1
                        n = (tt % TB + 1) * P
                        dve.wait_ge(exp_done, tt + 1)
                        link(dve.reciprocal(row_inv[:, tt:tt + 1], row_sum[:, tt:tt + 1]))
                        dve.tensor_scalar(probs[:, tt % 2, 0:n], probs[:, tt % 2, 0:n], row_inv[:, tt:tt + 1], None,
                                          ALU.mult).then_inc(probs_ready, 1)
                    if 0 <= t - 2 < HEADS * TB:
                        tt = t - 2
                        h, qb = tt // TB, tt % TB
                        dve.wait_ge(pthi_ready, tt + 1)
                        dst = (slice(None), slice(0, qb + 1), slice(qb * P, (qb + 1) * P))
                        dve.tensor_tensor(pt_lo[h % 2][dst],
                                          bank[4 + tt % 2][:, 0:(qb + 1) * P].rearrange("p (k q) -> p k q", q=P),
                                          raws(pt_hi[h % 2][dst]), ALU.subtract).then_inc(ptlo_ready, 1)
                    if t >= 8 and (t - 8) % TB == 0:
                        h = (t - 8) // TB
                        p0 = (h % 2) * HD
                        dve.wait_ge(ohi_ready, h + 1)
                        dve.tensor_tensor(cat_lo[p0:p0 + HD, CB + h // 2, :], bank[6 + h % 2][p0:p0 + HD, :],
                                          raws(cat_hi[p0:p0 + HD, CB + h // 2, :]), ALU.subtract).then_inc(olo_ready, 1)
                    conv_taps(TAPS_T[t] if t < len(TAPS_T) else 0)
                dve.wait_ge(a_sum, 1)
                dve.tensor_scalar(a_mean[:, :], bank[3][:, :], 1.0 / CONV, EPS, ALU.mult, ALU.add).then_inc(am_ready, 1)
                dve.wait_ge(ar_ready, 1)
                link(dve.reciprocal(a_rough[:, :], a_root[:, :]))
                link(invert(a_mean[:, :], a_rough[:, :], a_corr[:, :], rstd[:, :], CONV))
                for b in range(CB):
                    if b >= 2:
                        dve.wait_ge(a_acted, b - 1)
                    dve.tensor_tensor(a_nrm[:, b % 2, :], conv[:, b, :], rstd[:, :], ALU.mult).then_inc(a_scaled, 1)
                    dve.wait_ge(ahi_ready, b + 1)
                    dve.tensor_tensor(cat_lo[:, b, :], a_act[:, b % 2, :], raws(cat_hi[:, b, :]), ALU.subtract)\
                        .then_inc(alo_ready, 1)

            dve.wait_ge(vec_turned, 2)
            dve.tensor_copy(vec[:, :], bank[7][:, 0:NVEC]).then_inc(vec_ready, 1)
            dve.tensor_copy(conv_w[:, :], bank[6][:, 0:TAPS * CB]).then_inc(vec_ready, 1)
            with dve.Fori(0, KD // 2) as g:
                for half in range(2):
                    dve.wait_ge(x_turned, g * 2 + (half + 1))
                    dve.tensor_copy(x[:, bass.ds(g * 2 + half, 1), :], bank[4 + half][:, :].unsqueeze(1))\
                        .then_inc(x_new, 1)
                    xg_low(g * 2 + half, 0)
            split_lo(phases[0], 0, 0)
            split_lo(phases[0], 0, 1)

            for ph in phases:
                if ph.kind == "pair":
                    pair(ph)
                elif ph.kind == "resid":
                    resid(ph)
                elif ph.kind == "single":
                    for i in range(ph.units):
                        split_lo(ph, i // 4, i % 4 + 2)
                        dve.wait_ge(unit_done, ph.unit0 + i + 1)
                        dve.wait_ge(y_gated, i + 1)
                        if i:
                            dve.wait_ge(ylo_ready, i)
                        dve.tensor_tensor(hid[:, :], bank[i % 4][:, :], c_out[:, i, :], ALU.mult).then_inc(y_out, 1)
                        dve.wait_ge(yhi_ready, i + 1)
                        dve.tensor_tensor(y_lo[:, i, :], hid[:, :], raws(y_hi[:, i, :]), ALU.subtract)\
                            .then_inc(ylo_ready, 1)
                elif ph.kind == "qk":
                    dve.wait_ge(wfhi_ready, 1)
                    dve.tensor_tensor(wf_lo[:, :, 0:HEADS], wf_raw[:, :, :], raws(wf_hi[:, :, 0:HEADS]), ALU.subtract)\
                        .then_inc(wflo_ready, 1)
                    dve.wait_ge(col_done, 1)
                    dve.tensor_copy(rstd_col[:, :].unsqueeze(2),
                                    bank[4][:, :].rearrange("p (t c) -> p t c", t=TB)[:, :, 0:1]).then_inc(col_ready, 1)
                    for i in range(ph.units):
                        split_lo(ph, i // 4, i % 4 + 2)
                        if i == 1:
                            dve.wait_ge(f_done, 1)
                            link(dve.tensor_tensor(lf[4][:, :], bank[7][0:HEADS, :], rstd[0:HEADS, :], ALU.mult))
                            dve.tensor_scalar(lf[0][:, :], lf[4][:, :], b_f[:, 0:1], None, ALU.add).then_inc(lf_in, 1)
                        if i == 2:
                            dve.wait_ge(lf_in, 1)
                            link(dve.tensor_scalar(lf[4][:, :], lf[0][:, :], 0.0, None, ALU.min))
                            dve.wait_ge(lf_log, 1)
                            link(dve.tensor_tensor(lf[1][:, :], lf[4][:, :], lf[3][:, :], ALU.subtract))
                            link(dve.memset(lf[2][:, :], 1.0))
                            dve.tensor_tensor_scan(cum[:, :], lf[2][:, :], lf[1][:, :], 0.0, ALU.mult, ALU.add)\
                                .then_inc(cum_ready, 1)
                        dve.wait_ge(unit_done, ph.unit0 + i + 1)
                        dve.tensor_tensor(qk_raw[:, i, :], bank[i % 4][:, :], rstd[:, :], ALU.mult).then_inc(qk_out, 1)
                        conv_taps(TAPS_QK[i])
                elif ph.kind == "v":
                    attention(ph)

        @block.tensor
        def _(pe):
            def product(dst, a, b, start, stop):
                pe.matmul(dst, a[0], b[0], start=start, stop=False)
                pe.matmul(dst, a[0], b[1], start=False, stop=False)
                return pe.matmul(dst, a[1], b[0], start=False, stop=stop)

            def weights(ph, u):
                return [unit_view(ph, t, u % 2) for t in (w_hi, w_lo)]

            def run_groups(ph, group):
                peeled = 2 if ph is LAST else 1
                for g in range(min(peeled, ph.groups)):
                    group(g)
                if ph.groups > peeled:
                    with pe.Fori(peeled, ph.groups) as g:
                        group(g)

            def projection(ph, g, u, wait_x=False):
                pe.wait_ge(wlo_ready, g * 4 + (ph.unit0 + u + 1))
                wh, wl = weights(ph, u)
                for k in range(KD):
                    if wait_x:
                        pe.wait_ge(xlo_ready, KD * ph.norm + k + 1)
                    last = product(bank[u][:, :], (wh[:, k, :], wl[:, k, :]), (xg_hi[:, k, :], xg_lo[:, k, :]),
                                   k == 0, k == KD - 1)
                last.then_inc(unit_done, 1)

            def pair(ph):
                def group(g):
                    first = isinstance(g, int) and g == 0
                    for u in range(4):
                        if not first:
                            pe.wait_ge((gate_scaled, pair_out)[u % 2], g * 2 + (ph.pair0 + u // 2 - 1))
                        projection(ph, g, u, wait_x=first and u == 0)
                        if first and u == 0:
                            pe.wait_ge(sq_added, KD * (ph.norm + 1))
                            pe.matmul(bank[6][:, :], ones[:, :], sq_sum[:, :], start=True, stop=True)\
                                .then_inc(ssq_done, 1)

                run_groups(ph, group)

            def resid(ph):
                per_tile = 2 if ph.row_tiles == HALF else 1
                hi, lo = SRC[ph.source]
                x0 = KD * ph.next_norm if ph is not LAST else X_LAST

                def group(g):
                    first = isinstance(g, int) and g == 0
                    for u in range(4):
                        pe.wait_ge(wlo_ready, g * 4 + (ph.unit0 + u + 1))
                        wh, wl = weights(ph, u)
                        j, half, part = g * (4 // per_tile) + u // per_tile, (u // per_tile) % 2, u % per_tile
                        if part == 0 and (not isinstance(j, int) or j >= 2):
                            pe.wait_ge(x_new, j + (x0 - 1))
                        order = list(range(ph.row_tiles))
                        if ph.source == "cat":
                            order = order[CB:] + order[:CB]
                        for n, k in enumerate(order):
                            kk = part * ph.row_tiles + k
                            if first and j == 0:
                                if ph.source == "h":
                                    pe.wait_ge(hlo_ready, phases[phases.index(ph) - 1].h0 + kk + 1)
                                elif ph.source == "y":
                                    pe.wait_ge(ylo_ready, kk + 1)
                                elif k >= CB:
                                    pe.wait_ge(olo_ready, 2 * (k - CB) + 2)
                                else:
                                    pe.wait_ge(alo_ready, k + 1)
                            last = product(bank[4 + half][:, :], (wh[:, k, :], wl[:, k, :]), (hi[:, kk, :], lo[:, kk, :]),
                                           part == 0 and n == 0, part == per_tile - 1 and n == len(order) - 1)
                        last.then_inc(unit_done, 1)
                        if ph is LAST and part == 1:
                            if half == 1 or not first:
                                turn_out(j - 1, 1 - half)

                run_groups(ph, group)
                if ph is LAST:
                    turn_out(KD - 1, 1)

            X_LAST = KD * 6

            def turn_out(j, half):
                pe.wait_ge(x_new, j + (X_LAST + 1))
                if not isinstance(j, int) or j >= 2:
                    pe.wait_ge(out_staged, j - 1)
                for tb in range(TB):
                    last = pe.transpose(bank[6 + half][:, tb * P:(tb + 1) * P], fin[:, half, tb * P:(tb + 1) * P],
                                        ident[:, :])
                last.then_inc(out_turned, 1)

            def attention():
                def scores(t):
                    h, qb = t // TB, t % TB
                    n, p0, j = (qb + 1) * P, (h % 2) * HD, h // 2
                    dst, qs = bank[t % 3], slice(qb * P, (qb + 1) * P)
                    rows = slice(p0, p0 + HD)
                    if t >= 3:
                        pe.wait_ge(exp_done, t - 2)
                    product(dst[:, 0:n], (q_hi[rows, j, qs], q_lo[rows, j, qs]),
                            (k_hi[rows, j, 0:n], k_lo[rows, j, 0:n]), True, False)
                    pe.matmul(dst[:, 0:n], row_sel[rows, h, :], ncum_r[rows, 0:n], start=False, stop=False)
                    for kb in range(qb + 1):
                        pe.matmul(dst[:, kb * P:(kb + 1) * P], cum_r[rows, qs], row_sel[rows, h, :], start=False, stop=False)
                    pe.matmul(dst[:, qs], ident_r[:, :], mask_r[:, :], start=False, stop=True).then_inc(scores_done, 1)

                for t in range(STEPS):
                    if t < HEADS * TB:
                        scores(t)
                    if 0 <= t - 2 < HEADS * TB:
                        tt = t - 2
                        pe.wait_ge(probs_ready, tt + 1)
                        if tt >= 2:
                            pe.wait_ge(ptlo_ready, tt - 1)
                        for kb in range(tt % TB + 1):
                            last = pe.transpose(bank[4 + tt % 2][:, kb * P:(kb + 1) * P],
                                                probs[:, tt % 2, kb * P:(kb + 1) * P], ident[:, :])
                        last.then_inc(probs_turned, 1)
                    if t >= 7 and (t - 7) % TB == 0 and (t - 7) // TB < HEADS:
                        h = (t - 7) // TB
                        pe.wait_ge(ptlo_ready, TB * (h + 1))
                        if h >= 2:
                            pe.wait_ge(olo_ready, h - 1)
                        cols = slice((h // 2) * P, (h // 2 + 1) * P)
                        for kb in range(TB):
                            last = product(bank[6 + h % 2][:, kb * P:S], (v_hi[:, kb, cols], v_lo[:, kb, cols]),
                                           (pt_hi[h % 2][:, kb, kb * P:S], pt_lo[h % 2][:, kb, kb * P:S]),
                                           kb == 0, kb == TB - 1)
                        last.then_inc(pv_done, 1)
                pe.wait_ge(a_added, CB - 1)
                pe.matmul(bank[3][:, :], ones[:, :], sq_sum[:, :], start=True, stop=True).then_inc(a_sum, 1)

            def head_sum(t):
                pe.wait_ge(qk_sq, t + 1)
                pe.matmul(bank[6][0:2 * HEADS, :], head_sel[:, t, :], sq[:, t % 2, :], start=t == 0, stop=t == QK - 1)\
                    .then_inc(qk_sum, 1)

            pe.wait_ge(consts_ready, 3)
            pe.wait_ge(vec_arrived, 16 * 15)
            pe.transpose(bank[7][:, 0:NVEC], vec_rows[:, :], ident[0:NVEC, 0:NVEC]).then_inc(vec_turned, 1)
            pe.wait_ge(conv_arrived, 16)
            pe.transpose(bank[6][:, 0:TAPS * CB], conv_rows[:, :], ident[0:TAPS * CB, 0:TAPS * CB])\
                .then_inc(vec_turned, 1)
            for j in range(KD):
                if j >= 2:
                    pe.wait_ge(x_new, j - 1)
                for tb in range(TB):
                    if j == 0 and tb % 2 == 0:
                        pe.wait_ge(x_arrived[tb // 2], 16)
                    last = pe.transpose(bank[4 + j % 2][:, tb * P:(tb + 1) * P], x_rows[:, tb, j * P:(j + 1) * P],
                                        ident[:, :])
                last.then_inc(x_turned, 1)

            for ph in phases:
                if ph.kind == "pair":
                    pair(ph)
                elif ph.kind == "resid":
                    resid(ph)
                elif ph.kind == "single":
                    for i in range(ph.units):
                        if i >= 4:
                            pe.wait_ge(y_out, i - 3)
                        else:
                            p_end = ph.pair_end
                            pe.wait_ge((gate_scaled, pair_out)[i % 2], p_end - 1 + i // 2)
                        projection(ph, i // 4, i % 4)
                elif ph.kind == "qk":
                    pe.wait_ge(rstd_ready, 2)
                    for tb in range(TB):
                        last = pe.transpose(bank[4][:, tb * P:(tb + 1) * P], rstd[:, tb * P:(tb + 1) * P], ident[:, :])
                    last.then_inc(col_done, 1)
                    pe.wait_ge(sel_ready, 2 + 2 * QK)
                    pe.wait_ge(identr_ready, 1)
                    for i in range(ph.units):
                        if i >= 4:
                            pe.wait_ge(qk_out, i - 3)
                        else:
                            pe.wait_ge((gate_scaled, pair_out)[i % 2], A_GATE.pair0 + CB - 1 + i // 2)
                        projection(ph, i // 4, i % 4)
                        if i == 0:
                            pe.wait_ge(wflo_ready, 1)
                            for k in range(KD):
                                last = product(bank[7][:, :], (wf_hi[:, k, :], wf_lo[:, k, :]),
                                               (xg_hi[:, k, :], xg_lo[:, k, :]), k == 0, k == KD - 1)
                            last.then_inc(f_done, 1)
                        else:
                            head_sum(i - 1)
                elif ph.kind == "v":
                    for u in range(ph.units):
                        pe.wait_ge(wlo_ready, ph.unit0 + u + 1)
                        wh, wl = weights(ph, u)
                        for tb in range(TB):
                            if u == 0:
                                pe.wait_ge(qk_out, QK - TB + tb + 1)
                            ts = slice(tb * P, (tb + 1) * P)
                            for k in range(2):
                                kk = 2 * u + k
                                last = product(bank[tb][:, :], (xg_hi[:, kk, ts], xg_lo[:, kk, ts]),
                                               (wh[:, k, :], wl[:, k, :]), kk == 0, kk == KD - 1)
                        last.then_inc(unit_done, 1)
                        if u == 0:
                            head_sum(QK - 1)
                    pe.wait_ge(qk_rstd, 1)
                    pe.wait_ge(fan_ready, 2)
                    pe.wait_ge(col_ready, 1)
                    for t in range(QK):
                        if t >= 2:
                            pe.wait_ge(qk_scaled, t - 1)
                        pe.matmul(bank[4 + t % 2][:, :], head_fan[:, t, :], rstd[0:2 * HEADS, :], start=True, stop=True)\
                            .then_inc(qk_fanned, 1)
                    pe.wait_ge(qklo_ready, QK)
                    pe.wait_ge(cumlo_ready, 2 * (CP // HD))
                    pe.wait_ge(rsel_ready, 1)
                    pe.wait_ge(vlo_ready, TB)
                    attention()


_INS = ["x", "ffn1_norm", "ffn1_w_gate", "ffn1_w_up", "ffn1_w_down", "mix_norm", "ffn2_norm", "ffn2_w_gate",
        "ffn2_w_up", "ffn2_w_down", "ev_w_in", "ev_b_f", "ev_conv_w", "ev_conv_b", "ev_conv_norm", "ev_q_norm",
        "ev_k_norm", "ev_w_out", "od_w_in", "od_conv_w", "od_w_out"]


def kernel(**inputs):
    import numpy as np
    from concourse import bacc
    from concourse.bass_utils import run_bass_kernel_spmd

    nc = bacc.Bacc("TRN2", target_bir_lowering=False, num_devices=1)
    arrays, t_in = {}, {}
    for name in _INS:
        a = np.ascontiguousarray(inputs[name])
        arrays[f"in_{name}"] = a
        t_in[name] = nc.dram_tensor(f"in_{name}", a.shape, mybir.dt.from_np(a.dtype), kind="ExternalInput").ap()
    out = nc.dram_tensor("out", inputs["x"].shape, mybir.dt.float32, kind="ExternalOutput").ap()
    trunk(nc, t_in, out)
    return run_bass_kernel_spmd(nc, [arrays], core_ids=[0]).results[0]["out"]
```

```python
import math
from contextlib import ExitStack

import concourse.bass as bass
from concourse import mybir

P = 128
BANKS = 8
EPS = 1e-6
MASKED = -1.0e30


class Phase:

    def __init__(self, kind, units, row_tiles, **more):
        self.kind, self.units, self.row_tiles = kind, units, row_tiles
        self.groups = units // 4
        self.norm = more.get("norm")
        self.next_norm = more.get("next_norm")
        self.gate = more.get("gate")
        self.source = more.get("source")
        self.weights = more.get("weights")
        self.factor = more.get("factor", 1.0)
        self.next = None


def plan(phases):
    unit = pair = gate_act = h = 0
    for n, ph in enumerate(phases):
        ph.unit0, ph.pair0, ph.act0, ph.h0, ph.pair_end = unit, pair, gate_act, h, pair
        unit += ph.units
        if ph.kind == "pair":
            pair += ph.units // 2
            if ph.gate != "none":
                gate_act += ph.units // 2
            if ph.gate == "silu":
                h += ph.units // 2
        if n:
            phases[n - 1].next = ph
    return phases


def trunk(nc, t_in, out):
    f32, f32r = mybir.dt.float32, mybir.dt.float32r
    ACT, ALU, AX = mybir.ActivationFunctionType, mybir.AluOpType, mybir.AxisListType

    x_in = t_in["x"]
    _, S, D = x_in.shape
    FF = t_in["ffn1_w_gate"].shape[2]
    CONV = t_in["ev_conv_w"].shape[2]
    TAPS = t_in["ev_conv_w"].shape[1]
    TAPS_C = t_in["od_conv_w"].shape[1]
    HEADS = t_in["ev_b_f"].shape[1]
    HD = t_in["ev_q_norm"].shape[1]
    ATT = HEADS * HD
    KD, KF, TB = D // P, FF // P, S // P
    CB, AB = CONV // P, ATT // P
    HALF = KF // 2
    QK = 2 * AB

    w = {k: v[0] if v.shape[0] == 1 else v for k, v in t_in.items() if k.startswith(("ev_w", "od_w"))}

    def swiglu(name, layer, norm, next_norm):
        return [
            Phase("pair", 2 * KF, KD, norm=norm, gate="silu",
                  weights=(t_in[name + "_w_gate"][layer], 0, t_in[name + "_w_up"][layer], 0)),
            Phase("resid", 2 * KD, HALF, next_norm=next_norm, source="h", factor=0.5,
                  weights=t_in[name + "_w_down"][layer]),
        ]

    even_in, odd_in = w["ev_w_in"], w["od_w_in"]
    phases = plan(
        swiglu("ffn1", 0, 0, 1)
        + [Phase("pair", 2 * CB, KD, norm=1, gate="sigmoid", weights=(even_in, CONV, even_in, 0)),
           Phase("qk", QK, KD, norm=1, weights=(even_in, 2 * CONV)),
           Phase("v", KD // 2, KD, norm=1, weights=(even_in, 2 * CONV + 2 * ATT)),
           Phase("resid", KD, KD, next_norm=2, source="cat", weights=w["ev_w_out"])]
        + swiglu("ffn2", 0, 2, 3)
        + swiglu("ffn1", 1, 3, 4)
        + [Phase("pair", 2 * KD, KD, norm=4, gate="none", weights=(odd_in, D, odd_in, 2 * D)),
           Phase("single", KD, KD, norm=4, weights=(odd_in, 0)),
           Phase("resid", KD, KD, next_norm=5, source="y", weights=w["od_w_out"])]
        + swiglu("ffn2", 1, 5, None)
    )
    A_GATE, QKP, VP, A_OUT = phases[2], phases[3], phases[4], phases[5]
    LAST = phases[-1]
    TOTAL = LAST.unit0 + LAST.units

    base = -(-nc.sbuf_base // 64) * 64
    end = [base]

    def room(nbytes):
        at = end[0]
        end[0] += -(-nbytes // 32) * 32
        return at

    def at(name, shape, dt, offset):
        return nc.alloc_sbuf_tensor_at(name, shape, dt, offset=offset)

    def own(name, shape, dt=f32):
        return at(name, shape, dt, room(4 * math.prod(shape[1:])))

    ROW = 4 * S
    SLOT = P * HALF
    x = own("x", [P, KD, S])
    XG = room(2 * KD * ROW)
    xg_hi, xg_lo = at("xg_hi", [P, KD, S], f32r, XG), at("xg_lo", [P, KD, S], f32r, XG + KD * ROW)
    H = room(2 * KF * ROW)
    h_hi, h_lo = at("h_hi", [P, KF, S], f32r, H), at("h_lo", [P, KF, S], f32r, H + KF * ROW)
    raw = own("raw", [P, 4, SLOT])
    w_hi, w_lo = own("w_hi", [P, 2, SLOT], f32r), own("w_lo", [P, 2, SLOT], f32r)
    rstd = own("rstd", [P, S])
    GATE, ACTED, SCALED, HID = room(2 * ROW), room(2 * ROW), room(ROW), room(ROW)
    gate = at("gate", [P, 2, S], f32, GATE)
    acted = at("acted", [P, 2, S], f32, ACTED)
    scaled = at("scaled", [P, S], f32, SCALED)
    hid = at("hid", [P, S], f32, HID)
    sq = own("sq", [P, 2, S])
    sq_sum = own("sq_sum", [P, S])
    cum = own("cum", [HEADS, S])
    ident, ones = own("ident", [P, P]), own("ones", [P, P])
    ident_r, mask_r = own("ident_r", [P, P], f32r), own("mask_r", [P, P], f32r)
    GAINS = 6 * KD
    GAIN_COL = [(n % 3 * 2 + n // 3) * KD for n in range(6)]
    FIRST = 2 * KD
    V_CB, V_CN, V_OD = GAINS, GAINS + CB, GAINS + 2 * CB
    V_Q = V_OD + TAPS_C * KD
    NVEC = V_Q + 2
    vec = own("vec", [P, NVEC])
    conv_w = own("conv_w", [P, TAPS * CB])
    qk_gain = own("qk_gain", [P, 2])
    head_sel = own("head_sel", [P, QK, 2 * HEADS])
    wf_raw = own("wf_raw", [P, KD, HEADS])
    b_f = own("b_f", [HEADS, 1])
    rstd_col = own("rstd_col", [P, TB])
    neg_max = own("neg_max", [P, HEADS * TB])
    row_sum, row_inv = own("row_sum", [P, HEADS * TB]), own("row_inv", [P, HEADS * TB])

    mean_sq, root = at("mean_sq", [P, S], f32, GATE), at("root", [P, S], f32, GATE + ROW)
    rough, corr = at("rough", [P, S], f32, ACTED), at("corr", [P, S], f32, ACTED + ROW)

    x_rows = at("x_rows", [P, TB, D], f32, H)
    first_rows = at("first_rows", [FIRST, P], f32, H + TB * D * 4)
    vec_rows = at("vec_rows", [NVEC - FIRST, P], f32, H + TB * D * 4 + 4 * P)
    conv_rows = at("conv_rows", [TAPS * CB, P], f32, H + TB * D * 4 + 8 * P)

    q_hi, q_lo = at("q_hi", [P, AB, S], f32r, H), at("q_lo", [P, AB, S], f32r, H + AB * ROW)
    k_hi, k_lo = at("k_hi", [P, AB, S], f32r, H + 2 * AB * ROW), at("k_lo", [P, AB, S], f32r, H + 3 * AB * ROW)
    VAT = H + 4 * AB * ROW
    v_hi, v_lo = at("v_hi", [P, TB, ATT], f32r, VAT), at("v_lo", [P, TB, ATT], f32r, VAT + TB * ATT * 4)
    wf_hi, wf_lo = at("wf_hi", [P, KD, P], f32r, VAT), at("wf_lo", [P, KD, P], f32r, VAT + KD * P * 4)
    CAT = VAT + 2 * TB * ATT * 4
    cat_hi, cat_lo = at("cat_hi", [P, KD, S], f32r, CAT), at("cat_lo", [P, KD, S], f32r, CAT + KD * ROW)
    conv = at("conv", [P, CB, S], f32, CAT)
    qk_raw = at("qk_raw", [P, QK, S], f32, CAT + KD * ROW)
    AIN = CAT + 2 * KD * ROW
    a_in = at("a_in", [P, CB, S], f32, AIN)
    assert AIN + CB * ROW <= H + 2 * KF * ROW
    a_mean, a_root = at("a_mean", [P, S], f32, ACTED), at("a_root", [P, S], f32, ACTED + ROW)
    a_rough, a_corr = at("a_rough", [P, S], f32, SCALED), at("a_corr", [P, S], f32, HID)
    a_nrm = at("a_nrm", [P, 2, S], f32, ACTED)
    a_act = [at(f"a_act{b}", [P, S], f32, off)
             for b, off in enumerate((SCALED, HID, AIN + 2 * ROW, AIN + 3 * ROW))]
    assert HID == SCALED + ROW
    head_fan = at("head_fan", [2 * HEADS, QK, P], f32, SCALED)
    qk_nrm = at("qk_nrm", [P, 2, S], f32, ACTED)
    lf = [at(f"lf{i}", [HEADS, S], f32, H + (AB + i) * ROW) for i in range(5)]
    tap_prod = at("tap_prod", [P, 2, S], f32, H)
    CP = P
    row_sel = at("row_sel", [CP, HEADS, P], f32r, GATE)
    cum_r, ncum_r = at("cum_r", [CP, S], f32r, AIN), at("ncum_r", [CP, S], f32r, AIN + ROW)
    NPR = 4
    probs = at("probs", [P, NPR, S], f32, CAT + KD * ROW)
    pt_hi = [at(f"pt_hi{i}", [P, TB, S], f32r, XG + 2 * i * TB * ROW) for i in range(2)]
    pt_lo = [at(f"pt_lo{i}", [P, TB, S], f32r, XG + (2 * i + 1) * TB * ROW) for i in range(2)]
    y_hi, y_lo = at("y_hi", [P, KD, S], f32r, H), at("y_lo", [P, KD, S], f32r, H + KD * ROW)
    c_in = at("c_in", [P, KD, S], f32, H + 2 * KD * ROW)
    c_out = at("c_out", [P, KD, S], f32, H + 3 * KD * ROW)
    fin = at("fin", [P, 2, S], f32, XG)
    out_rows = at("out_rows", [P, 2, TB, P], f32, XG + 2 * ROW)
    assert end[0] <= nc.sbuf_top, (end[0], nc.sbuf_top)

    DVE_TILES = CB - 1
    TAPS_A, TAPS_QK = [0, 8, 10, 4], [5] * QK
    left = TAPS * DVE_TILES - sum(TAPS_A) - sum(TAPS_QK)
    TAPS_T = [0] * 3 + [2] * (left // 2) + [left % 2]
    ACT_TAPS = [4] * QK
    assert sum(ACT_TAPS) >= TAPS and sum(TAPS_A) + sum(TAPS_QK) >= 2 * TAPS
    SCALE_LAG, TURN_LAG = 2, 3
    PV_LAG, OUT_LAG = TURN_LAG + 2, TURN_LAG + 3
    STEPS = HEADS * TB + OUT_LAG
    A_STEP = len(TAPS_T) + 2
    HEAD_ORDER = [half * AB + j for j in range(AB) for half in range(2)]

    SRC = {"h": (h_hi, h_lo), "cat": (cat_hi, cat_lo), "y": (y_hi, y_lo)}

    def raws(ap):
        return ap.bitcast(f32)

    with ExitStack() as ctx:
        bank = [ctx.enter_context(nc.psum_tensor(f"bank{i}", [P, S], f32)) for i in range(BANKS)]

        def sem(name):
            return ctx.enter_context(nc.semaphore(name))

        x_arrived = [sem(f"x_arrived{i}") for i in range(4)]
        first_arrived, first_turned, first_ready = sem("first_arrived"), sem("first_turned"), sem("first_ready")
        tap_made, tap_added = sem("tap_made"), sem("tap_added")
        vec_arrived, conv_arrived, wf_arrived = sem("vec_arrived"), sem("conv_arrived"), sem("wf_arrived")
        w_arrived = [sem(f"w_arrived{i}") for i in range(4)]
        consts_ready, sel_ready, vec_turned, vec_ready = (
            sem("consts_ready"), sem("sel_ready"), sem("vec_turned"), sem("vec_ready"))
        qgain_ready, mask_cleared, identr_ready = (
            sem("qgain_ready"), sem("mask_cleared"), sem("identr_ready"))
        whi_ready, wlo_ready, unit_done = sem("whi_ready"), sem("wlo_ready"), sem("unit_done")
        x_turned = sem("x_turned")
        x_new, xhi_ready, xlo_ready = sem("x_new"), sem("xhi_ready"), sem("xlo_ready")
        sq_ready, sq_added, sq_cleared = sem("sq_ready"), sem("sq_added"), sem("sq_cleared")
        ssq_done, mean_ready, root_ready, rstd_ready = (
            sem("ssq_done"), sem("mean_ready"), sem("root_ready"), sem("rstd_ready"))
        gate_scaled, gate_acted, gate_ready, pair_out = (
            sem("gate_scaled"), sem("gate_acted"), sem("gate_ready"), sem("pair_out"))
        hhi_ready, hlo_ready = sem("hhi_ready"), sem("hlo_ready")
        step = sem("step")
        wf_cleared, wfhi_ready, wflo_ready, f_done = (
            sem("wf_cleared"), sem("wfhi_ready"), sem("wflo_ready"), sem("f_done"))
        col_done, col_ready = sem("col_done"), sem("col_ready")
        lf_in, lf_abs, lf_exp, lf_log, cum_ready = (
            sem("lf_in"), sem("lf_abs"), sem("lf_exp"), sem("lf_log"), sem("cum_ready"))
        cum_cleared, cumhi_ready, cumlo_ready = sem("cum_cleared"), sem("cumhi_ready"), sem("cumlo_ready")
        fan_ready, rsel_ready, rsel_step = sem("fan_ready"), sem("rsel_ready"), sem("rsel_step")
        qk_out, qk_sq, qk_sum = sem("qk_out"), sem("qk_sq"), sem("qk_sum")
        qk_mean, qk_root, qk_rstd, qk_fanned = sem("qk_mean"), sem("qk_root"), sem("qk_rstd"), sem("qk_fanned")
        qk_scaled, qkhi_ready, qklo_ready = sem("qk_scaled"), sem("qkhi_ready"), sem("qklo_ready")
        vhi_ready, vlo_ready = sem("vhi_ready"), sem("vlo_ready")
        scores_done, max_ready, exp_done, probs_ready = (
            sem("scores_done"), sem("max_ready"), sem("exp_done"), sem("probs_ready"))
        probs_turned, pthi_ready, ptlo_ready, pv_done = (
            sem("probs_turned"), sem("pthi_ready"), sem("ptlo_ready"), sem("pv_done"))
        ohi_ready, olo_ready = sem("ohi_ready"), sem("olo_ready")
        conv_done, a_sq, a_added, a_sum = sem("conv_done"), sem("a_sq"), sem("a_added"), sem("a_sum")
        am_ready, ar_ready = sem("am_ready"), sem("ar_ready")
        a_scaled, a_acted, ahi_ready, alo_ready = (
            sem("a_scaled"), sem("a_acted"), sem("ahi_ready"), sem("alo_ready"))
        conv3_step, conv3_done, y_gated = sem("conv3_step"), sem("conv3_done"), sem("y_gated")
        y_out, yhi_ready, ylo_ready = sem("y_out"), sem("yhi_ready"), sem("ylo_ready")
        out_turned, out_staged = sem("out_turned"), sem("out_staged")
        out_sent = [sem(f"out_sent{i}") for i in range(2)]

        block = ctx.enter_context(nc.Block())

        def unit_view(ph, tensor, slot):
            if ph.kind == "v":
                return tensor[:, slot, 0:2 * ATT].rearrange("p (k n) -> p k n", k=2)
            return tensor[:, slot, 0:ph.row_tiles * P].rearrange("p (k n) -> p k n", k=ph.row_tiles)

        @block.sync
        def _(sp):
            def load(ph, g, u):
                if isinstance(ph.weights, tuple) and ph.kind == "pair":
                    gw, gc, uw, uc = ph.weights
                    src, c0 = (gw, gc) if u % 2 == 0 else (uw, uc)
                    rows = src.rearrange("(k p) n -> p k n", p=P)
                    src = rows[:, :, bass.ds(c0 + (g * 2 + u // 2) * P, P)]
                elif ph.kind == "resid" and ph.row_tiles == HALF:
                    rows = ph.weights.rearrange("(k p) n -> p k n", p=P)
                    k0 = (u % 2) * HALF
                    src = rows[:, k0:k0 + HALF, bass.ds((g * 2 + u // 2) * P, P)]
                elif ph.kind == "v":
                    src = ph.weights[0].rearrange("(k p) n -> p k n", p=P)
                    src = src[:, 2 * u:2 * u + 2, ph.weights[1]:ph.weights[1] + ATT]
                else:
                    ww, c0 = ph.weights if isinstance(ph.weights, tuple) else (ph.weights, 0)
                    src = ww.rearrange("(k p) n -> p k n", p=P)[:, :, bass.ds(c0 + (g * 4 + u) * P, P)]
                if isinstance(g, int):
                    if ph.unit0 + 4 * g + u >= 4:
                        sp.wait_ge(wlo_ready, ph.unit0 + 4 * g + u - 3)
                else:
                    sp.wait_ge(wlo_ready, g * 4 + (ph.unit0 + u - 3))
                sp.dma_start(unit_view(ph, raw, u), src).then_inc(w_arrived[u], 16)

            QD = D // len(x_arrived)
            for i in range(len(x_arrived)):
                cols = slice(i * QD, (i + 1) * QD)
                sp.dma_start(x_rows[:, :, cols], x_in[0].rearrange("(t p) d -> p t d", p=P)[:, :, cols])\
                    .then_inc(x_arrived[i], 16)
                if i == 1:
                    load(phases[0], 0, 0)
            for ph in phases:
                for u in range(4):
                    if ph is not phases[0] or u > 0:
                        load(ph, 0, u)
                if ph.groups > 1:
                    with sp.Fori(1, ph.groups) as g:
                        for u in range(4):
                            load(ph, g, u)

        @block.gpsimd
        def _(pool):
            pool.memset(ident[:, :], 0.0).then_inc(consts_ready, 1)
            pool.memset(ones[:, :], 1.0).then_inc(consts_ready, 1)
            pool.memset(sq_sum[:, :], 0.0).then_inc(sq_cleared, 1)
            pool.wait_ge(consts_ready, 2)
            pool.affine_select(out=ident[:, :], in_=ident[:, :], compare_op=ALU.not_equal, fill=1.0, base=0,
                               pattern=[[-1, P]], channel_multiplier=1).then_inc(consts_ready, 1)
            pool.memset(head_sel[:, :, :], 0.0).then_inc(sel_ready, 1)
            pool.wait_ge(sel_ready, 1)
            for t in range(QK):
                for half in range(2):
                    pool.memset(head_sel[half * HD:(half + 1) * HD, t, 2 * t + half:2 * t + half + 1], 1.0)\
                        .then_inc(sel_ready, 1)
            pool.wait_ge(sel_ready, 1 + 2 * QK)
            pool.memset(raws(mask_r[:, :]), 0.0).then_inc(mask_cleared, 1)
            pool.wait_ge(mask_cleared, 1)
            pool.affine_select(out=mask_r[:, :], in_=raws(mask_r[:, :]), compare_op=ALU.is_ge, fill=MASKED, base=0,
                               pattern=[[-1, P]], channel_multiplier=1).then_inc(sel_ready, 1)

            def add_squares(norm):
                if norm:
                    pool.wait_ge(ssq_done, norm)
                    pool.memset(sq_sum[:, :], 0.0).then_inc(sq_cleared, 1)
                pool.wait_ge(sq_cleared, norm + 1)
                with pool.Fori(0, KD // 2) as g:
                    for half in range(2):
                        pool.wait_ge(sq_ready, g * 2 + (KD * norm + half + 1))
                        pool.tensor_tensor(sq_sum[:, :], sq_sum[:, :], sq[:, half, :], ALU.add)\
                            .then_inc(sq_added, 1)
                        pool.wait_ge(sq_added, g * 2 + (KD * norm + half + 1))

            def gates(ph):
                pool.wait_ge(rstd_ready, ph.norm + 1)
                n = ph.units // 2

                def one(f, par):
                    src = gate if ph.gate == "none" else acted
                    if ph.gate == "none":
                        pool.wait_ge(gate_scaled, f + (ph.pair0 + 1))
                    else:
                        pool.wait_ge(gate_acted, f + (ph.act0 + 1))
                    if not isinstance(f, int) or ph.pair0 + f > 0:
                        pool.wait_ge(pair_out, f + ph.pair0)
                    pool.tensor_tensor(scaled[:, :], src[:, par, :], rstd[:, :], ALU.mult).then_inc(gate_ready, 1)

                one(0, 0)
                one(1, 1)
                with pool.Fori(1, n // 2) as g:
                    for par in range(2):
                        one(g * 2 + par, par)

            for ph in phases:
                if ph.norm == 0 and ph.kind == "pair":
                    add_squares(0)
                if ph is A_GATE:
                    pool.wait_ge(unit_done, ph.unit0)
                    pool.memset(raws(wf_hi[:, :, :]), 0.0).then_inc(wf_cleared, 1)
                    pool.memset(raws(wf_lo[:, :, :]), 0.0).then_inc(wf_cleared, 1)
                if ph.kind == "pair":
                    gates(ph)
                if ph.kind == "single":
                    with pool.Fori(0, KD) as f:
                        pool.wait_ge(conv3_done, f + 1)
                        tile = c_out[:, bass.ds(f, 1), :]
                        pool.tensor_tensor(tile, tile, rstd[:, :].unsqueeze(1), ALU.mult).then_inc(y_gated, 1)
                if ph is A_GATE:
                    pool.wait_ge(pair_out, ph.pair0 + CB)
                    pool.memset(head_fan[:, :, :], 0.0).then_inc(fan_ready, 1)
                    pool.wait_ge(fan_ready, 1)
                    view = head_fan[:, :, :].rearrange("r t (a c) -> r t a c", a=2)
                    pool.affine_select(out=view, in_=view, compare_op=ALU.not_equal, fill=1.0, base=0,
                                       pattern=[[-2, QK], [-1, 2], [0, HD]], channel_multiplier=1)\
                        .then_inc(fan_ready, 1)
                    pool.wait_ge(fan_ready, 2)
                    for n in range(1, TAPS):
                        pool.wait_ge(tap_made, n + 1)
                        if n >= 2:
                            pool.wait_ge(tap_added, n - 1)
                        pool.tensor_tensor(conv[:, CB - 1, n:S], conv[:, CB - 1, n:S], tap_prod[:, n % 2, 0:S - n],
                                           ALU.add).then_inc(tap_added, 1)
                if ph is VP:
                    pool.wait_ge(conv_done, 2)
                    pool.memset(raws(cum_r[:, :]), 0.0).then_inc(cum_cleared, 1)
                    pool.memset(raws(ncum_r[:, :]), 0.0).then_inc(cum_cleared, 1)
                    pool.wait_ge(qk_rstd, 1)
                    pool.memset(raws(row_sel[:, :, :]), 0.0).then_inc(rsel_step, 1)
                    for n, off in enumerate(range(0, CP, 32)):
                        pool.wait_ge(rsel_step, n + 1)
                        pool.affine_select(out=row_sel[:, :, :], in_=raws(row_sel[:, :, :]), compare_op=ALU.not_equal,
                                           fill=1.0, base=-off, pattern=[[-1, HEADS], [0, P]],
                                           channel_multiplier=1).then_inc(rsel_ready if off == CP - 32 else rsel_step, 1)
                    pool.wait_ge(ssq_done, 2)
                    for b in range(1, CB):
                        pool.wait_ge(a_sq, b + 1)
                        if b > 1:
                            pool.wait_ge(a_added, b - 1)
                        first = sq[:, 0, :] if b == 1 else sq_sum[:, :]
                        pool.tensor_tensor(sq_sum[:, :], first, sq[:, b % 2, :], ALU.add).then_inc(a_added, 1)
                if ph.kind == "resid" and ph.next_norm is not None:
                    if ph is A_OUT:
                        pool.wait_ge(a_sum, 1)
                    add_squares(ph.next_norm)

        @block.scalar
        def _(act):
            act.dma_start(first_rows[:, :], t_in["ffn1_norm"].rearrange("l (k p) -> (l k) p", p=P))\
                .then_inc(first_arrived, 16)
            for n, name in enumerate(("mix_norm", "ffn2_norm")):
                act.dma_start(vec_rows[n * 2 * KD:(n + 1) * 2 * KD, :],
                              t_in[name].rearrange("l (k p) -> (l k) p", p=P)).then_inc(vec_arrived, 16)
            for name, r0, r1 in (("ev_conv_b", V_CB, V_CN), ("ev_conv_norm", V_CN, V_OD)):
                act.dma_start(vec_rows[r0 - FIRST:r1 - FIRST, :], t_in[name].rearrange("o (k p) -> (o k) p", p=P))\
                    .then_inc(vec_arrived, 16)
            act.dma_start(vec_rows[V_OD - FIRST:V_Q - FIRST, :],
                          t_in["od_conv_w"][0].rearrange("t (k p) -> (t k) p", p=P)).then_inc(vec_arrived, 16)
            for n, name in enumerate(("ev_q_norm", "ev_k_norm")):
                for half in range(2):
                    act.dma_start(vec_rows[V_Q + n - FIRST:V_Q + n + 1 - FIRST, half * HD:(half + 1) * HD], t_in[name])\
                        .then_inc(vec_arrived, 16)
            act.dma_start(conv_rows[:, :], t_in["ev_conv_w"][0].rearrange("t (b p) -> (t b) p", p=P))\
                .then_inc(conv_arrived, 16)
            act.dma_start(wf_raw[:, :, :],
                          even_in.rearrange("(k p) n -> p k n", p=P)[:, :, 2 * CONV + 3 * ATT:])\
                .then_inc(wf_arrived, 16)
            act.dma_start(b_f[:, :], t_in["ev_b_f"].rearrange("o h -> h o")).then_inc(wf_arrived, 16)

            def split_hi(ph, g, u):
                if u >= 4 and isinstance(g, int) and g == ph.groups - 1:
                    ph, g, u = ph.next, 0, u - 4
                    if ph is None:
                        return
                n = ph.row_tiles * P
                i = ph.unit0 + u if not isinstance(g, int) else ph.unit0 + u + 4 * g
                if isinstance(g, int):
                    act.wait_ge(w_arrived[u % 4], 16 * (i // 4 + 1))
                    if i >= 2:
                        act.wait_ge(unit_done, i - 1)
                else:
                    act.wait_ge(w_arrived[u % 4], g * 16 + 16 * (i // 4 + 1))
                    act.wait_ge(unit_done, g * 4 + (i - 1))
                act.activation(w_hi[:, u % 2, 0:n], raw[:, u % 4, 0:n], ACT.Copy).then_inc(whi_ready, 1)

            def new_x(j, half, norm):
                act.wait_ge(x_new, j + (KD * norm + 1))
                if not isinstance(j, int) or KD * norm + j >= 2:
                    act.wait_ge(sq_added, j + (KD * norm - 1))
                one = bass.ds(j, 1)
                act.activation(xg_hi[:, one, :], x[:, one, :], ACT.Copy, scale=vec[:, bass.ds(j + GAIN_COL[norm], 1)])\
                    .then_inc(xhi_ready, 1)
                act.activation(sq[:, half:half + 1, :], x[:, one, :], ACT.Square).then_inc(sq_ready, 1)

            def norm_root(ready, n, mean, out_root, done):
                act.wait_ge(ready, n)
                act.activation(out_root, mean, ACT.Sqrt).then_inc(done, 1)

            def pair(ph):
                def group(g):
                    first = isinstance(g, int) and g == 0
                    for u in range(4):
                        f, par = g * 2 + u // 2, u // 2
                        if not (first and u in (1, 2)):
                            split_hi(ph, g, u + 2)
                        if first and u == 1:
                            split_hi(ph, g, 4)
                        if ph is A_GATE and not first and u == 0:
                            act.wait_ge(wf_arrived, 32)
                            act.wait_ge(wf_cleared, 2)
                            act.activation(wf_hi[:, :, 0:HEADS], wf_raw[:, :, :], ACT.Copy).then_inc(wfhi_ready, 1)
                        if first and u == 0:
                            norm_root(mean_ready, ph.norm + 1, mean_sq[:, :], root[:, :], root_ready)
                            split_hi(ph, g, 3)
                        if u % 2 == 0 and ph.gate != "none":
                            func = ACT.Silu if ph.gate == "silu" else ACT.Sigmoid
                            act.wait_ge(gate_scaled, f + (ph.pair0 + 1))
                            if not first:
                                act.wait_ge(gate_ready, f + (ph.pair0 - 1))
                            act.activation(acted[:, par, :], gate[:, par, :], func).then_inc(gate_acted, 1)
                        if u % 2 == 1 and ph.gate == "silu":
                            act.wait_ge(pair_out, f + (ph.pair0 + 1))
                            act.activation(h_hi[:, bass.ds(f, 1), :], hid[:, :], ACT.Copy).then_inc(hhi_ready, 1)

                run_groups(ph, group)

            def run_groups(ph, group):
                peeled = 2 if ph is LAST else 1
                for g in range(min(peeled, ph.groups)):
                    group(g)
                if ph.groups - 1 > peeled:
                    with act.Fori(peeled, ph.groups - 1) as g:
                        group(g)
                if ph.groups > peeled:
                    group(ph.groups - 1)

            def resid(ph):
                per_tile = 2 if ph.row_tiles == HALF else 1

                def group(g):
                    for u in range(4):
                        split_hi(ph, g, u + 2)
                        if u % per_tile == per_tile - 1 and ph.next_norm is not None:
                            j = g * (4 // per_tile) + u // per_tile
                            new_x(j, (u // per_tile) % 2, ph.next_norm)
                        if ph is LAST and u % 2 == 1:
                            send(g * 2 + u // 2 - 1, 1 - u // 2)

                run_groups(ph, group)
                if ph is LAST:
                    send(KD - 1, 1)
                    for i in range(2):
                        act.wait_ge(out_sent[i], 16 * (KD // 2))

            def send(j, par):
                if isinstance(j, int):
                    if j < 0:
                        return
                    if j >= 2:
                        act.wait_ge(out_sent[par], 16 * (j // 2))
                else:
                    act.wait_ge(out_sent[par], (j - par) * 8)
                act.wait_ge(out_turned, j + 1)
                act.activation(out_rows[:, par, :, :], bank[6 + par][:, :].rearrange("p (t c) -> p t c", t=TB),
                               ACT.Copy).then_inc(out_staged, 1)
                act.wait_ge(out_staged, j + 1)
                act.dma_start(out[0].rearrange("(t p) d -> p t d", p=P)[:, :, bass.ds(j * P, P)],
                              out_rows[:, par, :, :]).then_inc(out_sent[par], 16)

            act_taps = [0]

            def conv_taps(n):
                for _ in range(n):
                    shift = act_taps[0]
                    if shift == TAPS:
                        return
                    k, b = TAPS - 1 - shift, CB - 1
                    wk = conv_w[:, k * CB + b:k * CB + b + 1]
                    if shift == 0:
                        act.wait_ge(pair_out, A_GATE.pair0 + CB)
                        act.activation(conv[:, b, :], a_in[:, b, :], ACT.Identity, scale=wk,
                                       bias=vec[:, V_CB + b:V_CB + b + 1]).then_inc(tap_made, 1)
                    else:
                        if shift >= 3:
                            act.wait_ge(tap_added, shift - 2)
                        act.activation(tap_prod[:, shift % 2, 0:S - shift], a_in[:, b, 0:S - shift], ACT.Copy,
                                       scale=wk).then_inc(tap_made, 1)
                    act_taps[0] += 1

            def qk_high(n):
                t = HEAD_ORDER[n]
                dst = q_hi if t < AB else k_hi
                act.wait_ge(qk_scaled, n + 1)
                act.activation(dst[:, t % AB, :], qk_nrm[:, n % 2, :], ACT.Copy,
                               scale=qk_gain[:, t // AB:t // AB + 1]).then_inc(qkhi_ready, 1)

            def norm_squares(b, n):
                if n >= 2:
                    act.wait_ge(a_added, 1)
                act.activation(sq[:, n % 2, :], conv[:, b, :], ACT.Square).then_inc(a_sq, 1)

            def conv_norm():
                norm_root(am_ready, 1, a_mean[:, :], a_root[:, :], ar_ready)
                for b in range(CB):
                    act.wait_ge(a_scaled, b + 1)
                    act.activation(a_act[b][:, :], a_nrm[:, b % 2, :], ACT.Silu,
                                   scale=vec[:, V_CN + b:V_CN + b + 1]).then_inc(a_acted, 1)
                    act.wait_ge(a_acted, b + 1)
                    act.activation(cat_hi[:, b, :], a_act[b][:, :], ACT.Copy).then_inc(ahi_ready, 1)

            def attention():
                for t in range(STEPS):
                    if t < HEADS * TB:
                        n = (t % TB + 1) * P
                        act.wait_ge(max_ready, t + 1)
                        if t >= NPR:
                            act.wait_ge(probs_turned, t - NPR + 1)
                        act.activation(probs[:, t % NPR, 0:n], bank[t % 3][:, 0:n], ACT.Exp,
                                       bias=neg_max[:, t:t + 1], accum_out=row_sum[:, t:t + 1]).then_inc(exp_done, 1)
                    if 0 <= t - TURN_LAG < HEADS * TB:
                        tt = t - TURN_LAG
                        h, qb = tt // TB, tt % TB
                        act.wait_ge(probs_turned, tt + 1)
                        if h >= 2:
                            act.wait_ge(pv_done, h - 1)
                        act.activation(pt_hi[h % 2][:, 0:qb + 1, qb * P:(qb + 1) * P],
                                       bank[4 + tt % 2][:, 0:(qb + 1) * P].rearrange("p (k q) -> p k q", q=P),
                                       ACT.Copy).then_inc(pthi_ready, 1)
                    if t >= TB - 1 + OUT_LAG and (t - (TB - 1) - OUT_LAG) % TB == 0:
                        h = (t - (TB - 1) - OUT_LAG) // TB
                        p0 = (h % 2) * HD
                        act.wait_ge(pv_done, h + 1)
                        act.activation(cat_hi[p0:p0 + HD, CB + h // 2, :], bank[6 + h % 2][p0:p0 + HD, :], ACT.Copy)\
                            .then_inc(ohi_ready, 1)
                    if t == 0:
                        act.wait_ge(conv_done, 2)
                        norm_squares(0, 0)
                        norm_squares(1, 1)
                        act.wait_ge(tap_added, TAPS - 1)
                        norm_squares(CB - 1, 2)
                    if t == len(TAPS_T):
                        act.wait_ge(conv_done, DVE_TILES)
                        norm_squares(2, 3)
                    if t == A_STEP:
                        conv_norm()

            act.wait_ge(consts_ready, 3)
            act.activation(ident_r[:, :], ident[:, :], ACT.Copy).then_inc(identr_ready, 1)
            act.wait_ge(first_ready, 1)
            new_x(0, 0, 0)
            split_hi(phases[0], 0, 0)
            new_x(1, 1, 0)
            with act.Fori(1, KD // 2) as g:
                for half in range(2):
                    new_x(g * 2 + half, half, 0)
            split_hi(phases[0], 0, 1)
            for ph in phases:
                if ph.kind == "pair":
                    pair(ph)
                elif ph.kind == "resid":
                    resid(ph)
                elif ph.kind == "single":
                    for i in range(ph.units):
                        split_hi(ph, i // 4, i % 4 + 2)
                        act.wait_ge(y_out, i + 1)
                        act.activation(y_hi[:, i, :], hid[:, :], ACT.Copy).then_inc(yhi_ready, 1)
                elif ph.kind == "qk":
                    for i in range(ph.units):
                        split_hi(ph, i // 4, i % 4 + 2)
                        act.wait_ge(qk_out, i + 1)
                        if i >= 2:
                            act.wait_ge(qk_sum, i - 1)
                        act.activation(sq[:, i % 2, :], qk_raw[:, i, :], ACT.Square).then_inc(qk_sq, 1)
                        if i == 3:
                            act.wait_ge(lf_in, 1)
                            act.activation(lf[1][:, :], lf[0][:, :], ACT.Abs).then_inc(lf_abs, 1)
                            act.wait_ge(lf_abs, 1)
                            act.activation(lf[2][:, :], lf[1][:, :], ACT.Exp, scale=-1.0).then_inc(lf_exp, 1)
                            act.wait_ge(lf_exp, 1)
                            act.activation(lf[3][:, :], lf[2][:, :], ACT.Ln, bias=1.0).then_inc(lf_log, 1)
                        conv_taps(ACT_TAPS[i])
                elif ph.kind == "v":
                    act.wait_ge(vec_ready, 2)
                    act.activation(qk_gain[:, 0:1], vec[:, V_Q:V_Q + 1], ACT.Copy, scale=1.0 / math.sqrt(HD))\
                        .then_inc(qgain_ready, 1)
                    act.activation(qk_gain[:, 1:2], vec[:, V_Q + 1:V_Q + 2], ACT.Copy).then_inc(qgain_ready, 1)
                    act.wait_ge(qgain_ready, 2)
                    split_hi(ph, 0, 2)
                    norm_root(qk_mean, 1, mean_sq[0:2 * HEADS, :], root[0:2 * HEADS, :], qk_root)
                    split_hi(ph, 0, 3)
                    split_hi(ph, 0, 4)
                    act.wait_ge(cum_ready, 1)
                    act.wait_ge(cum_cleared, 2)
                    for r in range(0, CP, HD):
                        act.activation(cum_r[r:r + HEADS, :], cum[:, :], ACT.Copy).then_inc(cumhi_ready, 1)
                        act.activation(ncum_r[r:r + HEADS, :], cum[:, :], ACT.Copy, scale=-1.0)\
                            .then_inc(cumhi_ready, 1)
                    for n in range(QK // 2):
                        qk_high(n)
                    split_hi(ph, 0, 5)
                    act.wait_ge(unit_done, ph.unit0 + ph.units)
                    act.wait_ge(col_ready, 1)
                    for tb in range(TB):
                        act.activation(v_hi[:, tb, :], bank[tb][:, :], ACT.Copy, scale=rstd_col[:, tb:tb + 1])\
                            .then_inc(vhi_ready, 1)
                    for n in range(QK // 2, QK):
                        qk_high(n)
                    attention()

        @block.vector
        def _(dve):
            links = [0]

            def link(instruction):
                links[0] += 1
                instruction.then_inc(step, 1)
                dve.wait_ge(step, links[0])

            def run_groups(ph, group):
                group(0)
                if ph.groups > 2:
                    with dve.Fori(1, ph.groups - 1) as g:
                        group(g)
                if ph.groups > 1:
                    group(ph.groups - 1)

            def split_lo(ph, g, u):
                if u >= 4 and isinstance(g, int) and g == ph.groups - 1:
                    ph, g, u = ph.next, 0, u - 4
                    if ph is None:
                        return
                n = ph.row_tiles * P
                dve.wait_ge(whi_ready, g * 4 + (ph.unit0 + u + 1))
                dve.tensor_tensor(w_lo[:, u % 2, 0:n], raw[:, u % 4, 0:n], raws(w_hi[:, u % 2, 0:n]), ALU.subtract)\
                    .then_inc(wlo_ready, 1)

            def xg_low(j, norm):
                dve.wait_ge(xhi_ready, j + (KD * norm + 1))
                one = bass.ds(j, 1)
                dve.scalar_tensor_tensor(xg_lo[:, one, :], x[:, one, :], vec[:, bass.ds(j + GAIN_COL[norm], 1)],
                                         raws(xg_hi[:, one, :]), ALU.mult, ALU.subtract).then_inc(xlo_ready, 1)

            def invert(mean, rough_, corr_, out_, size):
                link(dve.tensor_tensor(corr_, rough_, rough_, ALU.mult))
                link(dve.scalar_tensor_tensor(corr_, corr_, -0.5, mean, ALU.mult, ALU.mult))
                return dve.scalar_tensor_tensor(out_, corr_, 1.5, rough_, ALU.add, ALU.mult)

            taps = [0]

            def conv_taps(n):
                for _ in range(n):
                    if taps[0] == TAPS * DVE_TILES:
                        return
                    b, k = taps[0] // TAPS, TAPS - 1 - taps[0] % TAPS
                    wk = conv_w[:, k * CB + b:k * CB + b + 1]
                    shift = TAPS - 1 - k
                    if shift == 0:
                        dve.wait_ge(pair_out, A_GATE.pair0 + b + 1)
                        op = dve.tensor_scalar(conv[:, b, :], a_in[:, b, :], wk, vec[:, V_CB + b:V_CB + b + 1],
                                               ALU.mult, ALU.add)
                    else:
                        op = dve.scalar_tensor_tensor(conv[:, b, shift:S], a_in[:, b, 0:S - shift], wk,
                                                      conv[:, b, shift:S], ALU.mult, ALU.add)
                    if k == 0:
                        op.then_inc(conv_done, 1)
                    else:
                        link(op)
                    taps[0] += 1

            def pair(ph):
                def group(g):
                    first = isinstance(g, int) and g == 0
                    for u in range(4):
                        f, half = g * 2 + u // 2, u // 2
                        if not (first and u in (1, 2)):
                            split_lo(ph, g, u + 2)
                        if first and u == 1:
                            split_lo(ph, g, 4)
                        if first and u == 3 and ph is phases[0]:
                            dve.wait_ge(vec_turned, 2)
                            dve.tensor_copy(vec[:, FIRST:NVEC], bank[7][:, 0:NVEC - FIRST]).then_inc(vec_ready, 1)
                            dve.tensor_copy(conv_w[:, :], bank[7][:, P:P + TAPS * CB]).then_inc(vec_ready, 1)
                        if first and u == 0:
                            dve.wait_ge(ssq_done, ph.norm + 1)
                            dve.tensor_scalar(mean_sq[:, :], bank[6][:, :], 1.0 / D, EPS, ALU.mult, ALU.add)\
                                .then_inc(mean_ready, 1)
                            dve.wait_ge(root_ready, ph.norm + 1)
                            link(dve.reciprocal(rough[:, :], root[:, :]))
                            split_lo(ph, g, 3)
                            invert(mean_sq[:, :], rough[:, :], corr[:, :], rstd[:, :], D).then_inc(rstd_ready, 1)
                            dve.wait_ge(rstd_ready, ph.norm + 1)
                        dve.wait_ge(unit_done, g * 4 + (ph.unit0 + u + 1))
                        if u % 2 == 0:
                            dve.tensor_tensor(gate[:, half, :], bank[u][:, :], rstd[:, :], ALU.mult)\
                                .then_inc(gate_scaled, 1)
                            continue
                        dve.wait_ge(gate_ready, f + (ph.pair0 + 1))
                        if ph.gate == "silu":
                            dve.tensor_tensor(hid[:, :], bank[u][:, :], scaled[:, :], ALU.mult).then_inc(pair_out, 1)
                            dve.wait_ge(hhi_ready, f + (ph.h0 + 1))
                            one = bass.ds(f, 1)
                            dve.tensor_tensor(h_lo[:, one, :], hid[:, :].unsqueeze(1), raws(h_hi[:, one, :]),
                                              ALU.subtract).then_inc(hlo_ready, 1)
                        elif ph.gate == "sigmoid":
                            dve.tensor_tensor(a_in[:, f, :], bank[u][:, :], scaled[:, :], ALU.mult)\
                                .then_inc(pair_out, 1)
                            conv_taps(TAPS_A[f])
                        else:
                            c1, o1 = c_in[:, bass.ds(f, 1), :], c_out[:, bass.ds(f, 1), :]
                            dve.tensor_tensor(c1, bank[u][:, :].unsqueeze(1), scaled[:, :].unsqueeze(1), ALU.mult)\
                                .then_inc(pair_out, 1)
                            dve.wait_ge(pair_out, f + (ph.pair0 + 1))
                            for s in range(TAPS_C):
                                wk = vec[:, bass.ds(f + (V_OD + (TAPS_C - 1 - s) * KD), 1)]
                                if s == 0:
                                    op = dve.tensor_scalar(o1, c1, wk, None, ALU.mult)
                                else:
                                    o_, c_ = c_out[:, bass.ds(f, 1), s:S], c_in[:, bass.ds(f, 1), 0:S - s]
                                    op = dve.scalar_tensor_tensor(o_, c_, wk, o_, ALU.mult, ALU.add)
                                if s < TAPS_C - 1:
                                    op.then_inc(conv3_step, 1)
                                    dve.wait_ge(conv3_step, f * (TAPS_C - 1) + (s + 1))
                                else:
                                    op.then_inc(conv3_done, 1)

                run_groups(ph, group)

            def resid(ph):
                per_tile = 2 if ph.row_tiles == HALF else 1

                def group(g):
                    for u in range(4):
                        if u % per_tile == per_tile - 1:
                            j, half = g * (4 // per_tile) + u // per_tile, (u // per_tile) % 2
                            one = bass.ds(j, 1)
                            dve.wait_ge(unit_done, g * 4 + (ph.unit0 + u + 1))
                            ps = bank[4 + half][:, :].unsqueeze(1)
                            if ph is LAST:
                                if not isinstance(j, int) or j >= 2:
                                    dve.wait_ge(out_turned, j - 1)
                                dve.scalar_tensor_tensor(fin[:, half:half + 1, :], ps, ph.factor, x[:, one, :],
                                                         ALU.mult, ALU.add).then_inc(x_new, 1)
                            else:
                                dve.scalar_tensor_tensor(x[:, one, :], ps, ph.factor, x[:, one, :],
                                                         ALU.mult, ALU.add).then_inc(x_new, 1)
                        split_lo(ph, g, u + 2)
                        if u % per_tile == per_tile - 1 and ph is not LAST:
                            xg_low(j, ph.next_norm)

                run_groups(ph, group)

            def qk_low(n):
                t = HEAD_ORDER[n]
                lo, hi = (q_lo, q_hi) if t < AB else (k_lo, k_hi)
                dve.wait_ge(qk_fanned, n + 1)
                dve.tensor_tensor(qk_nrm[:, n % 2, :], qk_raw[:, t, :], bank[4 + n % 2][:, :], ALU.mult)\
                    .then_inc(qk_scaled, 1)
                dve.wait_ge(qkhi_ready, n + 1)
                dve.scalar_tensor_tensor(lo[:, t % AB, :], qk_nrm[:, n % 2, :], qk_gain[:, t // AB:t // AB + 1],
                                         raws(hi[:, t % AB, :]), ALU.mult, ALU.subtract).then_inc(qklo_ready, 1)

            def conv_norm():
                dve.wait_ge(a_sum, 1)
                dve.tensor_scalar(a_mean[:, :], bank[3][:, :], 1.0 / CONV, EPS, ALU.mult, ALU.add).then_inc(am_ready, 1)
                dve.wait_ge(ar_ready, 1)
                link(dve.reciprocal(a_rough[:, :], a_root[:, :]))
                link(invert(a_mean[:, :], a_rough[:, :], a_corr[:, :], rstd[:, :], CONV))
                for b in range(CB):
                    if b >= 2:
                        dve.wait_ge(a_acted, b - 1)
                    dve.tensor_tensor(a_nrm[:, b % 2, :], conv[:, b, :], rstd[:, :], ALU.mult).then_inc(a_scaled, 1)

            def attention(ph):
                split_lo(ph, 0, 2)
                heads = slice(0, 2 * HEADS)
                dve.wait_ge(qk_sum, QK)
                dve.wait_ge(cum_ready, 1)
                dve.tensor_scalar(mean_sq[heads, :], bank[6][heads, :], 1.0 / HD, EPS, ALU.mult, ALU.add)\
                    .then_inc(qk_mean, 1)
                dve.wait_ge(qk_root, 1)
                link(dve.reciprocal(rough[heads, :], root[heads, :]))
                split_lo(ph, 0, 3)
                invert(mean_sq[heads, :], rough[heads, :], corr[heads, :], rstd[heads, :], HD).then_inc(qk_rstd, 1)
                split_lo(ph, 0, 4)
                dve.wait_ge(cumhi_ready, 2 * (CP // HD))
                for r in range(32, CP, HD):
                    dve.tensor_tensor(cum_r[r:r + HEADS, :], cum[:, :], raws(cum_r[0:HEADS, :]), ALU.subtract)\
                        .then_inc(cumlo_ready, 1)
                    dve.tensor_tensor(ncum_r[r:r + HEADS, :], raws(cum_r[0:HEADS, :]), cum[:, :], ALU.subtract)\
                        .then_inc(cumlo_ready, 1)
                for n in range(QK // 2):
                    qk_low(n)
                split_lo(ph, 0, 5)
                for tb in range(TB):
                    dve.wait_ge(vhi_ready, tb + 1)
                    dve.scalar_tensor_tensor(v_lo[:, tb, :], bank[tb][:, :], rstd_col[:, tb:tb + 1],
                                             raws(v_hi[:, tb, :]), ALU.mult, ALU.subtract).then_inc(vlo_ready, 1)
                for n in range(QK // 2, QK):
                    qk_low(n)
                for t in range(STEPS):
                    if t < HEADS * TB:
                        n = (t % TB + 1) * P
                        dve.wait_ge(scores_done, t + 1)
                        dve.tensor_reduce(neg_max[:, t:t + 1], bank[t % 3][:, 0:n], AX.X, ALU.max, negate=True)\
                            .then_inc(max_ready, 1)
                    if 0 <= t - SCALE_LAG < HEADS * TB:
                        tt = t - SCALE_LAG
                        n = (tt % TB + 1) * P
                        dve.wait_ge(exp_done, tt + 1)
                        link(dve.reciprocal(row_inv[:, tt:tt + 1], row_sum[:, tt:tt + 1]))
                        dve.tensor_scalar(probs[:, tt % NPR, 0:n], probs[:, tt % NPR, 0:n], row_inv[:, tt:tt + 1], None,
                                          ALU.mult).then_inc(probs_ready, 1)
                    if 0 <= t - TURN_LAG < HEADS * TB:
                        tt = t - TURN_LAG
                        h, qb = tt // TB, tt % TB
                        dve.wait_ge(pthi_ready, tt + 1)
                        dst = (slice(None), slice(0, qb + 1), slice(qb * P, (qb + 1) * P))
                        dve.tensor_tensor(pt_lo[h % 2][dst],
                                          bank[4 + tt % 2][:, 0:(qb + 1) * P].rearrange("p (k q) -> p k q", q=P),
                                          raws(pt_hi[h % 2][dst]), ALU.subtract).then_inc(ptlo_ready, 1)
                    if t >= TB - 1 + OUT_LAG and (t - (TB - 1) - OUT_LAG) % TB == 0:
                        h = (t - (TB - 1) - OUT_LAG) // TB
                        p0 = (h % 2) * HD
                        dve.wait_ge(ohi_ready, h + 1)
                        dve.tensor_tensor(cat_lo[p0:p0 + HD, CB + h // 2, :], bank[6 + h % 2][p0:p0 + HD, :],
                                          raws(cat_hi[p0:p0 + HD, CB + h // 2, :]), ALU.subtract).then_inc(olo_ready, 1)
                    conv_taps(TAPS_T[t] if t < len(TAPS_T) else 0)
                    if t == A_STEP:
                        conv_norm()
                    if t == HEADS * TB - 1 + TURN_LAG:
                        dve.wait_ge(probs_turned, HEADS * TB)
                        dve.wait_ge(ahi_ready, CB)
                        for b in range(CB):
                            dve.tensor_tensor(cat_lo[:, b, :], a_act[b][:, :], raws(cat_hi[:, b, :]), ALU.subtract)\
                                .then_inc(alo_ready, 1)

            dve.wait_ge(first_turned, 1)
            dve.tensor_copy(vec[:, 0:FIRST], bank[7][:, 0:FIRST]).then_inc(first_ready, 1)
            for j in range(KD + 1):
                if j < KD:
                    dve.wait_ge(x_turned, j + 1)
                    dve.tensor_copy(x[:, j, :], bank[4 + j % 2][:, :]).then_inc(x_new, 1)
                if j == 2:
                    split_lo(phases[0], 0, 0)
                if j:
                    if j == 1:
                        dve.wait_ge(first_ready, 1)
                    xg_low(j - 1, 0)
            split_lo(phases[0], 0, 1)

            for ph in phases:
                if ph.kind == "pair":
                    pair(ph)
                elif ph.kind == "resid":
                    resid(ph)
                elif ph.kind == "single":
                    for i in range(ph.units):
                        split_lo(ph, i // 4, i % 4 + 2)
                        dve.wait_ge(unit_done, ph.unit0 + i + 1)
                        dve.wait_ge(y_gated, i + 1)
                        if i:
                            dve.wait_ge(ylo_ready, i)
                        dve.tensor_tensor(hid[:, :], bank[i % 4][:, :], c_out[:, i, :], ALU.mult).then_inc(y_out, 1)
                        dve.wait_ge(yhi_ready, i + 1)
                        dve.tensor_tensor(y_lo[:, i, :], hid[:, :], raws(y_hi[:, i, :]), ALU.subtract)\
                            .then_inc(ylo_ready, 1)
                elif ph.kind == "qk":
                    dve.wait_ge(wfhi_ready, 1)
                    dve.tensor_tensor(wf_lo[:, :, 0:HEADS], wf_raw[:, :, :], raws(wf_hi[:, :, 0:HEADS]), ALU.subtract)\
                        .then_inc(wflo_ready, 1)
                    dve.wait_ge(col_done, 1)
                    dve.tensor_copy(rstd_col[:, :].unsqueeze(2),
                                    bank[4][:, :].rearrange("p (t c) -> p t c", t=TB)[:, :, 0:1]).then_inc(col_ready, 1)
                    for i in range(ph.units):
                        split_lo(ph, i // 4, i % 4 + 2)
                        if i == 3:
                            dve.wait_ge(f_done, 1)
                            link(dve.tensor_tensor(lf[4][:, :], bank[7][0:HEADS, :], rstd[0:HEADS, :], ALU.mult))
                            dve.tensor_scalar(lf[0][:, :], lf[4][:, :], b_f[:, 0:1], None, ALU.add).then_inc(lf_in, 1)
                        if i == 4:
                            dve.wait_ge(lf_in, 1)
                            link(dve.tensor_scalar(lf[4][:, :], lf[0][:, :], 0.0, None, ALU.min))
                            dve.wait_ge(lf_log, 1)
                            link(dve.tensor_tensor(lf[1][:, :], lf[4][:, :], lf[3][:, :], ALU.subtract))
                            link(dve.memset(lf[2][:, :], 1.0))
                            dve.tensor_tensor_scan(cum[:, :], lf[2][:, :], lf[1][:, :], 0.0, ALU.mult, ALU.add)\
                                .then_inc(cum_ready, 1)
                        dve.wait_ge(unit_done, ph.unit0 + i + 1)
                        dve.tensor_tensor(qk_raw[:, i, :], bank[i % 4][:, :], rstd[:, :], ALU.mult).then_inc(qk_out, 1)
                        conv_taps(TAPS_QK[i])
                elif ph.kind == "v":
                    attention(ph)

        @block.tensor
        def _(pe):
            def product(dst, a, b, start, stop):
                pe.matmul(dst, a[0], b[0], start=start, stop=False)
                pe.matmul(dst, a[0], b[1], start=False, stop=False)
                return pe.matmul(dst, a[1], b[0], start=False, stop=stop)

            def weights(ph, u):
                return [unit_view(ph, t, u % 2) for t in (w_hi, w_lo)]

            def run_groups(ph, group):
                peeled = 2 if ph is LAST else 1
                for g in range(min(peeled, ph.groups)):
                    group(g)
                if ph.groups > peeled:
                    with pe.Fori(peeled, ph.groups) as g:
                        group(g)

            def projection(ph, g, u, wait_x=False, before=None):
                if before is None:
                    pe.wait_ge(wlo_ready, g * 4 + (ph.unit0 + u + 1))
                wh, wl = weights(ph, u)
                for k in range(KD):
                    if before:
                        before(k)
                    if wait_x:
                        pe.wait_ge(xlo_ready, KD * ph.norm + k + 1)
                    last = product(bank[u][:, :], (wh[:, k, :], wl[:, k, :]), (xg_hi[:, k, :], xg_lo[:, k, :]),
                                   k == 0, k == KD - 1)
                last.then_inc(unit_done, 1)

            def pair(ph):
                def group(g):
                    first = isinstance(g, int) and g == 0
                    for u in range(4):
                        if not first:
                            pe.wait_ge((gate_scaled, pair_out)[u % 2], g * 2 + (ph.pair0 + u // 2 - 1))
                        projection(ph, g, u, wait_x=first and u == 0,
                                   before=turn_in if first and u == 0 and ph is phases[0] else None)
                        if first and u == 1 and ph is phases[0]:
                            pe.wait_ge(first_ready, 1)
                            pe.wait_ge(vec_arrived, 16 * 9)
                            pe.transpose(bank[7][:, 0:NVEC - FIRST], vec_rows[:, :],
                                         ident[0:NVEC - FIRST, 0:NVEC - FIRST]).then_inc(vec_turned, 1)
                            pe.wait_ge(conv_arrived, 16)
                            pe.transpose(bank[7][:, P:P + TAPS * CB], conv_rows[:, :],
                                         ident[0:TAPS * CB, 0:TAPS * CB]).then_inc(vec_turned, 1)
                        if first and u == 0:
                            pe.wait_ge(sq_added, KD * (ph.norm + 1))
                            pe.matmul(bank[6][:, :], ones[:, :], sq_sum[:, :], start=True, stop=True)\
                                .then_inc(ssq_done, 1)

                run_groups(ph, group)

            def turn_x(j):
                if j >= 2:
                    pe.wait_ge(x_new, j - 1)
                if j % (KD // len(x_arrived)) == 0:
                    pe.wait_ge(x_arrived[j // (KD // len(x_arrived))], 16)
                for tb in range(TB):
                    last = pe.transpose(bank[4 + j % 2][:, tb * P:(tb + 1) * P], x_rows[:, tb, j * P:(j + 1) * P],
                                        ident[:, :])
                last.then_inc(x_turned, 1)

            def turn_in(k):
                for j in ((0, 1, 2) if k == 0 else (k + 2,)):
                    if j < KD:
                        turn_x(j)
                if k == 0:
                    pe.wait_ge(wlo_ready, 1)

            def resid(ph):
                per_tile = 2 if ph.row_tiles == HALF else 1
                hi, lo = SRC[ph.source]
                x0 = KD * ph.next_norm if ph is not LAST else X_LAST

                def group(g):
                    first = isinstance(g, int) and g == 0
                    for u in range(4):
                        pe.wait_ge(wlo_ready, g * 4 + (ph.unit0 + u + 1))
                        wh, wl = weights(ph, u)
                        j, half, part = g * (4 // per_tile) + u // per_tile, (u // per_tile) % 2, u % per_tile
                        if part == 0 and (not isinstance(j, int) or j >= 2):
                            pe.wait_ge(x_new, j + (x0 - 1))
                        order = list(range(ph.row_tiles))
                        if ph.source == "cat":
                            order = order[CB:] + order[:CB]
                        for n, k in enumerate(order):
                            kk = part * ph.row_tiles + k
                            if first and j == 0:
                                if ph.source == "h":
                                    pe.wait_ge(hlo_ready, phases[phases.index(ph) - 1].h0 + kk + 1)
                                elif ph.source == "y":
                                    pe.wait_ge(ylo_ready, kk + 1)
                                elif k >= CB:
                                    pe.wait_ge(olo_ready, 2 * (k - CB) + 2)
                                else:
                                    pe.wait_ge(alo_ready, k + 1)
                            last = product(bank[4 + half][:, :], (wh[:, k, :], wl[:, k, :]), (hi[:, kk, :], lo[:, kk, :]),
                                           part == 0 and n == 0, part == per_tile - 1 and n == len(order) - 1)
                        last.then_inc(unit_done, 1)
                        if ph is LAST and part == 1:
                            if half == 1 or not first:
                                turn_out(j - 1, 1 - half)

                run_groups(ph, group)
                if ph is LAST:
                    turn_out(KD - 1, 1)

            X_LAST = KD * 6

            def turn_out(j, half):
                pe.wait_ge(x_new, j + (X_LAST + 1))
                if not isinstance(j, int) or j >= 2:
                    pe.wait_ge(out_staged, j - 1)
                for tb in range(TB):
                    last = pe.transpose(bank[6 + half][:, tb * P:(tb + 1) * P], fin[:, half, tb * P:(tb + 1) * P],
                                        ident[:, :])
                last.then_inc(out_turned, 1)

            def attention():
                def scores(t):
                    h, qb = t // TB, t % TB
                    n, p0, j = (qb + 1) * P, (h % 2) * HD, h // 2
                    dst, qs = bank[t % 3], slice(qb * P, (qb + 1) * P)
                    rows = slice(p0, p0 + HD)
                    if t >= 3:
                        pe.wait_ge(exp_done, t - 2)
                    if t % (2 * TB) == 0:
                        pe.wait_ge(qklo_ready, 2 * (h // 2 + 1))
                    product(dst[:, 0:n], (q_hi[rows, j, qs], q_lo[rows, j, qs]),
                            (k_hi[rows, j, 0:n], k_lo[rows, j, 0:n]), True, False)
                    pe.matmul(dst[:, 0:n], row_sel[rows, h, :], ncum_r[rows, 0:n], start=False, stop=False)
                    for kb in range(qb + 1):
                        pe.matmul(dst[:, kb * P:(kb + 1) * P], cum_r[rows, qs], row_sel[rows, h, :], start=False, stop=False)
                    pe.matmul(dst[:, qs], ident_r[:, :], mask_r[:, :], start=False, stop=True).then_inc(scores_done, 1)

                for t in range(STEPS):
                    if t < HEADS * TB:
                        scores(t)
                    if t == A_STEP:
                        pe.wait_ge(a_added, CB - 1)
                        pe.matmul(bank[3][:, :], ones[:, :], sq_sum[:, :], start=True, stop=True).then_inc(a_sum, 1)
                    if 0 <= t - TURN_LAG < HEADS * TB:
                        tt = t - TURN_LAG
                        pe.wait_ge(probs_ready, tt + 1)
                        if tt >= 2:
                            pe.wait_ge(ptlo_ready, tt - 1)
                        for kb in range(tt % TB + 1):
                            last = pe.transpose(bank[4 + tt % 2][:, kb * P:(kb + 1) * P],
                                                probs[:, tt % NPR, kb * P:(kb + 1) * P], ident[:, :])
                        last.then_inc(probs_turned, 1)
                    if t >= TB - 1 + PV_LAG and (t - (TB - 1) - PV_LAG) % TB == 0 and t < HEADS * TB + PV_LAG:
                        h = (t - (TB - 1) - PV_LAG) // TB
                        pe.wait_ge(ptlo_ready, TB * (h + 1))
                        if h >= 2:
                            pe.wait_ge(olo_ready, h - 1)
                        cols = slice((h // 2) * P, (h // 2 + 1) * P)
                        for kb in range(TB):
                            last = product(bank[6 + h % 2][:, kb * P:S], (v_hi[:, kb, cols], v_lo[:, kb, cols]),
                                           (pt_hi[h % 2][:, kb, kb * P:S], pt_lo[h % 2][:, kb, kb * P:S]),
                                           kb == 0, kb == TB - 1)
                        last.then_inc(pv_done, 1)

            def fan(n):
                if n >= 2:
                    pe.wait_ge(qk_scaled, n - 1)
                pe.matmul(bank[4 + n % 2][:, :], head_fan[:, HEAD_ORDER[n], :], rstd[0:2 * HEADS, :],
                          start=True, stop=True).then_inc(qk_fanned, 1)

            def head_sum(t):
                pe.wait_ge(qk_sq, t + 1)
                pe.matmul(bank[6][0:2 * HEADS, :], head_sel[:, t, :], sq[:, t % 2, :], start=t == 0, stop=t == QK - 1)\
                    .then_inc(qk_sum, 1)

            pe.wait_ge(consts_ready, 3)
            pe.wait_ge(first_arrived, 16)
            pe.transpose(bank[7][:, 0:FIRST], first_rows[:, :], ident[0:FIRST, 0:FIRST]).then_inc(first_turned, 1)

            for ph in phases:
                if ph.kind == "pair":
                    pair(ph)
                elif ph.kind == "resid":
                    resid(ph)
                elif ph.kind == "single":
                    for i in range(ph.units):
                        if i >= 4:
                            pe.wait_ge(y_out, i - 3)
                        else:
                            p_end = ph.pair_end
                            pe.wait_ge((gate_scaled, pair_out)[i % 2], p_end - 1 + i // 2)
                        projection(ph, i // 4, i % 4)
                elif ph.kind == "qk":
                    pe.wait_ge(rstd_ready, 2)
                    for tb in range(TB):
                        last = pe.transpose(bank[4][:, tb * P:(tb + 1) * P], rstd[:, tb * P:(tb + 1) * P], ident[:, :])
                    last.then_inc(col_done, 1)
                    pe.wait_ge(sel_ready, 2 + 2 * QK)
                    pe.wait_ge(identr_ready, 1)
                    for i in range(ph.units):
                        if i >= 4:
                            pe.wait_ge(qk_out, i - 3)
                        else:
                            pe.wait_ge((gate_scaled, pair_out)[i % 2], A_GATE.pair0 + CB - 1 + i // 2)
                        projection(ph, i // 4, i % 4)
                        if i:
                            head_sum(i - 1)
                        if i == 2:
                            pe.wait_ge(wflo_ready, 1)
                            for k in range(KD):
                                last = product(bank[7][:, :], (wf_hi[:, k, :], wf_lo[:, k, :]),
                                               (xg_hi[:, k, :], xg_lo[:, k, :]), k == 0, k == KD - 1)
                            last.then_inc(f_done, 1)
                elif ph.kind == "v":
                    for u in range(ph.units):
                        pe.wait_ge(wlo_ready, ph.unit0 + u + 1)
                        wh, wl = weights(ph, u)
                        for tb in range(TB):
                            if u == 0:
                                pe.wait_ge(qk_out, QK - TB + tb + 1)
                            ts = slice(tb * P, (tb + 1) * P)
                            for k in range(2):
                                kk = 2 * u + k
                                last = product(bank[tb][:, :], (xg_hi[:, kk, ts], xg_lo[:, kk, ts]),
                                               (wh[:, k, :], wl[:, k, :]), kk == 0, kk == KD - 1)
                        last.then_inc(unit_done, 1)
                        if u == 0:
                            head_sum(QK - 1)
                        if u == 2:
                            pe.wait_ge(fan_ready, 2)
                            pe.wait_ge(col_ready, 1)
                            pe.wait_ge(qk_rstd, 1)
                            fan(0)
                            fan(1)
                    for n in range(2, QK):
                        fan(n)
                    pe.wait_ge(cumlo_ready, 2 * (CP // HD))
                    pe.wait_ge(rsel_ready, 1)
                    pe.wait_ge(vlo_ready, TB)
                    attention()


_INS = ["x", "ffn1_norm", "ffn1_w_gate", "ffn1_w_up", "ffn1_w_down", "mix_norm", "ffn2_norm", "ffn2_w_gate",
        "ffn2_w_up", "ffn2_w_down", "ev_w_in", "ev_b_f", "ev_conv_w", "ev_conv_b", "ev_conv_norm", "ev_q_norm",
        "ev_k_norm", "ev_w_out", "od_w_in", "od_conv_w", "od_w_out"]


def kernel(**inputs):
    import numpy as np
    from concourse import bacc
    from concourse.bass_utils import run_bass_kernel_spmd

    nc = bacc.Bacc("TRN2", target_bir_lowering=False, num_devices=1)
    arrays, t_in = {}, {}
    for name in _INS:
        a = np.ascontiguousarray(inputs[name])
        arrays[f"in_{name}"] = a
        t_in[name] = nc.dram_tensor(f"in_{name}", a.shape, mybir.dt.from_np(a.dtype), kind="ExternalInput").ap()
    out = nc.dram_tensor("out", inputs["x"].shape, mybir.dt.float32, kind="ExternalOutput").ap()
    trunk(nc, t_in, out)
    return run_bass_kernel_spmd(nc, [arrays], core_ids=[0]).results[0]["out"]
```

```python
import math
from contextlib import ExitStack

import concourse.bass as bass
from concourse import mybir

P = 128
BANKS = 8
EPS = 1e-6
MASKED = -1.0e30


class Phase:

    def __init__(self, kind, units, row_tiles, **more):
        self.kind, self.units, self.row_tiles = kind, units, row_tiles
        self.groups = units // 4
        self.norm = more.get("norm")
        self.next_norm = more.get("next_norm")
        self.gate = more.get("gate")
        self.source = more.get("source")
        self.weights = more.get("weights")
        self.factor = more.get("factor", 1.0)
        self.next = None


def plan(phases):
    unit = pair = gate_act = h = 0
    for n, ph in enumerate(phases):
        ph.unit0, ph.pair0, ph.act0, ph.h0, ph.pair_end = unit, pair, gate_act, h, pair
        unit += ph.units
        if ph.kind == "pair":
            pair += ph.units // 2
            if ph.gate != "none":
                gate_act += ph.units // 2
            if ph.gate == "silu":
                h += ph.units // 2
        if n:
            phases[n - 1].next = ph
    return phases


def trunk(nc, t_in, out):
    f32, f32r = mybir.dt.float32, mybir.dt.float32r
    ACT, ALU, AX = mybir.ActivationFunctionType, mybir.AluOpType, mybir.AxisListType

    x_in = t_in["x"]
    _, S, D = x_in.shape
    FF = t_in["ffn1_w_gate"].shape[2]
    CONV = t_in["ev_conv_w"].shape[2]
    TAPS = t_in["ev_conv_w"].shape[1]
    TAPS_C = t_in["od_conv_w"].shape[1]
    HEADS = t_in["ev_b_f"].shape[1]
    HD = t_in["ev_q_norm"].shape[1]
    ATT = HEADS * HD
    KD, KF, TB = D // P, FF // P, S // P
    CB, AB = CONV // P, ATT // P
    HALF = KF // 2
    QK = 2 * AB

    w = {k: v[0] if v.shape[0] == 1 else v for k, v in t_in.items() if k.startswith(("ev_w", "od_w"))}

    def swiglu(name, layer, norm, next_norm):
        return [
            Phase("pair", 2 * KF, KD, norm=norm, gate="silu",
                  weights=(t_in[name + "_w_gate"][layer], 0, t_in[name + "_w_up"][layer], 0)),
            Phase("resid", 2 * KD, HALF, next_norm=next_norm, source="h", factor=0.5,
                  weights=t_in[name + "_w_down"][layer]),
        ]

    even_in, odd_in = w["ev_w_in"], w["od_w_in"]
    phases = plan(
        swiglu("ffn1", 0, 0, 1)
        + [Phase("pair", 2 * CB, KD, norm=1, gate="sigmoid", weights=(even_in, CONV, even_in, 0)),
           Phase("qk", QK, KD, norm=1, weights=(even_in, 2 * CONV)),
           Phase("v", KD // 2, KD, norm=1, weights=(even_in, 2 * CONV + 2 * ATT)),
           Phase("resid", KD, KD, next_norm=2, source="cat", weights=w["ev_w_out"])]
        + swiglu("ffn2", 0, 2, 3)
        + swiglu("ffn1", 1, 3, 4)
        + [Phase("pair", 2 * KD, KD, norm=4, gate="none", weights=(odd_in, D, odd_in, 2 * D)),
           Phase("single", KD, KD, norm=4, weights=(odd_in, 0)),
           Phase("resid", KD, KD, next_norm=5, source="y", weights=w["od_w_out"])]
        + swiglu("ffn2", 1, 5, None)
    )
    A_GATE, VP, A_OUT = phases[2], phases[4], phases[5]
    LAST = phases[-1]

    base = -(-nc.sbuf_base // 64) * 64
    end = [base]

    def room(nbytes):
        at = end[0]
        end[0] += -(-nbytes // 32) * 32
        return at

    def at(name, shape, dt, offset):
        return nc.alloc_sbuf_tensor_at(name, shape, dt, offset=offset)

    def own(name, shape, dt=f32):
        return at(name, shape, dt, room(4 * math.prod(shape[1:])))

    ROW = 4 * S
    SLOT = P * HALF
    x = own("x", [P, KD, S])
    XG = room(2 * KD * ROW)
    xg_hi, xg_lo = at("xg_hi", [P, KD, S], f32r, XG), at("xg_lo", [P, KD, S], f32r, XG + KD * ROW)
    H = room(2 * KF * ROW)
    h_hi, h_lo = at("h_hi", [P, KF, S], f32r, H), at("h_lo", [P, KF, S], f32r, H + KF * ROW)
    raw = own("raw", [P, 4, SLOT])
    w_hi, w_lo = own("w_hi", [P, 2, SLOT], f32r), own("w_lo", [P, 2, SLOT], f32r)
    rstd = own("rstd", [P, S])
    GATE, ACTED, SCALED, HID = room(2 * ROW), room(2 * ROW), room(ROW), room(ROW)
    gate = at("gate", [P, 2, S], f32, GATE)
    acted = at("acted", [P, 2, S], f32, ACTED)
    scaled = at("scaled", [P, S], f32, SCALED)
    hid = at("hid", [P, S], f32, HID)
    sq = own("sq", [P, 2, S])
    sq_sum = own("sq_sum", [P, S])
    cum = own("cum", [HEADS, S])
    WIDE = 2 * P
    ident, ones = own("ident", [P, P]), own("ones", [P, P])
    ident_r, mask_r = own("ident_r", [P, P], f32r), own("mask_r", [P, P + WIDE], f32r)
    GAINS = 6 * KD
    GAIN_COL = [(n % 3 * 2 + n // 3) * KD for n in range(6)]
    FIRST = 2 * KD
    V_CB, V_CN, V_OD = GAINS, GAINS + CB, GAINS + 2 * CB
    V_Q = V_OD + TAPS_C * KD
    NVEC = V_Q + 2
    vec = own("vec", [P, NVEC])
    conv_w = own("conv_w", [P, TAPS * CB])
    qk_gain = own("qk_gain", [P, 2])
    head_sel = own("head_sel", [P, QK, 2 * HEADS])
    wf_raw = own("wf_raw", [P, KD, HEADS])
    b_f = own("b_f", [HEADS, 1])
    rstd_col = own("rstd_col", [P, TB])
    neg_max = own("neg_max", [P, HEADS * TB])
    row_sum, row_inv = own("row_sum", [P, HEADS * TB]), own("row_inv", [P, HEADS * TB])

    mean_sq, root = at("mean_sq", [P, S], f32, GATE), at("root", [P, S], f32, GATE + ROW)
    rough, corr = at("rough", [P, S], f32, ACTED), at("corr", [P, S], f32, ACTED + ROW)

    x_rows = at("x_rows", [P, TB, D], f32, H)
    first_rows = at("first_rows", [FIRST, P], f32, H + TB * D * 4)
    vec_rows = at("vec_rows", [NVEC - FIRST, P], f32, H + TB * D * 4 + 4 * P)
    conv_rows = at("conv_rows", [TAPS * CB, P], f32, H + TB * D * 4 + 8 * P)

    q_hi, q_lo = at("q_hi", [P, AB, S], f32r, H), at("q_lo", [P, AB, S], f32r, H + AB * ROW)
    k_hi, k_lo = at("k_hi", [P, AB, S], f32r, H + 2 * AB * ROW), at("k_lo", [P, AB, S], f32r, H + 3 * AB * ROW)
    VAT = H + 4 * AB * ROW
    v_hi, v_lo = at("v_hi", [P, TB, ATT], f32r, VAT), at("v_lo", [P, TB, ATT], f32r, VAT + TB * ATT * 4)
    wf_hi, wf_lo = at("wf_hi", [P, KD, P], f32r, VAT), at("wf_lo", [P, KD, P], f32r, VAT + KD * P * 4)
    CAT = VAT + 2 * TB * ATT * 4
    cat_hi, cat_lo = at("cat_hi", [P, KD, S], f32r, CAT), at("cat_lo", [P, KD, S], f32r, CAT + KD * ROW)
    conv = at("conv", [P, CB, S], f32, CAT)
    qk_raw = at("qk_raw", [P, QK, S], f32, CAT + KD * ROW)
    AIN = CAT + 2 * KD * ROW
    a_in = at("a_in", [P, CB, S], f32, AIN)
    assert AIN + CB * ROW <= H + 2 * KF * ROW
    a_mean, a_root = at("a_mean", [P, S], f32, ACTED), at("a_root", [P, S], f32, ACTED + ROW)
    a_rough, a_corr = at("a_rough", [P, S], f32, SCALED), at("a_corr", [P, S], f32, HID)
    a_act = [at(f"a_act{b}", [P, S], f32, off)
             for b, off in enumerate((SCALED, HID, AIN + 2 * ROW, AIN + 3 * ROW))]
    assert HID == SCALED + ROW
    NORM_AT = H + (AB + 2) * ROW
    h_rough, h_corr = at("h_rough", [2 * HEADS, S], f32, NORM_AT), at("h_corr", [2 * HEADS, S], f32, NORM_AT + ROW)
    h_mean, h_root = (at(name, [2 * HEADS, S], f32, H + (2 * AB + 2 + n) * ROW)
                      for n, name in enumerate(("h_mean", "h_root")))
    head_rstd = [at(f"head_rstd{n}", [2 * HEADS, S], f32, H + (4 * AB - 2 + n) * ROW)
                 for n in range(2)]
    head_fan = at("head_fan", [2 * HEADS, QK, P], f32, SCALED)
    qk_nrm = at("qk_nrm", [P, 2, S], f32, ACTED)
    lf = [at(f"lf{i}", [HEADS, S], f32, H + (AB + i) * ROW) for i in range(4)]
    NPROD = 4
    tap_prod = at("tap_prod", [P, NPROD, S], f32, CAT + CB * ROW)
    row_sel = at("row_sel", [P, HEADS, P], f32r, GATE)
    cum_r, ncum_r = at("cum_r", [P, S], f32r, AIN), at("ncum_r", [P, S], f32r, AIN + ROW)
    NPR = 4
    probs = at("probs", [P, NPR, S], f32, CAT + KD * ROW)
    pt_hi = [at(f"pt_hi{i}", [P, TB, S], f32r, XG + 2 * i * TB * ROW) for i in range(2)]
    pt_lo = [at(f"pt_lo{i}", [P, TB, S], f32r, XG + (2 * i + 1) * TB * ROW) for i in range(2)]
    y_hi, y_lo = at("y_hi", [P, KD, S], f32r, H), at("y_lo", [P, KD, S], f32r, H + KD * ROW)
    c_in = at("c_in", [P, KD, S], f32, H + 2 * KD * ROW)
    c_out = at("c_out", [P, KD, S], f32, H + 3 * KD * ROW)
    fin = at("fin", [P, 2, S], f32, XG)
    out_rows = at("out_rows", [P, 2, TB, P], f32, XG + 2 * ROW)
    assert end[0] <= nc.sbuf_top, (end[0], nc.sbuf_top)

    DVE_TILES, ACT_TILES = list(range(1, CB - 1)), [0, CB - 1]
    TAPS_A, TAPS_QK = [0, 7, 9, 7], [3, 4, 5, 5, 4, 0, 5, 1]
    TAPS_LEFT = TAPS * len(DVE_TILES) - sum(TAPS_A) - sum(TAPS_QK)
    TAPS_T = [1, 1, 1] + [2] * ((TAPS_LEFT - 3) // 2) + [(TAPS_LEFT - 3) % 2]
    ACT_TAPS_A, ACT_TAPS_QK = [0, 6, 7, 7], [3, 1, 4, 4, 4, 4, 4, 4]
    ACT_TAPS_V, ACT_TAPS_T = 4, 2
    HEAD_ORDER = [half * AB + j for j in range(AB) for half in range(2)]
    CUM_AT = 6
    V_FANS = [(1, 1), (1, 3), (2, 1), (2, 3), (3, 1), (3, 3)]
    Q_ORDER = [TB - 1, 0, TB - 2, 1]
    SCALE_LAG, TURN_LAG = 2, 4
    LOW_LAG = TURN_LAG + 1
    PV_LAG = TURN_LAG + 2
    OUT_LAG = PV_LAG + TB
    STEPS = HEADS * TB + OUT_LAG
    NEXT_SPLIT = (22, 30)
    A_SUM = 10
    A_ROOT = A_SUM + 1
    A_SCALE = A_ROOT + TB
    A_SILU = HEADS * TB + 2
    assert len(TAPS_T) <= A_SUM - 2 and sorted(Q_ORDER) == list(range(TB))

    SRC = {"h": (h_hi, h_lo), "cat": (cat_hi, cat_lo), "y": (y_hi, y_lo)}

    def raws(ap):
        return ap.bitcast(f32)

    with ExitStack() as ctx:
        bank = [ctx.enter_context(nc.psum_tensor(f"bank{i}", [P, S], f32)) for i in range(BANKS)]

        def sem(name):
            return ctx.enter_context(nc.semaphore(name))

        x_arrived = [sem(f"x_arrived{i}") for i in range(4)]
        first_arrived, first_turned, first_ready = sem("first_arrived"), sem("first_turned"), sem("first_ready")
        tap_made, tap_added = sem("tap_made"), sem("tap_added")
        vec_arrived, conv_arrived, wf_arrived = sem("vec_arrived"), sem("conv_arrived"), sem("wf_arrived")
        w_arrived = [sem(f"w_arrived{i}") for i in range(4)]
        consts_ready, sel_ready, vec_turned, vec_ready = (
            sem("consts_ready"), sem("sel_ready"), sem("vec_turned"), sem("vec_ready"))
        qgain_ready, mask_cleared, identr_ready = (
            sem("qgain_ready"), sem("mask_cleared"), sem("identr_ready"))
        whi_ready, wlo_ready, unit_done = sem("whi_ready"), sem("wlo_ready"), sem("unit_done")
        x_turned = sem("x_turned")
        x_new, xhi_ready, xlo_ready = sem("x_new"), sem("xhi_ready"), sem("xlo_ready")
        sq_ready, sq_added, sq_cleared = sem("sq_ready"), sem("sq_added"), sem("sq_cleared")
        ssq_done, mean_ready, root_ready, rstd_ready = (
            sem("ssq_done"), sem("mean_ready"), sem("root_ready"), sem("rstd_ready"))
        gate_scaled, gate_acted, gate_ready, pair_out = (
            sem("gate_scaled"), sem("gate_acted"), sem("gate_ready"), sem("pair_out"))
        hhi_ready, hlo_ready = sem("hhi_ready"), sem("hlo_ready")
        step = sem("step")
        wf_cleared, wfhi_ready, wflo_ready, f_done = (
            sem("wf_cleared"), sem("wfhi_ready"), sem("wflo_ready"), sem("f_done"))
        col_done, col_ready = sem("col_done"), sem("col_ready")
        lf_abs, lf_exp, lf_log, cum_ready = (
            sem("lf_abs"), sem("lf_exp"), sem("lf_log"), sem("cum_ready"))
        cum_cleared, cumhi_ready, cumlo_ready = sem("cum_cleared"), sem("cumhi_ready"), sem("cumlo_ready")
        inv_ready, a_rstd = sem("inv_ready"), sem("a_rstd")
        pt_cleared = sem("pt_cleared")
        fan_ready, rsel_ready, rsel_step = sem("fan_ready"), sem("rsel_ready"), sem("rsel_step")
        qk_out, qk_sq, qk_sum = sem("qk_out"), sem("qk_sq"), sem("qk_sum")
        qk_mean, qk_root, qk_rstd, qk_fanned = sem("qk_mean"), sem("qk_root"), sem("qk_rstd"), sem("qk_fanned")
        qk_scaled, qkhi_ready, qklo_ready = sem("qk_scaled"), sem("qkhi_ready"), sem("qklo_ready")
        vhi_ready, vlo_ready = sem("vhi_ready"), sem("vlo_ready")
        scores_done, max_ready, exp_done, probs_ready = (
            sem("scores_done"), sem("max_ready"), sem("exp_done"), sem("probs_ready"))
        probs_turned, pthi_ready, ptlo_ready, pv_done = (
            sem("probs_turned"), sem("pthi_ready"), sem("ptlo_ready"), sem("pv_done"))
        ohi_ready, olo_ready = sem("ohi_ready"), sem("olo_ready")
        conv_done, a_sq, a_added, a_sum = sem("conv_done"), sem("a_sq"), sem("a_added"), sem("a_sum")
        am_ready, ar_ready = sem("am_ready"), sem("ar_ready")
        a_scaled, a_acted, ahi_ready, alo_ready = (
            sem("a_scaled"), sem("a_acted"), sem("ahi_ready"), sem("alo_ready"))
        conv3_step, conv3_done, y_gated = sem("conv3_step"), sem("conv3_done"), sem("y_gated")
        y_out, yhi_ready, ylo_ready = sem("y_out"), sem("yhi_ready"), sem("ylo_ready")
        out_turned, out_staged = sem("out_turned"), sem("out_staged")
        out_sent = [sem(f"out_sent{i}") for i in range(2)]

        block = ctx.enter_context(nc.Block())

        def unit_view(ph, tensor, slot):
            if ph.kind == "v":
                return tensor[:, slot, 0:2 * ATT].rearrange("p (k n) -> p k n", k=2)
            return tensor[:, slot, 0:ph.row_tiles * P].rearrange("p (k n) -> p k n", k=ph.row_tiles)

        @block.sync
        def _(sp):
            def load(ph, g, u):
                if isinstance(ph.weights, tuple) and ph.kind == "pair":
                    gw, gc, uw, uc = ph.weights
                    src, c0 = (gw, gc) if u % 2 == 0 else (uw, uc)
                    rows = src.rearrange("(k p) n -> p k n", p=P)
                    src = rows[:, :, bass.ds(c0 + (g * 2 + u // 2) * P, P)]
                elif ph.kind == "resid" and ph.row_tiles == HALF:
                    rows = ph.weights.rearrange("(k p) n -> p k n", p=P)
                    k0 = (u % 2) * HALF
                    src = rows[:, k0:k0 + HALF, bass.ds((g * 2 + u // 2) * P, P)]
                elif ph.kind == "v":
                    src = ph.weights[0].rearrange("(k p) n -> p k n", p=P)
                    src = src[:, 2 * u:2 * u + 2, ph.weights[1]:ph.weights[1] + ATT]
                else:
                    ww, c0 = ph.weights if isinstance(ph.weights, tuple) else (ph.weights, 0)
                    tile = HEAD_ORDER[g * 4 + u] if ph.kind == "qk" else g * 4 + u
                    src = ww.rearrange("(k p) n -> p k n", p=P)[:, :, bass.ds(c0 + tile * P, P)]
                if isinstance(g, int):
                    if ph.unit0 + 4 * g + u >= 4:
                        sp.wait_ge(wlo_ready, ph.unit0 + 4 * g + u - 3)
                else:
                    sp.wait_ge(wlo_ready, g * 4 + (ph.unit0 + u - 3))
                sp.dma_start(unit_view(ph, raw, u), src).then_inc(w_arrived[u], 16)

            def load_vectors():
                for n, name in enumerate(("mix_norm", "ffn2_norm")):
                    sp.dma_start(vec_rows[n * 2 * KD:(n + 1) * 2 * KD, :],
                                 t_in[name].rearrange("l (k p) -> (l k) p", p=P)).then_inc(vec_arrived, 16)
                for name, r0, r1 in (("ev_conv_b", V_CB, V_CN), ("ev_conv_norm", V_CN, V_OD)):
                    sp.dma_start(vec_rows[r0 - FIRST:r1 - FIRST, :], t_in[name].rearrange("o (k p) -> (o k) p", p=P))\
                        .then_inc(vec_arrived, 16)
                sp.dma_start(vec_rows[V_OD - FIRST:V_Q - FIRST, :],
                              t_in["od_conv_w"][0].rearrange("t (k p) -> (t k) p", p=P)).then_inc(vec_arrived, 16)
                for n, name in enumerate(("ev_q_norm", "ev_k_norm")):
                    for half in range(2):
                        row = V_Q + n - FIRST
                        sp.dma_start(vec_rows[row:row + 1, half * HD:(half + 1) * HD], t_in[name])\
                            .then_inc(vec_arrived, 16)
                sp.dma_start(conv_rows[:, :], t_in["ev_conv_w"][0].rearrange("t (b p) -> (t b) p", p=P))\
                    .then_inc(conv_arrived, 16)
                sp.dma_start(wf_raw[:, :, :],
                              even_in.rearrange("(k p) n -> p k n", p=P)[:, :, 2 * CONV + 3 * ATT:])\
                    .then_inc(wf_arrived, 16)
                sp.dma_start(b_f[:, :], t_in["ev_b_f"].rearrange("o h -> h o")).then_inc(wf_arrived, 16)

            QD = D // len(x_arrived)
            for i in range(len(x_arrived)):
                cols = slice(i * QD, (i + 1) * QD)
                sp.dma_start(x_rows[:, :, cols], x_in[0].rearrange("(t p) d -> p t d", p=P)[:, :, cols])\
                    .then_inc(x_arrived[i], 16)
                if i == 0:
                    load(phases[0], 0, 0)
            for ph in phases:
                for u in range(4):
                    if ph is not phases[0] or u > 0:
                        load(ph, 0, u)
                if ph is phases[0]:
                    load_vectors()
                if ph.groups > 1:
                    with sp.Fori(1, ph.groups) as g:
                        for u in range(4):
                            load(ph, g, u)

        @block.gpsimd
        def _(pool):
            pool.memset(ident[:, :], 0.0).then_inc(consts_ready, 1)
            pool.memset(ones[:, :], 1.0).then_inc(consts_ready, 1)
            pool.memset(sq_sum[:, :], 0.0).then_inc(sq_cleared, 1)
            pool.wait_ge(consts_ready, 2)
            pool.affine_select(out=ident[:, :], in_=ident[:, :], compare_op=ALU.not_equal, fill=1.0, base=0,
                               pattern=[[-1, P]], channel_multiplier=1).then_inc(consts_ready, 1)
            pool.memset(head_sel[:, :, :], 0.0).then_inc(sel_ready, 1)
            pool.wait_ge(sel_ready, 1)
            for t in range(QK):
                for half in range(2):
                    pool.memset(head_sel[half * HD:(half + 1) * HD, t, 2 * t + half:2 * t + half + 1], 1.0)\
                        .then_inc(sel_ready, 1)
            pool.wait_ge(sel_ready, 1 + 2 * QK)
            pool.memset(raws(mask_r[:, :]), 0.0).then_inc(mask_cleared, 1)
            pool.wait_ge(mask_cleared, 1)
            pool.affine_select(out=mask_r[:, P:2 * P], in_=raws(mask_r[:, P:2 * P]), compare_op=ALU.is_ge,
                               fill=MASKED, base=0, pattern=[[-1, P]], channel_multiplier=1).then_inc(sel_ready, 1)

            def add_squares(norm):
                if norm:
                    pool.wait_ge(ssq_done, norm)
                    pool.memset(sq_sum[:, :], 0.0).then_inc(sq_cleared, 1)
                pool.wait_ge(sq_cleared, norm + 1)
                with pool.Fori(0, KD // 2) as g:
                    for half in range(2):
                        pool.wait_ge(sq_ready, g * 2 + (KD * norm + half + 1))
                        pool.tensor_tensor(sq_sum[:, :], sq_sum[:, :], sq[:, half, :], ALU.add)\
                            .then_inc(sq_added, 1)
                        pool.wait_ge(sq_added, g * 2 + (KD * norm + half + 1))

            pool_taps = [0]

            def add_taps(n):
                for m in range(pool_taps[0], min(pool_taps[0] + n, TAPS * len(ACT_TILES))):
                    b, shift = ACT_TILES[m // TAPS], m % TAPS
                    if shift == 0:
                        continue
                    p = m - m // TAPS - 1
                    pool.wait_ge(tap_made, m + 1)
                    if p:
                        pool.wait_ge(tap_added, p)
                    pool.tensor_tensor(conv[:, b, shift:S], conv[:, b, shift:S], tap_prod[:, p % NPROD, 0:S - shift],
                                       ALU.add).then_inc(tap_added, 1)
                pool_taps[0] += n

            def gates(ph):
                pool.wait_ge(rstd_ready, ph.norm + 1)
                n = ph.units // 2

                def one(f, par):
                    src = gate if ph.gate == "none" else acted
                    if ph.gate == "none":
                        pool.wait_ge(gate_scaled, f + (ph.pair0 + 1))
                    else:
                        pool.wait_ge(gate_acted, f + (ph.act0 + 1))
                    if not isinstance(f, int) or ph.pair0 + f > 0:
                        pool.wait_ge(pair_out, f + ph.pair0)
                    pool.tensor_tensor(scaled[:, :], src[:, par, :], rstd[:, :], ALU.mult).then_inc(gate_ready, 1)

                one(0, 0)
                one(1, 1)
                if ph is A_GATE:
                    add_taps(ACT_TAPS_A[1])
                    for f in range(2, n):
                        one(f, f % 2)
                        add_taps(ACT_TAPS_A[f])
                    return
                with pool.Fori(1, n // 2) as g:
                    for par in range(2):
                        one(g * 2 + par, par)

            for ph in phases:
                if ph.norm == 0 and ph.kind == "pair":
                    add_squares(0)
                if ph is A_GATE:
                    pool.wait_ge(unit_done, ph.unit0)
                    pool.memset(raws(wf_hi[:, :, :]), 0.0).then_inc(wf_cleared, 1)
                    pool.memset(raws(wf_lo[:, :, :]), 0.0).then_inc(wf_cleared, 1)
                if ph.kind == "pair":
                    gates(ph)
                if ph.kind == "single":
                    with pool.Fori(0, KD) as f:
                        pool.wait_ge(conv3_done, f + 1)
                        tile = c_out[:, bass.ds(f, 1), :]
                        pool.tensor_tensor(tile, tile, rstd[:, :].unsqueeze(1), ALU.mult).then_inc(y_gated, 1)
                if ph is A_GATE:
                    pool.wait_ge(pair_out, ph.pair0 + CB)
                    pool.memset(head_fan[:, :, :], 0.0).then_inc(fan_ready, 1)
                    pool.wait_ge(fan_ready, 1)
                    view = head_fan[:, :, :].rearrange("r t (a c) -> r t a c", a=2)
                    pool.affine_select(out=view, in_=view, compare_op=ALU.not_equal, fill=1.0, base=0,
                                       pattern=[[-2, QK], [-1, 2], [0, HD]], channel_multiplier=1)\
                        .then_inc(fan_ready, 1)
                    pool.wait_ge(fan_ready, 2)
                    pool.wait_ge(rstd_ready, 2)
                    pool.wait_ge(gate_acted, ph.act0 + CB)
                    pool.memset(raws(row_sel[:, :, :]), 0.0).then_inc(rsel_step, 1)
                    for n, off in enumerate(range(0, P, 32)):
                        pool.wait_ge(rsel_step, n + 1)
                        done = rsel_ready if off == P - 32 else rsel_step
                        pool.affine_select(out=row_sel[:, :, :], in_=raws(row_sel[:, :, :]), compare_op=ALU.not_equal,
                                           fill=1.0, base=-off, pattern=[[-1, HEADS], [0, P]],
                                           channel_multiplier=1).then_inc(done, 1)
                    for n in range(QK):
                        add_taps(ACT_TAPS_QK[n])
                        if n == CUM_AT - 1:
                            pool.wait_ge(conv_done, 1)
                            pool.memset(raws(cum_r[:, :]), 0.0).then_inc(cum_cleared, 1)
                            pool.memset(raws(ncum_r[:, :]), 0.0).then_inc(cum_cleared, 1)
                if ph is VP:
                    add_taps(ACT_TAPS_V)
                    pool.wait_ge(unit_done, ph.unit0 + ph.units)
                    for pt in pt_hi + pt_lo:
                        pool.memset(raws(pt[:, TB - 1, S - WIDE:S - P]), 0.0).then_inc(pt_cleared, 1)
                    add_taps(TAPS * len(ACT_TILES))
                    pool.wait_ge(ssq_done, 2)
                    for b in range(1, CB):
                        pool.wait_ge(a_sq, b + 1)
                        if b > 1:
                            pool.wait_ge(a_added, b - 1)
                        first = sq[:, 0, :] if b == 1 else sq_sum[:, :]
                        pool.tensor_tensor(sq_sum[:, :], first, sq[:, b % 2, :], ALU.add).then_inc(a_added, 1)
                    pool.wait_ge(a_rstd, 1)
                    for b in range(CB):
                        pool.tensor_tensor(conv[:, b, :], conv[:, b, :], rstd[:, :], ALU.mult).then_inc(a_scaled, 1)
                if ph.kind == "resid" and ph.next_norm is not None:
                    if ph is A_OUT:
                        pool.wait_ge(a_sum, 1)
                    add_squares(ph.next_norm)

        @block.scalar
        def _(act):
            act.dma_start(first_rows[:, :], t_in["ffn1_norm"].rearrange("l (k p) -> (l k) p", p=P))\
                .then_inc(first_arrived, 16)

            def split_hi(ph, g, u):
                if u >= 4 and isinstance(g, int) and g == ph.groups - 1:
                    ph, g, u = ph.next, 0, u - 4
                    if ph is None:
                        return
                n = ph.row_tiles * P
                i = ph.unit0 + u if not isinstance(g, int) else ph.unit0 + u + 4 * g
                if isinstance(g, int):
                    act.wait_ge(w_arrived[u % 4], 16 * (i // 4 + 1))
                    if i >= 2:
                        act.wait_ge(unit_done, i - 1)
                else:
                    act.wait_ge(w_arrived[u % 4], g * 16 + 16 * (i // 4 + 1))
                    act.wait_ge(unit_done, g * 4 + (i - 1))
                act.activation(w_hi[:, u % 2, 0:n], raw[:, u % 4, 0:n], ACT.Copy).then_inc(whi_ready, 1)

            def new_x(j, half, norm):
                act.wait_ge(x_new, j + (KD * norm + 1))
                if not isinstance(j, int) or KD * norm + j >= 2:
                    act.wait_ge(sq_added, j + (KD * norm - 1))
                one = bass.ds(j, 1)
                act.activation(xg_hi[:, one, :], x[:, one, :], ACT.Copy, scale=vec[:, bass.ds(j + GAIN_COL[norm], 1)])\
                    .then_inc(xhi_ready, 1)
                act.activation(sq[:, half:half + 1, :], x[:, one, :], ACT.Square).then_inc(sq_ready, 1)

            def norm_root(ready, n, mean, out_root, done):
                act.wait_ge(ready, n)
                act.activation(out_root, mean, ACT.Sqrt).then_inc(done, 1)

            def pair(ph):
                def group(g):
                    first = isinstance(g, int) and g == 0
                    for u in range(4):
                        f, par = g * 2 + u // 2, u // 2
                        if not (first and u in (1, 2)):
                            split_hi(ph, g, u + 2)
                        if first and u == 1:
                            split_hi(ph, g, 4)
                        if ph is A_GATE and first and u == 3:
                            act.wait_ge(wf_arrived, 32)
                            act.wait_ge(wf_cleared, 2)
                            act.activation(wf_hi[:, :, 0:HEADS], wf_raw[:, :, :], ACT.Copy).then_inc(wfhi_ready, 1)
                        if first and u == 0:
                            norm_root(mean_ready, ph.norm + 1, mean_sq[:, :], root[:, :], root_ready)
                            split_hi(ph, g, 3)
                        if u % 2 == 0 and ph.gate != "none":
                            func = ACT.Silu if ph.gate == "silu" else ACT.Sigmoid
                            act.wait_ge(gate_scaled, f + (ph.pair0 + 1))
                            if not first:
                                act.wait_ge(gate_ready, f + (ph.pair0 - 1))
                            act.activation(acted[:, par, :], gate[:, par, :], func).then_inc(gate_acted, 1)
                        if u % 2 == 1 and ph.gate == "silu":
                            act.wait_ge(pair_out, f + (ph.pair0 + 1))
                            act.activation(h_hi[:, bass.ds(f, 1), :], hid[:, :], ACT.Copy).then_inc(hhi_ready, 1)
                        if u % 2 == 1 and ph is A_GATE:
                            conv_taps(ACT_TAPS_A[f])

                run_groups(ph, group)

            def run_groups(ph, group):
                peeled = 2 if ph is LAST else 1
                for g in range(min(peeled, ph.groups)):
                    group(g)
                if ph.groups - 1 > peeled:
                    with act.Fori(peeled, ph.groups - 1) as g:
                        group(g)
                if ph.groups > peeled:
                    group(ph.groups - 1)

            def resid(ph):
                per_tile = 2 if ph.row_tiles == HALF else 1

                def group(g):
                    for u in range(4):
                        split_hi(ph, g, u + 2)
                        if u % per_tile == per_tile - 1 and ph.next_norm is not None:
                            j = g * (4 // per_tile) + u // per_tile
                            new_x(j, (u // per_tile) % 2, ph.next_norm)
                        if ph is LAST and u % 2 == 1:
                            send(g * 2 + u // 2 - 1, 1 - u // 2)

                run_groups(ph, group)
                if ph is LAST:
                    send(KD - 1, 1)
                    for i in range(2):
                        act.wait_ge(out_sent[i], 16 * (KD // 2))

            def send(j, par):
                if isinstance(j, int):
                    if j < 0:
                        return
                    if j >= 2:
                        act.wait_ge(out_sent[par], 16 * (j // 2))
                else:
                    act.wait_ge(out_sent[par], (j - par) * 8)
                act.wait_ge(out_turned, j + 1)
                act.activation(out_rows[:, par, :, :], bank[6 + par][:, :].rearrange("p (t c) -> p t c", t=TB),
                               ACT.Copy).then_inc(out_staged, 1)
                act.wait_ge(out_staged, j + 1)
                act.dma_start(out[0].rearrange("(t p) d -> p t d", p=P)[:, :, bass.ds(j * P, P)],
                              out_rows[:, par, :, :]).then_inc(out_sent[par], 16)

            act_taps = [0]

            def conv_taps(n):
                for m in range(act_taps[0], min(act_taps[0] + n, TAPS * len(ACT_TILES))):
                    b, shift = ACT_TILES[m // TAPS], m % TAPS
                    k = TAPS - 1 - shift
                    wk = conv_w[:, k * CB + b:k * CB + b + 1]
                    if shift == 0:
                        act.wait_ge(pair_out, A_GATE.pair0 + b + 1)
                        act.activation(conv[:, b, :], a_in[:, b, :], ACT.Identity, scale=wk,
                                       bias=vec[:, V_CB + b:V_CB + b + 1]).then_inc(tap_made, 1)
                        continue
                    p = m - m // TAPS - 1
                    if p >= NPROD:
                        act.wait_ge(tap_added, p - NPROD + 1)
                    act.activation(tap_prod[:, p % NPROD, 0:S - shift], a_in[:, b, 0:S - shift], ACT.Copy,
                                   scale=wk).then_inc(tap_made, 1)
                act_taps[0] += n

            def qk_high(n):
                t = HEAD_ORDER[n]
                dst = q_hi if t < AB else k_hi
                act.wait_ge(qk_scaled, n + 1)
                act.activation(dst[:, t % AB, :], qk_nrm[:, n % 2, :], ACT.Copy,
                               scale=qk_gain[:, t // AB:t // AB + 1]).then_inc(qkhi_ready, 1)

            def norm_squares(b, n):
                if n >= 2:
                    act.wait_ge(a_added, 1)
                act.activation(sq[:, n % 2, :], conv[:, b, :], ACT.Square).then_inc(a_sq, 1)

            def conv_silu(b):
                act.wait_ge(a_scaled, b + 1)
                act.activation(a_act[b][:, :], conv[:, b, :], ACT.Silu,
                               scale=vec[:, V_CN + b:V_CN + b + 1]).then_inc(a_acted, 1)
                act.wait_ge(a_acted, b + 1)
                act.activation(cat_hi[:, b, :], a_act[b][:, :], ACT.Copy).then_inc(ahi_ready, 1)

            def attention(ph):
                for t in range(STEPS):
                    if t in NEXT_SPLIT:
                        split_hi(ph, 0, 4 + NEXT_SPLIT.index(t))
                    if t < HEADS * TB:
                        n = (Q_ORDER[t % TB] + 1) * P
                        act.wait_ge(max_ready, t + 1)
                        if t >= NPR:
                            act.wait_ge(probs_turned, t - NPR + 1)
                        act.activation(probs[:, t % NPR, 0:n], bank[t % 3][:, 0:n], ACT.Exp,
                                       bias=neg_max[:, t:t + 1], accum_out=row_sum[:, t:t + 1]).then_inc(exp_done, 1)
                    if 0 <= t - SCALE_LAG < HEADS * TB:
                        tt = t - SCALE_LAG
                        n = (Q_ORDER[tt % TB] + 1) * P
                        act.wait_ge(inv_ready, tt + 1)
                        act.activation(probs[:, tt % NPR, 0:n], probs[:, tt % NPR, 0:n], ACT.Copy,
                                       scale=row_inv[:, tt:tt + 1]).then_inc(probs_ready, 1)
                    if 0 <= t - TURN_LAG < HEADS * TB:
                        tt = t - TURN_LAG
                        h, qb = tt // TB, Q_ORDER[tt % TB]
                        act.wait_ge(probs_turned, tt + 1)
                        if h >= 2:
                            act.wait_ge(pv_done, h - 1)
                        act.activation(pt_hi[h % 2][:, 0:qb + 1, qb * P:(qb + 1) * P],
                                       bank[4 + tt % 2][:, 0:(qb + 1) * P].rearrange("p (k q) -> p k q", q=P),
                                       ACT.Copy).then_inc(pthi_ready, 1)
                    if t >= TB - 1 + OUT_LAG and (t - (TB - 1) - OUT_LAG) % TB == 0:
                        h = (t - (TB - 1) - OUT_LAG) // TB
                        p0 = (h % 2) * HD
                        act.wait_ge(pv_done, h + 1)
                        act.activation(cat_hi[p0:p0 + HD, CB + h // 2, :], bank[6 + h % 2][p0:p0 + HD, :], ACT.Copy)\
                            .then_inc(ohi_ready, 1)
                    if t == 0:
                        qk_high(QK - 1)
                    conv_taps(ACT_TAPS_T)
                    if t == A_SUM - 3:
                        act.wait_ge(tap_added, TAPS - 1)
                        norm_squares(0, 0)
                        act.wait_ge(conv_done, 1)
                        norm_squares(1, 1)
                    if t == A_SUM - 2:
                        act.wait_ge(conv_done, 2)
                        norm_squares(2, 2)
                    if t == A_SUM - 1:
                        act.wait_ge(tap_added, 2 * (TAPS - 1))
                        norm_squares(3, 3)
                    if t == A_ROOT:
                        norm_root(am_ready, 1, a_mean[:, :], a_root[:, :], ar_ready)
                    if A_SILU <= t < A_SILU + CB:
                        conv_silu(t - A_SILU)

            act.wait_ge(consts_ready, 3)
            act.activation(ident_r[:, :], ident[:, :], ACT.Copy).then_inc(identr_ready, 1)
            act.wait_ge(first_ready, 1)
            new_x(0, 0, 0)
            split_hi(phases[0], 0, 0)
            new_x(1, 1, 0)
            with act.Fori(1, KD // 2) as g:
                for half in range(2):
                    new_x(g * 2 + half, half, 0)
            split_hi(phases[0], 0, 1)
            for ph in phases:
                if ph.kind == "pair":
                    pair(ph)
                elif ph.kind == "resid":
                    resid(ph)
                elif ph.kind == "single":
                    for i in range(ph.units):
                        split_hi(ph, i // 4, i % 4 + 2)
                        act.wait_ge(y_out, i + 1)
                        act.activation(y_hi[:, i, :], hid[:, :], ACT.Copy).then_inc(yhi_ready, 1)
                elif ph.kind == "qk":
                    act.wait_ge(vec_ready, 2)
                    act.activation(qk_gain[:, 0:1], vec[:, V_Q:V_Q + 1], ACT.Copy, scale=1.0 / math.sqrt(HD))\
                        .then_inc(qgain_ready, 1)
                    act.activation(qk_gain[:, 1:2], vec[:, V_Q + 1:V_Q + 2], ACT.Copy).then_inc(qgain_ready, 1)
                    for i in range(ph.units):
                        if i == AB + 1:
                            norm_root(qk_mean, 1, h_mean[:, :], h_root[:, :], qk_root)
                        split_hi(ph, i // 4, i % 4 + 2)
                        act.wait_ge(qk_out, i + 1)
                        if i >= 2:
                            act.wait_ge(qk_sum, i - 1)
                        act.activation(sq[:, i % 2, :], qk_raw[:, i, :], ACT.Square).then_inc(qk_sq, 1)
                        if i == 1:
                            act.wait_ge(lf_abs, 1)
                            act.activation(lf[2][:, :], lf[1][:, :], ACT.Exp, scale=-1.0).then_inc(lf_exp, 1)
                            act.wait_ge(lf_exp, 1)
                            act.activation(lf[3][:, :], lf[2][:, :], ACT.Ln, bias=1.0).then_inc(lf_log, 1)
                        if i == CUM_AT:
                            act.wait_ge(cum_ready, 1)
                            act.wait_ge(cum_cleared, 2)
                            for r in range(0, P, HD):
                                act.activation(cum_r[r:r + HEADS, :], cum[:, :], ACT.Copy).then_inc(cumhi_ready, 1)
                                act.activation(ncum_r[r:r + HEADS, :], cum[:, :], ACT.Copy, scale=-1.0)\
                                    .then_inc(cumhi_ready, 1)
                        conv_taps(ACT_TAPS_QK[i])
                elif ph.kind == "v":
                    norm_root(qk_mean, 2, h_mean[:, :], h_root[:, :], qk_root)
                    act.wait_ge(qgain_ready, 2)
                    qk_high(0)
                    split_hi(ph, 0, 2)
                    qk_high(1)
                    qk_high(2)
                    qk_high(3)
                    split_hi(ph, 0, 3)
                    conv_taps(ACT_TAPS_V)
                    for n in range(AB, QK - 1):
                        qk_high(n)
                    act.wait_ge(unit_done, ph.unit0 + ph.units)
                    act.wait_ge(col_ready, 1)
                    for tb in range(TB):
                        act.activation(v_hi[:, tb, :], bank[tb][:, :], ACT.Copy, scale=rstd_col[:, tb:tb + 1])\
                            .then_inc(vhi_ready, 1)
                    attention(ph)

        @block.vector
        def _(dve):
            links = [0]

            def link(instruction):
                links[0] += 1
                instruction.then_inc(step, 1)
                dve.wait_ge(step, links[0])

            def run_groups(ph, group):
                group(0)
                if ph.groups > 2:
                    with dve.Fori(1, ph.groups - 1) as g:
                        group(g)
                if ph.groups > 1:
                    group(ph.groups - 1)

            def split_lo(ph, g, u):
                if u >= 4 and isinstance(g, int) and g == ph.groups - 1:
                    ph, g, u = ph.next, 0, u - 4
                    if ph is None:
                        return
                n = ph.row_tiles * P
                dve.wait_ge(whi_ready, g * 4 + (ph.unit0 + u + 1))
                dve.tensor_tensor(w_lo[:, u % 2, 0:n], raw[:, u % 4, 0:n], raws(w_hi[:, u % 2, 0:n]), ALU.subtract)\
                    .then_inc(wlo_ready, 1)

            def xg_low(j, norm):
                dve.wait_ge(xhi_ready, j + (KD * norm + 1))
                one = bass.ds(j, 1)
                dve.scalar_tensor_tensor(xg_lo[:, one, :], x[:, one, :], vec[:, bass.ds(j + GAIN_COL[norm], 1)],
                                         raws(xg_hi[:, one, :]), ALU.mult, ALU.subtract).then_inc(xlo_ready, 1)

            def invert(mean, rough_, corr_, out_):
                link(dve.tensor_tensor(corr_, rough_, rough_, ALU.mult))
                link(dve.scalar_tensor_tensor(corr_, corr_, -0.5, mean, ALU.mult, ALU.mult))
                return dve.scalar_tensor_tensor(out_, corr_, 1.5, rough_, ALU.add, ALU.mult)

            tap_order = [(b, n) for b in DVE_TILES for n in range(TAPS)]
            taps, tap_step = [0], {}

            def conv_taps(n):
                for b, shift in tap_order[taps[0]:taps[0] + n]:
                    k = TAPS - 1 - shift
                    wk = conv_w[:, k * CB + b:k * CB + b + 1]
                    if shift == 0:
                        dve.wait_ge(pair_out, A_GATE.pair0 + b + 1)
                        op = dve.tensor_scalar(conv[:, b, :], a_in[:, b, :], wk, vec[:, V_CB + b:V_CB + b + 1],
                                               ALU.mult, ALU.add)
                    else:
                        dve.wait_ge(step, tap_step[b])
                        op = dve.scalar_tensor_tensor(conv[:, b, shift:S], a_in[:, b, 0:S - shift], wk,
                                                      conv[:, b, shift:S], ALU.mult, ALU.add)
                    if k == 0:
                        op.then_inc(conv_done, 1)
                    else:
                        links[0] += 1
                        op.then_inc(step, 1)
                        tap_step[b] = links[0]
                taps[0] += n

            def pair(ph):
                def group(g):
                    first = isinstance(g, int) and g == 0
                    for u in range(4):
                        f, half = g * 2 + u // 2, u // 2
                        if ph is A_GATE and not first and u == 0:
                            dve.wait_ge(wfhi_ready, 1)
                            dve.tensor_tensor(wf_lo[:, :, 0:HEADS], wf_raw[:, :, :], raws(wf_hi[:, :, 0:HEADS]),
                                              ALU.subtract).then_inc(wflo_ready, 1)
                        if not (first and u in (1, 2)):
                            split_lo(ph, g, u + 2)
                        if first and u == 1:
                            split_lo(ph, g, 4)
                        if first and u == 3 and ph is phases[0]:
                            dve.wait_ge(vec_turned, 2)
                            dve.tensor_copy(vec[:, FIRST:NVEC], bank[7][:, 0:NVEC - FIRST]).then_inc(vec_ready, 1)
                            dve.tensor_copy(conv_w[:, :], bank[7][:, P:P + TAPS * CB]).then_inc(vec_ready, 1)
                        if first and u == 0:
                            dve.wait_ge(ssq_done, ph.norm + 1)
                            dve.tensor_scalar(mean_sq[:, :], bank[6][:, :], 1.0 / D, EPS, ALU.mult, ALU.add)\
                                .then_inc(mean_ready, 1)
                            dve.wait_ge(root_ready, ph.norm + 1)
                            link(dve.reciprocal(rough[:, :], root[:, :]))
                            split_lo(ph, g, 3)
                            invert(mean_sq[:, :], rough[:, :], corr[:, :], rstd[:, :]).then_inc(rstd_ready, 1)
                            dve.wait_ge(rstd_ready, ph.norm + 1)
                        dve.wait_ge(unit_done, g * 4 + (ph.unit0 + u + 1))
                        if u % 2 == 0:
                            dve.tensor_tensor(gate[:, half, :], bank[u][:, :], rstd[:, :], ALU.mult)\
                                .then_inc(gate_scaled, 1)
                            continue
                        dve.wait_ge(gate_ready, f + (ph.pair0 + 1))
                        if ph.gate == "silu":
                            dve.tensor_tensor(hid[:, :], bank[u][:, :], scaled[:, :], ALU.mult).then_inc(pair_out, 1)
                            dve.wait_ge(hhi_ready, f + (ph.h0 + 1))
                            one = bass.ds(f, 1)
                            dve.tensor_tensor(h_lo[:, one, :], hid[:, :].unsqueeze(1), raws(h_hi[:, one, :]),
                                              ALU.subtract).then_inc(hlo_ready, 1)
                        elif ph.gate == "sigmoid":
                            dve.tensor_tensor(a_in[:, f, :], bank[u][:, :], scaled[:, :], ALU.mult)\
                                .then_inc(pair_out, 1)
                            conv_taps(TAPS_A[f])
                        else:
                            c1, o1 = c_in[:, bass.ds(f, 1), :], c_out[:, bass.ds(f, 1), :]
                            dve.tensor_tensor(c1, bank[u][:, :].unsqueeze(1), scaled[:, :].unsqueeze(1), ALU.mult)\
                                .then_inc(pair_out, 1)
                            dve.wait_ge(pair_out, f + (ph.pair0 + 1))
                            for s in range(TAPS_C):
                                wk = vec[:, bass.ds(f + (V_OD + (TAPS_C - 1 - s) * KD), 1)]
                                if s == 0:
                                    op = dve.tensor_scalar(o1, c1, wk, None, ALU.mult)
                                else:
                                    o_, c_ = c_out[:, bass.ds(f, 1), s:S], c_in[:, bass.ds(f, 1), 0:S - s]
                                    op = dve.scalar_tensor_tensor(o_, c_, wk, o_, ALU.mult, ALU.add)
                                if s < TAPS_C - 1:
                                    op.then_inc(conv3_step, 1)
                                    dve.wait_ge(conv3_step, f * (TAPS_C - 1) + (s + 1))
                                else:
                                    op.then_inc(conv3_done, 1)

                run_groups(ph, group)

            def resid(ph):
                per_tile = 2 if ph.row_tiles == HALF else 1

                def group(g):
                    for u in range(4):
                        if u % per_tile == per_tile - 1:
                            j, half = g * (4 // per_tile) + u // per_tile, (u // per_tile) % 2
                            one = bass.ds(j, 1)
                            dve.wait_ge(unit_done, g * 4 + (ph.unit0 + u + 1))
                            ps = bank[4 + half][:, :].unsqueeze(1)
                            if ph is LAST:
                                if not isinstance(j, int) or j >= 2:
                                    dve.wait_ge(out_turned, j - 1)
                                dve.scalar_tensor_tensor(fin[:, half:half + 1, :], ps, ph.factor, x[:, one, :],
                                                         ALU.mult, ALU.add).then_inc(x_new, 1)
                            else:
                                dve.scalar_tensor_tensor(x[:, one, :], ps, ph.factor, x[:, one, :],
                                                         ALU.mult, ALU.add).then_inc(x_new, 1)
                        split_lo(ph, g, u + 2)
                        if u % per_tile == per_tile - 1 and ph is not LAST:
                            xg_low(j, ph.next_norm)

                run_groups(ph, group)

            def qk_low(n):
                t = HEAD_ORDER[n]
                lo, hi = (q_lo, q_hi) if t < AB else (k_lo, k_hi)
                dve.wait_ge(qk_fanned, n + 1)
                dve.tensor_tensor(qk_nrm[:, n % 2, :], qk_raw[:, n, :], bank[4 + n % 2][:, :], ALU.mult)\
                    .then_inc(qk_scaled, 1)
                dve.wait_ge(qkhi_ready, n + 1)
                dve.scalar_tensor_tensor(lo[:, t % AB, :], qk_nrm[:, n % 2, :], qk_gain[:, t // AB:t // AB + 1],
                                         raws(hi[:, t % AB, :]), ALU.mult, ALU.subtract).then_inc(qklo_ready, 1)

            heads = slice(0, 2 * HEADS)

            def head_mean(n):
                dve.wait_ge(qk_sum, AB * n)
                dve.tensor_scalar(h_mean[:, :], bank[5 + n][heads, :], 1.0 / HD, EPS, ALU.mult, ALU.add)\
                    .then_inc(qk_mean, 1)

            def head_rough(n):
                dve.wait_ge(qk_root, n)
                link(dve.reciprocal(h_rough[:, :], h_root[:, :]))

            def head_invert(n):
                invert(h_mean[:, :], h_rough[:, :], h_corr[:, :], head_rstd[n - 1][:, :]).then_inc(qk_rstd, 1)

            def conv_norm(t):
                if t == A_SUM:
                    dve.wait_ge(a_sum, 1)
                    dve.tensor_scalar(a_mean[:, :], bank[3][:, :], 1.0 / CONV, EPS, ALU.mult, ALU.add)\
                        .then_inc(am_ready, 1)
                if A_ROOT <= t < A_ROOT + TB:
                    dve.wait_ge(ar_ready, 1)
                    part = slice((t - A_ROOT) * P, (t - A_ROOT + 1) * P)
                    link(dve.reciprocal(a_rough[:, part], a_root[:, part]))
                if t == A_SCALE:
                    link(dve.tensor_tensor(a_corr[:, :], a_rough[:, :], a_rough[:, :], ALU.mult))
                if t == A_SCALE + 1:
                    link(dve.scalar_tensor_tensor(a_corr[:, :], a_corr[:, :], -0.5, a_mean[:, :], ALU.mult, ALU.mult))
                if t == A_SCALE + 2:
                    dve.scalar_tensor_tensor(rstd[:, :], a_corr[:, :], 1.5, a_rough[:, :], ALU.add, ALU.mult)\
                        .then_inc(a_rstd, 1)

            def attention(ph):
                head_mean(2)
                qk_low(0)
                head_rough(2)
                split_lo(ph, 0, 2)
                head_invert(2)
                qk_low(1)
                qk_low(2)
                qk_low(3)
                dve.wait_ge(cumhi_ready, 2 * (P // HD))
                for r in range(32, P, HD):
                    dve.tensor_tensor(cum_r[r:r + HEADS, :], cum[:, :], raws(cum_r[0:HEADS, :]), ALU.subtract)\
                        .then_inc(cumlo_ready, 1)
                    dve.tensor_tensor(ncum_r[r:r + HEADS, :], raws(cum_r[0:HEADS, :]), cum[:, :], ALU.subtract)\
                        .then_inc(cumlo_ready, 1)
                split_lo(ph, 0, 3)
                for n in range(AB, QK - 1):
                    qk_low(n)
                for tb in range(TB):
                    dve.wait_ge(vhi_ready, tb + 1)
                    dve.scalar_tensor_tensor(v_lo[:, tb, :], bank[tb][:, :], rstd_col[:, tb:tb + 1],
                                             raws(v_hi[:, tb, :]), ALU.mult, ALU.subtract).then_inc(vlo_ready, 1)
                for t in range(STEPS):
                    if t < HEADS * TB:
                        n = (Q_ORDER[t % TB] + 1) * P
                        dve.wait_ge(scores_done, t + 1)
                        dve.tensor_reduce(neg_max[:, t:t + 1], bank[t % 3][:, 0:n], AX.X, ALU.max, negate=True)\
                            .then_inc(max_ready, 1)
                    if 0 <= t - 1 < HEADS * TB:
                        dve.wait_ge(exp_done, t)
                        dve.reciprocal(row_inv[:, t - 1:t], row_sum[:, t - 1:t]).then_inc(inv_ready, 1)
                    if 0 <= t - LOW_LAG < HEADS * TB:
                        tt = t - LOW_LAG
                        h, qb = tt // TB, Q_ORDER[tt % TB]
                        dve.wait_ge(pthi_ready, tt + 1)
                        dst = (slice(None), slice(0, qb + 1), slice(qb * P, (qb + 1) * P))
                        dve.tensor_tensor(pt_lo[h % 2][dst],
                                          bank[4 + tt % 2][:, 0:(qb + 1) * P].rearrange("p (k q) -> p k q", q=P),
                                          raws(pt_hi[h % 2][dst]), ALU.subtract).then_inc(ptlo_ready, 1)
                    if t >= TB - 1 + OUT_LAG and (t - (TB - 1) - OUT_LAG) % TB == 0:
                        h = (t - (TB - 1) - OUT_LAG) // TB
                        p0 = (h % 2) * HD
                        dve.wait_ge(ohi_ready, h + 1)
                        dve.tensor_tensor(cat_lo[p0:p0 + HD, CB + h // 2, :], bank[6 + h % 2][p0:p0 + HD, :],
                                          raws(cat_hi[p0:p0 + HD, CB + h // 2, :]), ALU.subtract).then_inc(olo_ready, 1)
                    if t == 0:
                        qk_low(QK - 1)
                    if t < len(TAPS_T):
                        conv_taps(TAPS_T[t])
                    conv_norm(t)
                    if t in NEXT_SPLIT:
                        split_lo(ph, 0, 4 + NEXT_SPLIT.index(t))
                    if A_SILU + 2 <= t < A_SILU + 2 + CB:
                        b = t - A_SILU - 2
                        dve.wait_ge(probs_turned, HEADS * TB)
                        dve.wait_ge(ahi_ready, b + 1)
                        dve.tensor_tensor(cat_lo[:, b, :], a_act[b][:, :], raws(cat_hi[:, b, :]), ALU.subtract)\
                            .then_inc(alo_ready, 1)

            dve.wait_ge(first_turned, 1)
            dve.tensor_copy(vec[:, 0:FIRST], bank[7][:, 0:FIRST]).then_inc(first_ready, 1)
            for j in range(KD + 1):
                if j < KD:
                    dve.wait_ge(x_turned, j + 1)
                    dve.tensor_copy(x[:, j, :], bank[4 + j % 2][:, :]).then_inc(x_new, 1)
                if j == 2:
                    split_lo(phases[0], 0, 0)
                if j:
                    if j == 1:
                        dve.wait_ge(first_ready, 1)
                    xg_low(j - 1, 0)
            split_lo(phases[0], 0, 1)

            for ph in phases:
                if ph.kind == "pair":
                    pair(ph)
                elif ph.kind == "resid":
                    resid(ph)
                elif ph.kind == "single":
                    for i in range(ph.units):
                        split_lo(ph, i // 4, i % 4 + 2)
                        dve.wait_ge(unit_done, ph.unit0 + i + 1)
                        dve.wait_ge(y_gated, i + 1)
                        if i:
                            dve.wait_ge(ylo_ready, i)
                        dve.tensor_tensor(hid[:, :], bank[i % 4][:, :], c_out[:, i, :], ALU.mult).then_inc(y_out, 1)
                        dve.wait_ge(yhi_ready, i + 1)
                        dve.tensor_tensor(y_lo[:, i, :], hid[:, :], raws(y_hi[:, i, :]), ALU.subtract)\
                            .then_inc(ylo_ready, 1)
                elif ph.kind == "qk":
                    dve.wait_ge(col_done, 1)
                    dve.tensor_copy(rstd_col[:, :].unsqueeze(2),
                                    bank[4][:, :].rearrange("p (t c) -> p t c", t=TB)[:, :, 0:1]).then_inc(col_ready, 1)
                    for i in range(ph.units):
                        if i == AB + 1:
                            head_mean(1)
                        if i == 3:
                            dve.wait_ge(lf_log, 1)
                            link(dve.scalar_tensor_tensor(lf[1][:, :], lf[0][:, :], 0.0, lf[3][:, :], ALU.min,
                                                          ALU.subtract))
                            link(dve.memset(lf[2][:, :], 1.0))
                            dve.tensor_tensor_scan(cum[:, :], lf[2][:, :], lf[1][:, :], 0.0, ALU.mult, ALU.add)\
                                .then_inc(cum_ready, 1)
                        dve.wait_ge(unit_done, ph.unit0 + i + 1)
                        dve.tensor_tensor(qk_raw[:, i, :], bank[i % 4][:, :], rstd[:, :], ALU.mult).then_inc(qk_out, 1)
                        split_lo(ph, i // 4, i % 4 + 2)
                        if i == 0:
                            dve.wait_ge(f_done, 1)
                            link(dve.tensor_tensor(lf[2][:, :], bank[7][0:HEADS, :], rstd[0:HEADS, :], ALU.mult))
                            link(dve.tensor_scalar(lf[0][:, :], lf[2][:, :], b_f[:, 0:1], None, ALU.add))
                            dve.scalar_tensor_tensor(lf[1][:, :], lf[0][:, :], -1.0, lf[0][:, :], ALU.mult, ALU.max)\
                                .then_inc(lf_abs, 1)
                        if i == AB + 1:
                            head_rough(1)
                            head_invert(1)
                        conv_taps(TAPS_QK[i])
                elif ph.kind == "v":
                    attention(ph)

        @block.tensor
        def _(pe):
            def product(dst, a, b, start, stop):
                pe.matmul(dst, a[0], b[0], start=start, stop=False)
                pe.matmul(dst, a[0], b[1], start=False, stop=False)
                return pe.matmul(dst, a[1], b[0], start=False, stop=stop)

            def weights(ph, u):
                return [unit_view(ph, t, u % 2) for t in (w_hi, w_lo)]

            def run_groups(ph, group):
                peeled = 2 if ph is LAST else 1
                for g in range(min(peeled, ph.groups)):
                    group(g)
                if ph.groups > peeled:
                    with pe.Fori(peeled, ph.groups) as g:
                        group(g)

            def projection(ph, g, u, wait_x=False, before=None):
                if before is None:
                    pe.wait_ge(wlo_ready, g * 4 + (ph.unit0 + u + 1))
                wh, wl = weights(ph, u)
                for k in range(KD):
                    if before:
                        before(k)
                    if wait_x:
                        pe.wait_ge(xlo_ready, KD * ph.norm + k + 1)
                    last = product(bank[u][:, :], (wh[:, k, :], wl[:, k, :]), (xg_hi[:, k, :], xg_lo[:, k, :]),
                                   k == 0, k == KD - 1)
                last.then_inc(unit_done, 1)

            def pair(ph):
                def group(g):
                    first = isinstance(g, int) and g == 0
                    for u in range(4):
                        if not first:
                            pe.wait_ge((gate_scaled, pair_out)[u % 2], g * 2 + (ph.pair0 + u // 2 - 1))
                        projection(ph, g, u, wait_x=first and u == 0,
                                   before=turn_in if first and u == 0 and ph is phases[0] else None)
                        if ph is A_GATE and not first and u == 2:
                            pe.wait_ge(wflo_ready, 1)
                            for k in range(KD):
                                last = product(bank[7][:, :], (wf_hi[:, k, :], wf_lo[:, k, :]),
                                               (xg_hi[:, k, :], xg_lo[:, k, :]), k == 0, k == KD - 1)
                            last.then_inc(f_done, 1)
                        if first and u == 1 and ph is phases[0]:
                            pe.wait_ge(first_ready, 1)
                            pe.wait_ge(vec_arrived, 16 * 9)
                            pe.transpose(bank[7][:, 0:NVEC - FIRST], vec_rows[:, :],
                                         ident[0:NVEC - FIRST, 0:NVEC - FIRST]).then_inc(vec_turned, 1)
                            pe.wait_ge(conv_arrived, 16)
                            pe.transpose(bank[7][:, P:P + TAPS * CB], conv_rows[:, :],
                                         ident[0:TAPS * CB, 0:TAPS * CB]).then_inc(vec_turned, 1)
                        if first and u == 0:
                            pe.wait_ge(sq_added, KD * (ph.norm + 1))
                            pe.matmul(bank[6][:, :], ones[:, :], sq_sum[:, :], start=True, stop=True)\
                                .then_inc(ssq_done, 1)

                run_groups(ph, group)

            def turn_x(j):
                if j >= 2:
                    pe.wait_ge(x_new, j - 1)
                if j % (KD // len(x_arrived)) == 0:
                    pe.wait_ge(x_arrived[j // (KD // len(x_arrived))], 16)
                for tb in range(TB):
                    last = pe.transpose(bank[4 + j % 2][:, tb * P:(tb + 1) * P], x_rows[:, tb, j * P:(j + 1) * P],
                                        ident[:, :])
                last.then_inc(x_turned, 1)

            def turn_in(k):
                for j in ((0, 1, 2) if k == 0 else (k + 2,)):
                    if j < KD:
                        turn_x(j)
                if k == 0:
                    pe.wait_ge(wlo_ready, 1)

            def resid(ph):
                per_tile = 2 if ph.row_tiles == HALF else 1
                hi, lo = SRC[ph.source]
                x0 = KD * ph.next_norm if ph is not LAST else X_LAST

                def group(g):
                    first = isinstance(g, int) and g == 0
                    for u in range(4):
                        pe.wait_ge(wlo_ready, g * 4 + (ph.unit0 + u + 1))
                        wh, wl = weights(ph, u)
                        j, half, part = g * (4 // per_tile) + u // per_tile, (u // per_tile) % 2, u % per_tile
                        if part == 0 and (not isinstance(j, int) or j >= 2):
                            pe.wait_ge(x_new, j + (x0 - 1))
                        for k in range(ph.row_tiles):
                            kk = part * ph.row_tiles + k
                            if first and j == 0:
                                if ph.source == "h":
                                    pe.wait_ge(hlo_ready, phases[phases.index(ph) - 1].h0 + kk + 1)
                                elif ph.source == "y":
                                    pe.wait_ge(ylo_ready, kk + 1)
                                elif k >= CB:
                                    pe.wait_ge(olo_ready, 2 * (k - CB) + 2)
                                else:
                                    pe.wait_ge(alo_ready, k + 1)
                            last = product(bank[4 + half][:, :], (wh[:, k, :], wl[:, k, :]),
                                           (hi[:, kk, :], lo[:, kk, :]),
                                           part == 0 and k == 0, part == per_tile - 1 and k == ph.row_tiles - 1)
                        last.then_inc(unit_done, 1)
                        if ph is LAST and part == 1:
                            if half == 1 or not first:
                                turn_out(j - 1, 1 - half)

                run_groups(ph, group)
                if ph is LAST:
                    turn_out(KD - 1, 1)

            X_LAST = KD * 6

            def turn_out(j, half):
                pe.wait_ge(x_new, j + (X_LAST + 1))
                if not isinstance(j, int) or j >= 2:
                    pe.wait_ge(out_staged, j - 1)
                for tb in range(TB):
                    last = pe.transpose(bank[6 + half][:, tb * P:(tb + 1) * P], fin[:, half, tb * P:(tb + 1) * P],
                                        ident[:, :])
                last.then_inc(out_turned, 1)

            def attention():
                def scores(t):
                    h, qb = t // TB, Q_ORDER[t % TB]
                    n, p0, j = (qb + 1) * P, (h % 2) * HD, h // 2
                    dst, qs = bank[t % 3], slice(qb * P, (qb + 1) * P)
                    n = max(n, WIDE)
                    rows = slice(p0, p0 + HD)
                    if t >= 3:
                        pe.wait_ge(exp_done, t - 2)
                    else:
                        pe.wait_ge(vlo_ready, t + 1)
                    if t % (2 * TB) == 0:
                        pe.wait_ge(qklo_ready, 2 * (h // 2 + 1))
                    product(dst[:, 0:n], (q_hi[rows, j, qs], q_lo[rows, j, qs]),
                            (k_hi[rows, j, 0:n], k_lo[rows, j, 0:n]), True, False)
                    pe.matmul(dst[:, 0:n], row_sel[rows, h, :], ncum_r[rows, 0:n], start=False, stop=False)
                    pe.matmul(dst[:, 0:n].rearrange("p (k c) -> p k c", c=P), cum_r[rows, qs],
                              row_sel[rows, h:h + 1, :].broadcast_to([HD, n // P, P]), start=False, stop=False)
                    c0 = max(qb - 1, 0) * P
                    m0 = (qb - c0 // P) * P
                    pe.matmul(dst[:, c0:c0 + WIDE], ident_r[:, :], mask_r[:, P - m0:P - m0 + WIDE],
                              start=False, stop=True).then_inc(scores_done, 1)

                for t in range(STEPS):
                    if t < HEADS * TB:
                        scores(t)
                    if t == A_SUM:
                        pe.wait_ge(vlo_ready, TB)
                        pe.wait_ge(a_added, CB - 1)
                        pe.matmul(bank[3][:, :], ones[:, :], sq_sum[:, :], start=True, stop=True).then_inc(a_sum, 1)
                    if 0 <= t - TURN_LAG < HEADS * TB:
                        tt = t - TURN_LAG
                        pe.wait_ge(probs_ready, tt + 1)
                        if tt >= 2:
                            pe.wait_ge(ptlo_ready, tt - 1)
                        for kb in range(Q_ORDER[tt % TB] + 1):
                            last = pe.transpose(bank[4 + tt % 2][:, kb * P:(kb + 1) * P],
                                                probs[:, tt % NPR, kb * P:(kb + 1) * P], ident[:, :])
                        last.then_inc(probs_turned, 1)
                    first = TB - 1 + PV_LAG
                    if first <= t < first + HEADS * TB:
                        h, kb = (t - first) // TB, (t - first) % TB
                        if kb == 0:
                            pe.wait_ge(ptlo_ready, TB * (h + 1))
                            if h == 0:
                                pe.wait_ge(vlo_ready, TB)
                                pe.wait_ge(pt_cleared, 4)
                            if h >= 2:
                                pe.wait_ge(olo_ready, h - 1)
                        cols = slice((h // 2) * P, (h // 2 + 1) * P)
                        c0 = min(kb * P, S - WIDE)
                        last = product(bank[6 + h % 2][:, c0:S], (v_hi[:, kb, cols], v_lo[:, kb, cols]),
                                       (pt_hi[h % 2][:, kb, c0:S], pt_lo[h % 2][:, kb, c0:S]), kb == 0, kb == TB - 1)
                        if kb == TB - 1:
                            last.then_inc(pv_done, 1)

            def fan(n):
                if n == 0:
                    pe.wait_ge(fan_ready, 2)
                    pe.wait_ge(col_ready, 1)
                if n % AB == 0:
                    pe.wait_ge(qk_rstd, n // AB + 1)
                if n >= 2:
                    pe.wait_ge(qk_scaled, n - 1)
                pe.matmul(bank[4 + n % 2][:, :], head_fan[:, HEAD_ORDER[n], :], head_rstd[n // AB][:, :],
                          start=True, stop=True).then_inc(qk_fanned, 1)

            def head_sum(n):
                pe.wait_ge(qk_sq, n + 1)
                pe.matmul(bank[6 + n // AB][0:2 * HEADS, :], head_sel[:, HEAD_ORDER[n], :], sq[:, n % 2, :],
                          start=n % AB == 0, stop=n % AB == AB - 1).then_inc(qk_sum, 1)

            pe.wait_ge(consts_ready, 3)
            pe.wait_ge(first_arrived, 16)
            pe.transpose(bank[7][:, 0:FIRST], first_rows[:, :], ident[0:FIRST, 0:FIRST]).then_inc(first_turned, 1)

            for ph in phases:
                if ph.kind == "pair":
                    pair(ph)
                elif ph.kind == "resid":
                    resid(ph)
                elif ph.kind == "single":
                    for i in range(ph.units):
                        if i >= 4:
                            pe.wait_ge(y_out, i - 3)
                        else:
                            pe.wait_ge((gate_scaled, pair_out)[i % 2], ph.pair_end - 1 + i // 2)
                        projection(ph, i // 4, i % 4)
                elif ph.kind == "qk":
                    pe.wait_ge(rstd_ready, 2)
                    for tb in range(TB):
                        last = pe.transpose(bank[4][:, tb * P:(tb + 1) * P], rstd[:, tb * P:(tb + 1) * P], ident[:, :])
                    last.then_inc(col_done, 1)
                    pe.wait_ge(sel_ready, 2 + 2 * QK)
                    pe.wait_ge(identr_ready, 1)
                    for i in range(ph.units):
                        if i >= 4:
                            pe.wait_ge(qk_out, i - 3)
                        else:
                            pe.wait_ge((gate_scaled, pair_out)[i % 2], A_GATE.pair0 + CB - 1 + i // 2)
                        projection(ph, i // 4, i % 4)
                        if i:
                            head_sum(i - 1)
                        if i == QK - 1:
                            fan(0)
                            fan(1)
                elif ph.kind == "v":
                    for u in range(ph.units):
                        pe.wait_ge(wlo_ready, ph.unit0 + u + 1)
                        wh, wl = weights(ph, u)
                        for tb in range(TB):
                            if u == 0:
                                pe.wait_ge(qk_out, QK - TB + tb + 1)
                            ts = slice(tb * P, (tb + 1) * P)
                            for k in range(2):
                                kk = 2 * u + k
                                last = product(bank[tb][:, :], (xg_hi[:, kk, ts], xg_lo[:, kk, ts]),
                                               (wh[:, k, :], wl[:, k, :]), kk == 0, kk == KD - 1)
                            if tb == TB - 1:
                                last.then_inc(unit_done, 1)
                            if (u, tb) == (0, 1):
                                head_sum(QK - 1)
                            elif (u, tb) in V_FANS:
                                fan(2 + V_FANS.index((u, tb)))
                    pe.wait_ge(cumlo_ready, 2 * (P // HD))
                    pe.wait_ge(rsel_ready, 1)
                    attention()


_INS = ["x", "ffn1_norm", "ffn1_w_gate", "ffn1_w_up", "ffn1_w_down", "mix_norm", "ffn2_norm", "ffn2_w_gate",
        "ffn2_w_up", "ffn2_w_down", "ev_w_in", "ev_b_f", "ev_conv_w", "ev_conv_b", "ev_conv_norm", "ev_q_norm",
        "ev_k_norm", "ev_w_out", "od_w_in", "od_conv_w", "od_w_out"]


def kernel(**inputs):
    import numpy as np
    from concourse import bacc
    from concourse.bass_utils import run_bass_kernel_spmd

    nc = bacc.Bacc("TRN2", target_bir_lowering=False, num_devices=1)
    arrays, t_in = {}, {}
    for name in _INS:
        a = np.ascontiguousarray(inputs[name])
        arrays[f"in_{name}"] = a
        t_in[name] = nc.dram_tensor(f"in_{name}", a.shape, mybir.dt.from_np(a.dtype), kind="ExternalInput").ap()
    out = nc.dram_tensor("out", inputs["x"].shape, mybir.dt.float32, kind="ExternalOutput").ap()
    trunk(nc, t_in, out)
    return run_bass_kernel_spmd(nc, [arrays], core_ids=[0]).results[0]["out"]
```
